# Optimizing a Trainium2 kernel written in Bass

```python
import math
import jax, jax.numpy as jnp
from jax import lax
import numpy as np

D_MODEL = 1024
BATCH = 1
SEQ = 256
DEPTH = 1
DEC_BATCH = 8
DEC_SEQ = 4
PAST_LEN = 1024
PAGE_SIZE = 128

M_HEADS = 4
M_HEAD_DIM = 256
M_WIDTH = M_HEADS * M_HEAD_DIM
M_CHUNK = 64
A_GROUPS = ((128, 1), (512, 4), (2048, 16))
A_N_GROUPS = len(A_GROUPS)
A_HEADS_PER_GROUP = 4
A_HEAD_DIM = 128
A_HEADS = A_N_GROUPS * A_HEADS_PER_GROUP
A_WIDTH = A_HEADS * A_HEAD_DIM
A_OUT = A_HEADS_PER_GROUP * A_HEAD_DIM
ROPE_THETA = 500000.0
ROPE_DIM = A_HEAD_DIM // 4
N_EXPERTS = 32
TOP_K = 4
D_FF = D_MODEL
SWIGLU_ALPHA = 1.702
SWIGLU_LIMIT = 7.0
MOE_BLOCK = 128
PLE_DIM = 256
EPS = 1e-6
PROJ_SIZES = (M_WIDTH,) * 4 + (M_HEADS,) * 2 + (A_WIDTH,) * 3 + (D_MODEL,) * 2
IN_COLS = sum(PROJ_SIZES)

kernel_name = 'hybrid_mlstm_dilated_attn_moe_step'

def rmsnorm(x, w):
    xf = x.astype(jnp.float32)
    y = xf * lax.rsqrt(jnp.mean(xf * xf, axis=-1, keepdims=True) + EPS)
    return (y * w.astype(jnp.float32)).astype(x.dtype)

def rope(x, pos):
    inv = 1.0 / (ROPE_THETA ** (jnp.arange(0, ROPE_DIM, 2, dtype=jnp.float32) / ROPE_DIM))
    ang = pos[:, None] * inv[None, :]
    cos = jnp.cos(ang)[None, :, None, :]
    sin = jnp.sin(ang)[None, :, None, :]
    half = ROPE_DIM // 2
    xr = x[..., :ROPE_DIM].astype(jnp.float32)
    x1, x2 = xr[..., :half], xr[..., half:]
    rot = jnp.concatenate([x1 * cos - x2 * sin, x2 * cos + x1 * sin], axis=-1)
    return jnp.concatenate([rot.astype(x.dtype), x[..., ROPE_DIM:]], axis=-1)

def split_proj(xn, w_in):
    z = xn @ w_in
    cuts = [int(c) for c in np.cumsum(PROJ_SIZES)[:-1]]
    return jnp.split(z, cuts, axis=-1)

def mlstm_chunkwise(q, k, v, ig, lf, C0, n0, m0):
    B, T, H, E = q.shape
    L = math.gcd(T, M_CHUNK)
    nc = T // L

    def to_chunks(a):
        a = a.reshape((B, nc, L) + a.shape[2:])
        return jnp.swapaxes(jnp.moveaxis(a, 1, 0), 2, 3)

    causal = jnp.tril(jnp.ones((L, L), dtype=bool))

    def step(carry, inp):
        C, n, m = carry
        qc, kc, vc, ic, fc = inp
        b = jnp.cumsum(fc, axis=-1)
        dmat = jnp.where(causal, b[..., :, None] - b[..., None, :] + ic[..., None, :], -jnp.inf)
        inter = b + m[..., None]
        mj = jnp.maximum(inter, jnp.max(dmat, axis=-1))
        sc = jnp.einsum('bhje,bhse->bhjs', qc, kc) * jnp.exp(dmat - mj[..., None])
        a_int = jnp.exp(inter - mj)
        num = jnp.einsum('bhjs,bhsd->bhjd', sc, vc) + a_int[..., None] * jnp.einsum('bhde,bhje->bhjd', C, qc)
        den = jnp.sum(sc, axis=-1) + a_int * jnp.einsum('bhe,bhje->bhj', n, qc)
        h = num / jnp.maximum(jnp.abs(den), jnp.exp(-mj))[..., None]
        bl = b[..., -1]
        g = bl[..., None] - b + ic
        m_new = jnp.maximum(bl + m, jnp.max(g, axis=-1))
        ws = jnp.exp(g - m_new[..., None])
        a_c = jnp.exp(bl + m - m_new)
        C_new = a_c[..., None, None] * C + jnp.einsum('bhs,bhsd,bhse->bhde', ws, vc, kc)
        n_new = a_c[..., None] * n + jnp.einsum('bhs,bhse->bhe', ws, kc)
        return (C_new, n_new, m_new), h

    xs = (to_chunks(q), to_chunks(k), to_chunks(v), to_chunks(ig), to_chunks(lf))
    (C, n, m), hs = lax.scan(step, (C0, n0, m0), xs)
    h = jnp.transpose(hs, (1, 0, 3, 2, 4)).reshape(B, T, H, E)
    return h, C, n, m

def mlstm_branch(mq, mk, mv, mo, mi, mf, norm_w, C0, n0, m0):
    B, T, _ = mq.shape
    f32 = jnp.float32
    shp = (B, T, M_HEADS, M_HEAD_DIM)
    q = mq.reshape(shp).astype(f32)
    k = mk.reshape(shp).astype(f32) * (M_HEAD_DIM ** -0.5)
    v = mv.reshape(shp).astype(f32)
    ig = mi.astype(f32)
    lf = jax.nn.log_sigmoid(mf.astype(f32))
    h, C, n, m = mlstm_chunkwise(q, k, v, ig, lf, C0, n0, m0)
    h = h * jax.nn.sigmoid(mo.astype(f32)).reshape(shp)
    h = h * lax.rsqrt(jnp.mean(h * h, axis=-1, keepdims=True) + EPS)
    h = h.reshape(B, T, M_WIDTH) * norm_w.astype(f32)
    return h.astype(mq.dtype), C, n, m

def attn_qkv(aq, ak, av, pos):
    B, T, _ = aq.shape
    shp = (B, T, A_HEADS, A_HEAD_DIM)
    return rope(aq.reshape(shp), pos), rope(ak.reshape(shp), pos), av.reshape(shp)

def masked_softmax_stats(s, valid):
    s = jnp.where(valid, s, -jnp.inf)
    mx = jnp.max(s, axis=-1, keepdims=True)
    p = jnp.exp(s - mx)
    l = jnp.sum(p, axis=-1)
    return p, l, mx[..., 0] + jnp.log(l)

def dilated_group_prompt(q, k, v, dil, window):
    B, S, H, E = q.shape
    nw = window // dil
    blk = nw
    L = S // dil
    nb = -(-L // blk)
    Lp = nb * blk

    def strided(a):
        return a.reshape(B, L, dil, H, E).transpose(0, 2, 3, 1, 4)

    qs = jnp.pad(strided(q), ((0, 0), (0, 0), (0, 0), (0, Lp - L), (0, 0))).reshape(B, dil, H, nb, blk, E)

    def band(a):
        a = jnp.pad(strided(a), ((0, 0), (0, 0), (0, 0), (blk, Lp - L), (0, 0))).reshape(B, dil, H, nb + 1, blk, E)
        return jnp.concatenate([a[:, :, :, :-1], a[:, :, :, 1:]], axis=-2)

    kb, vb = band(k), band(v)
    s = jnp.einsum('bdhnqe,bdhnke->bdhnqk', qs, kb, preferred_element_type=jnp.float32) * (E ** -0.5)
    qi = jnp.arange(blk)[:, None]
    ki = jnp.arange(2 * blk)[None, :]
    dist = qi + blk - ki
    kpos = jnp.arange(nb)[:, None, None] * blk + ki[None] - blk
    valid = (dist >= 0)[None] & (dist <= nw)[None] & (kpos >= 0)
    p, l, lse = masked_softmax_stats(s, valid)
    o = jnp.einsum('bdhnqk,bdhnke->bdhnqe', p, vb.astype(jnp.float32)) / l[..., None]
    o = o.reshape(B, dil, H, Lp, E)[:, :, :, :L].transpose(0, 3, 1, 2, 4).reshape(B, S, H, E)
    lse = lse.reshape(B, dil, H, Lp)[..., :L].transpose(0, 3, 1, 2).reshape(B, S, H)
    return o, lse

def dilated_group_sample(q, k, v, kbuf, vbuf, dil, window):
    B, T, H, E = q.shape
    Wb = kbuf.shape[1]
    nw = window // dil
    kf = jnp.concatenate([kbuf, k.astype(kbuf.dtype)], axis=1)
    vf = jnp.concatenate([vbuf, v.astype(vbuf.dtype)], axis=1)
    idx = Wb + jnp.arange(T)[:, None] - dil * jnp.arange(nw + 1)[None, :]
    valid = idx >= 0
    idx = jnp.maximum(idx, 0)
    kg = kf[:, idx]
    vg = vf[:, idx]
    s = jnp.einsum('bthe,btjhe->bthj', q, kg, preferred_element_type=jnp.float32) * (E ** -0.5)
    p, l, lse = masked_softmax_stats(s, valid[None, :, None, :])
    o = jnp.einsum('bthj,btjhe->bthe', p, vg.astype(jnp.float32)) / l[..., None]
    return o, lse, kf[:, -Wb:], vf[:, -Wb:]

def combine_groups(outs, lses, dtype):
    o = jnp.stack(outs)
    alpha = jax.nn.softmax(jnp.stack(lses), axis=0)
    y = jnp.einsum('gbth,gbthe->bthe', alpha, o)
    B, T = y.shape[:2]
    return y.reshape(B, T, A_OUT).astype(dtype)

def clamped_swiglu(h):
    x_glu, x_lin = jnp.split(h, 2, axis=-1)
    x_glu = jnp.minimum(x_glu, SWIGLU_LIMIT)
    x_lin = jnp.clip(x_lin, -SWIGLU_LIMIT, SWIGLU_LIMIT)
    return x_glu * jax.nn.sigmoid(SWIGLU_ALPHA * x_glu) * (x_lin + 1.0)

def moe(xn, w_router, b_router, w1, b1, w2, b2):
    N, D = xn.shape
    logits = (xn @ w_router).astype(jnp.float32) + b_router.astype(jnp.float32)
    top_v, top_e = lax.top_k(logits, TOP_K)
    gate = jax.nn.softmax(top_v, axis=-1)
    NA = N * TOP_K
    e_flat = top_e.reshape(-1).astype(jnp.int32)
    tok_flat = jnp.repeat(jnp.arange(N, dtype=jnp.int32), TOP_K)
    order = jnp.argsort(e_flat)
    e_sorted = e_flat[order]
    tok_sorted = tok_flat[order]
    gate_sorted = gate.reshape(-1)[order]
    counts = jnp.bincount(e_flat, length=N_EXPERTS).astype(jnp.int32)
    padded = ((counts + MOE_BLOCK - 1) // MOE_BLOCK) * MOE_BLOCK
    start = jnp.cumsum(counts) - counts
    pend = jnp.cumsum(padded)
    pstart = pend - padded
    dest = pstart[e_sorted] + jnp.arange(NA, dtype=jnp.int32) - start[e_sorted]
    n_blocks = -(-NA // MOE_BLOCK) + N_EXPERTS
    P = n_blocks * MOE_BLOCK
    slot_tok = jnp.full((P,), N, dtype=jnp.int32).at[dest].set(tok_sorted)
    blk_start = jnp.arange(n_blocks, dtype=jnp.int32) * MOE_BLOCK
    blk_exp = jnp.minimum(jnp.searchsorted(pend, blk_start, side='right'), N_EXPERTS - 1)
    x_pad = jnp.concatenate([xn, jnp.zeros((1, D), xn.dtype)], axis=0)

    def run_block(args):
        toks, e = args
        h = x_pad[toks] @ w1[e] + b1[e]
        return clamped_swiglu(h) @ w2[e] + b2[e]

    ys = lax.map(run_block, (slot_tok.reshape(n_blocks, MOE_BLOCK), blk_exp)).reshape(P, D)
    y_assign = ys[dest].astype(jnp.float32) * gate_sorted[:, None]
    return jax.ops.segment_sum(y_assign, tok_sorted, num_segments=N).astype(xn.dtype)

def finish(h, hA, hB, ga, gb, p, w_pa, w_pb, w_o, norm2, w_router, b_router, w1, b1, w2, b2, norm3, w_ple, w_ple_gate):
    u = jax.nn.sigmoid(ga) * (hA @ w_pa) + jax.nn.sigmoid(gb) * (hB @ w_pb)
    h = h + u @ w_o
    B, T, D = h.shape
    h = h + moe(rmsnorm(h, norm2).reshape(B * T, D), w_router, b_router, w1, b1, w2, b2).reshape(B, T, D)
    h = h + (p.astype(h.dtype) @ w_ple) * jax.nn.sigmoid(rmsnorm(h, norm3) @ w_ple_gate)
    return h

def setup_inputs(seed: int = 0) -> dict:
    key = jax.random.key(seed)
    ks = list(jax.random.split(key, 48))
    f32 = jnp.float32
    D = D_MODEL

    def nrm(shape, scale=1.0):
        return jax.random.normal(ks.pop(), shape, f32) * scale

    def gain(shape):
        return 1.0 + nrm(shape, 0.05)

    inp = {}
    inp['x_prompt'] = nrm((BATCH, SEQ, D))
    inp['x_sample'] = nrm((DEC_BATCH, DEC_SEQ, D))
    inp['state_C'] = nrm((DEPTH, DEC_BATCH, M_HEADS, M_HEAD_DIM, M_HEAD_DIM), 0.1)
    inp['state_n'] = nrm((DEPTH, DEC_BATCH, M_HEADS, M_HEAD_DIM), 0.1)
    inp['state_m'] = nrm((DEPTH, DEC_BATCH, M_HEADS))
    for g, (win, dil) in enumerate(A_GROUPS):
        wb = min(win, PAST_LEN)
        inp['cache_k' + str(g)] = nrm((DEPTH, DEC_BATCH, wb, A_HEADS_PER_GROUP, A_HEAD_DIM))
        inp['cache_v' + str(g)] = nrm((DEPTH, DEC_BATCH, wb, A_HEADS_PER_GROUP, A_HEAD_DIM))
    inp['p_prompt'] = nrm((DEPTH, BATCH, SEQ, PLE_DIM))
    inp['p_sample'] = nrm((DEPTH, DEC_BATCH, DEC_SEQ, PLE_DIM))
    inp['norm1'] = gain((DEPTH, D))
    inp['w_in'] = nrm((DEPTH, D, IN_COLS), D ** -0.5)
    inp['b_igate'] = nrm((DEPTH, M_HEADS), 0.1)
    inp['b_fgate'] = jnp.linspace(3.0, 6.0, M_HEADS, dtype=f32)[None, :] + nrm((DEPTH, M_HEADS), 0.1)
    inp['m_norm'] = gain((DEPTH, M_WIDTH))
    inp['w_pa'] = nrm((DEPTH, M_WIDTH, D), M_WIDTH ** -0.5)
    inp['w_pb'] = nrm((DEPTH, A_OUT, D), A_OUT ** -0.5)
    inp['w_o'] = nrm((DEPTH, D, D), D ** -0.5)
    inp['norm2'] = gain((DEPTH, D))
    inp['w_router'] = nrm((DEPTH, D, N_EXPERTS), D ** -0.5)
    inp['b_router'] = nrm((DEPTH, N_EXPERTS), 0.01)
    inp['w1'] = nrm((DEPTH, N_EXPERTS, D, 2 * D_FF), D ** -0.5)
    inp['b1'] = nrm((DEPTH, N_EXPERTS, 2 * D_FF), 0.01)
    inp['w2'] = nrm((DEPTH, N_EXPERTS, D_FF, D), D_FF ** -0.5)
    inp['b2'] = nrm((DEPTH, N_EXPERTS, D), 0.01)
    inp['norm3'] = gain((DEPTH, D))
    inp['w_ple'] = nrm((DEPTH, PLE_DIM, D), PLE_DIM ** -0.5)
    inp['w_ple_gate'] = nrm((DEPTH, D, D), D ** -0.5)
    inp['norm_f'] = gain((D,))
    return inp

def reference(x_prompt, x_sample, state_C, state_n, state_m, cache_k0, cache_v0, cache_k1, cache_v1,
              cache_k2, cache_v2, p_prompt, p_sample, norm1, w_in, b_igate, b_fgate, m_norm, w_pa, w_pb,
              w_o, norm2, w_router, b_router, w1, b1, w2, b2, norm3, w_ple, w_ple_gate, norm_f):
    f32 = jnp.float32
    Bp, S, _ = x_prompt.shape
    T = x_sample.shape[1]
    pos_p = jnp.arange(S, dtype=f32)
    pos_s = jnp.arange(T, dtype=f32) + float(PAST_LEN)
    ck_in = (cache_k0, cache_k1, cache_k2)
    cv_in = (cache_v0, cache_v1, cache_v2)
    pC, pn, pm, sC, sn, sm = [], [], [], [], [], []
    pk = [[] for _ in A_GROUPS]
    pv = [[] for _ in A_GROUPS]
    sk = [[] for _ in A_GROUPS]
    sv = [[] for _ in A_GROUPS]
    hp, hs = x_prompt, x_sample
    for i in range(DEPTH):
        post = (w_pa[i], w_pb[i], w_o[i], norm2[i], w_router[i], b_router[i], w1[i], b1[i], w2[i], b2[i],
                norm3[i], w_ple[i], w_ple_gate[i])
        xn = rmsnorm(hp, norm1[i])
        mq, mk, mv, mo, mi, mf, aq, ak, av, ga, gb = split_proj(xn, w_in[i])
        hA, C, n, m = mlstm_branch(mq, mk, mv, mo, mi + b_igate[i], mf + b_fgate[i], m_norm[i],
                                   jnp.zeros((Bp, M_HEADS, M_HEAD_DIM, M_HEAD_DIM), f32),
                                   jnp.zeros((Bp, M_HEADS, M_HEAD_DIM), f32),
                                   jnp.zeros((Bp, M_HEADS), f32))
        pC.append(C)
        pn.append(n)
        pm.append(m)
        q, k, v = attn_qkv(aq, ak, av, pos_p)
        outs, lses = [], []
        for g, (win, dil) in enumerate(A_GROUPS):
            sl = slice(g * A_HEADS_PER_GROUP, (g + 1) * A_HEADS_PER_GROUP)
            o, l = dilated_group_prompt(q[:, :, sl], k[:, :, sl], v[:, :, sl], dil, win)
            outs.append(o)
            lses.append(l)
            keep = min(win, S)
            pk[g].append(k[:, S - keep:, sl])
            pv[g].append(v[:, S - keep:, sl])
        hB = combine_groups(outs, lses, hp.dtype)
        hp = finish(hp, hA, hB, ga, gb, p_prompt[i], *post)
        xn = rmsnorm(hs, norm1[i])
        mq, mk, mv, mo, mi, mf, aq, ak, av, ga, gb = split_proj(xn, w_in[i])
        hA, C, n, m = mlstm_branch(mq, mk, mv, mo, mi + b_igate[i], mf + b_fgate[i], m_norm[i],
                                   state_C[i].astype(f32), state_n[i].astype(f32), state_m[i].astype(f32))
        sC.append(C)
        sn.append(n)
        sm.append(m)
        q, k, v = attn_qkv(aq, ak, av, pos_s)
        outs, lses = [], []
        for g, (win, dil) in enumerate(A_GROUPS):
            sl = slice(g * A_HEADS_PER_GROUP, (g + 1) * A_HEADS_PER_GROUP)
            o, l, kb, vb = dilated_group_sample(q[:, :, sl], k[:, :, sl], v[:, :, sl], ck_in[g][i], cv_in[g][i], dil, win)
            outs.append(o)
            lses.append(l)
            sk[g].append(kb)
            sv[g].append(vb)
        hB = combine_groups(outs, lses, hs.dtype)
        hs = finish(hs, hA, hB, ga, gb, p_sample[i], *post)
    y_prompt = rmsnorm(hp, norm_f)
    y_sample = rmsnorm(hs, norm_f)
    return (y_prompt, y_sample,
            jnp.stack(pC), jnp.stack(pn), jnp.stack(pm),
            jnp.stack(pk[0]), jnp.stack(pv[0]), jnp.stack(pk[1]), jnp.stack(pv[1]), jnp.stack(pk[2]), jnp.stack(pv[2]),
            jnp.stack(sC), jnp.stack(sn), jnp.stack(sm),
            jnp.stack(sk[0]), jnp.stack(sv[0]), jnp.stack(sk[1]), jnp.stack(sv[1]), jnp.stack(sk[2]), jnp.stack(sv[2]))


_drawn_inputs = setup_inputs


def setup_inputs(seed=0):
    import zlib

    import numpy as np

    out = dict(_drawn_inputs(seed))
    spreads = {}
    factors = {'b_igate': 3.547, 'b1': 8.0, 'b2': 8.0, 'norm3': 7.258}
    for name, (base, spread) in spreads.items():
        noise = np.random.default_rng([zlib.crc32(name.encode()), seed]).standard_normal(out[name].shape)
        drawn = base * np.exp(spread * noise) if base else spread * noise
        out[name] = __import__('jax').numpy.asarray(drawn.astype(out[name].dtype))
    for name, factor in factors.items():
        out[name] = (out[name] * factor).astype(out[name].dtype)
    return out
```

```python
from contextlib import ExitStack

import numpy as np
import concourse.bass as bass
from concourse import mybir

F32 = mybir.dt.float32
I32 = mybir.dt.int32
ALU = mybir.AluOpType
ACT = mybir.ActivationFunctionType
AX = mybir.AxisListType

P = 128
D = 1024
KT = D // P
SEQ = 256
NB, NT = 8, 4
NS = NB * NT
TOK = SEQ + NS
ROWS = (P, P, NS)
MH, MD = 4, 256
MW = MH * MD
AH, AD = 4, 128
GW = AH * AD
AW = 3 * GW
RH = AD // 8
PAST = 1024
GROUPS = ((128, 1), (512, 4), (2048, 16))
WB = tuple(min(w, PAST) for w, _ in GROUPS)
E = 32
TOPK = 4
FF = 1024
ALPHA, LIMIT = 1.702, 7.0
PLE = 256
EPS = 1e-6
NEG = -1e30
CAP = 64
PASSES = -(-TOK // CAP)

ZQ, ZK, ZV, ZO = 0, MW, 2 * MW, 3 * MW
ZAQ = 4 * MW
ZAK, ZAV = ZAQ + AW, ZAQ + 2 * AW
ZGA = ZAQ + 3 * AW
ZGB = ZGA + D
NZ = ZGB + D
GATE0 = 4 * MW
NKEY = P * 7
SKEY = NKEY + 3 * P


def constants():
    p = np.arange(P)[:, None]
    f = np.arange(P)[None, :]
    a = {}
    a["ident"] = (p == f)
    a["ones"] = np.ones((P, P))
    a["before"] = (p < f)
    a["halves"] = (p == f // CAP)
    a["valid"] = np.stack([np.ones(P), np.ones(P), np.arange(P) < NS], 1)
    a["slot"] = np.broadcast_to(f % CAP, (P, P))
    b = {}
    b["causal"] = np.where(p <= f, 0, NEG)
    am = np.full((P, 2, 3, SEQ), NEG)
    s = np.arange(SEQ)[None, :]
    for jt in range(2):
        for g, (win, dil) in enumerate(GROUPS):
            d = jt * P + p - s
            am[:, jt, g] = np.where((d >= 0) & (d % dil == 0) & (d <= win), 0, NEG)
    b["amask"] = am.reshape(P, -1)
    t = p % NT
    sm = np.full((P, SKEY), NEG)
    sm[:, 0:P] = np.where(f >= t, 0, NEG)
    for u in range(4):
        sm[:, (1 + u) * P:(2 + u) * P] = np.where(t == u, 0, NEG)
    for v in range(2):
        sm[:, (5 + v) * P:(6 + v) * P] = np.where(t == 2 * v + f // 64, 0, NEG)
    own = (p // NT == f // NT)
    sm[:, NKEY:NKEY + P] = np.where(own & (f <= p), 0, NEG)
    for g in (1, 2):
        sm[:, NKEY + g * P:NKEY + (g + 1) * P] = np.where(p == f, 0, NEG)
    b["smask"] = sm
    b["scausal"] = np.where(own & (p <= f), 0, NEG)
    bf = (np.arange(P) // NT) % NB
    b["bcol"] = np.broadcast_to((np.arange(NB)[:, None] == bf[None, :]).reshape(1, -1), (P, NB * P))
    b["brow"] = (bf[:, None] == np.arange(NB)[None, :])
    b["bhsel"] = (p // NT == np.arange(NS)[None, :])
    hs = np.zeros((P, MH, P))
    for h in range(MH):
        hs[h, h] = 1
    b["hsel"] = hs.reshape(P, -1)
    half = RH
    inv = (1.0 / (np.float32(500000.0) ** (np.arange(0, 2 * half, 2, dtype=np.float32) / np.float32(2 * half)))).astype(np.float32)
    for name, pos in (("p0", np.arange(P)), ("p1", P + np.arange(P)), ("s", PAST + np.arange(P) % NT)):
        ang = pos.astype(np.float32)[:, None] * inv[None, :]
        a["cos" + name] = np.cos(ang)
        a["sin" + name] = np.sin(ang)
    out = []
    for d in (a, b):
        at, place = 0, {}
        for k, v in d.items():
            place[k] = (at, v.shape[1])
            at += v.shape[1]
        out += [np.concatenate([np.asarray(v, np.float32) for v in d.values()], 1), place]
    return out


CA, CA_AT, CB, CB_AT = constants()

BLOCKS = ([(i * MW, MW) for i in range(4)] + [(ZAQ + i * GW, GW) for i in range(9)] + [(ZGA, D), (ZGB, D)])


def lay_out(x):
    x = {k: np.ascontiguousarray(v) for k, v in x.items()}
    a = {k: x[k] for k in ("x_prompt", "x_sample", "cache_k0", "cache_v0", "cache_k1", "cache_v1", "cache_k2",
                           "cache_v2", "w_in", "w_pa", "w_pb", "w_o", "w1", "w2", "b2", "w_ple",
                           "w_ple_gate", "norm_f", "b_router")}
    a["ca_in"], a["cb_in"] = CA, CB
    col = lambda v: v.reshape(-1, P).T
    a["norm_cols"] = np.concatenate([col(x[k][0]) for k in ("norm1", "m_norm", "norm2", "norm3")], 1)
    a["w_gates"] = x["w_in"][0][:, GATE0:GATE0 + 2 * MH].reshape(KT, P, 2 * MH).transpose(1, 0, 2)
    a["b_gates"] = np.stack([x["b_igate"][0], x["b_fgate"][0]], 1)
    a["b1"] = x["b1"].reshape(E, 2, 2, 512).transpose(0, 2, 1, 3)
    a["w_router"] = x["w_router"][0].reshape(KT, P, E).transpose(1, 0, 2)
    a["p_prompt"], a["p_sample"] = x["p_prompt"][0, 0], x["p_sample"][0].reshape(NS, PLE)
    C = x["state_C"][0].transpose(1, 0, 3, 2).reshape(MH, NB, 2, P, MD)
    a["CT"] = C.transpose(3, 0, 1, 2, 4)
    n = x["state_n"][0].transpose(1, 0, 2)
    a["n_rows"] = n.reshape(MH * NB, MD)
    a["n_tok"] = np.repeat(n.reshape(MH * NB, MD), NT, 0)
    a["m_rows"] = x["state_m"][0].T
    def keys(c):
        t = [x[f"cache_{c}{g}"][0] for g in range(3)]
        g1 = t[1].reshape(NB, P, 4, AH, AD).transpose(0, 2, 1, 3, 4)
        g2 = t[2].reshape(NB, 64, 16, AH, AD)[:, :, 0:4].transpose(0, 2, 1, 3, 4).reshape(NB, 2, 2, 64, AH, AD)
        return np.concatenate([t[0], g1.reshape(NB, 4 * P, AH, AD), g2.reshape(NB, 2 * P, AH, AD)], 1)
    a["KT_cache"] = keys("k").transpose(0, 3, 2, 1)
    a["VK"] = keys("v").reshape(NB, 7, P, GW).transpose(0, 2, 1, 3)
    return {k: np.ascontiguousarray(v) for k, v in a.items()}


OUT_SHAPES = dict(
    y_prompt=(SEQ, D), y_sample=(NS, D), C_p=(MH, MD, MD), n_p=(MH, MD), m_p=(MH, 1),
    k0_p=(1, 1, 128, AH, AD), v0_p=(1, 1, 128, AH, AD), k1_p=(1, 1, 256, AH, AD), v1_p=(1, 1, 256, AH, AD),
    k2_p=(1, 1, 256, AH, AD), v2_p=(1, 1, 256, AH, AD),
    C_s=(P, MH, NB, 2, MD), n_s=(MH * NB, MD), m_s=(MH, NB),
    k0_s=(1, NB, 128, AH, AD), v0_s=(1, NB, 128, AH, AD), k1_s=(1, NB, 512, AH, AD), v1_s=(1, NB, 512, AH, AD),
    k2_s=(1, NB, 1024, AH, AD), v2_s=(1, NB, 1024, AH, AD))


def arrange(r):
    r = {k: np.asarray(v) for k, v in r.items()}
    r["y_prompt"] = r["y_prompt"].reshape(1, SEQ, D)
    r["y_sample"] = r["y_sample"].reshape(NB, NT, D)
    r["C_p"] = r["C_p"].reshape(1, 1, MH, MD, MD)
    r["n_p"] = r["n_p"].reshape(1, 1, MH, MD)
    r["m_p"] = r["m_p"].reshape(1, 1, MH)
    r["C_s"] = np.ascontiguousarray(r["C_s"].transpose(2, 1, 4, 3, 0).reshape(1, NB, MH, MD, MD))
    r["n_s"] = np.ascontiguousarray(r["n_s"].reshape(MH, NB, MD).transpose(1, 0, 2))[None]
    r["m_s"] = np.ascontiguousarray(r["m_s"].T)[None]
    return tuple(r[k] for k in OUT_SHAPES)


def layer(nc, x_prompt, x_sample, cache_k0, cache_v0, cache_k1, cache_v1, cache_k2, cache_v2, w_in, w_pa, w_pb,
          w_o, w1, w2, b2, w_ple, w_ple_gate, norm_f, b_router, ca_in, cb_in, norm_cols, w_gates, b_gates, b1,
          w_router, p_prompt, p_sample, CT, n_rows, n_tok, m_rows, KT_cache, VK,
          y_prompt, y_sample, C_p, n_p, m_p, k0_p, v0_p, k1_p, v1_p, k2_p, v2_p,
          C_s, n_s, m_s, k0_s, v0_s, k1_s, v1_s, k2_s, v2_s):
    caches = ((cache_k0, cache_v0), (cache_k1, cache_v1), (cache_k2, cache_v2))
    outs_p = ((k0_p, v0_p), (k1_p, v1_p), (k2_p, v2_p))
    outs_s = ((k0_s, v0_s), (k1_s, v1_s), (k2_s, v2_s))
    top = ExitStack()

    def sem(stack, name):
        return stack.enter_context(nc.semaphore(name))

    def sb(stack, name, shape, dt=F32):
        return stack.enter_context(nc.sbuf_tensor(name, shape, dt))

    def pb(stack, name, shape):
        return stack.enter_context(nc.psum_tensor(name, shape, F32))

    s_steps = sem(top, "s_steps")
    steps = [0]

    class Chain:

        def __init__(self, eng):
            self.eng, self.s, self.n = eng, s_steps, steps[0]

        def __call__(self, ins):
            ins.then_inc(self.s, 1)
            self.n += 1
            steps[0] = self.n
            self.eng.wait_ge(self.s, self.n)

        def many(self, *instructions):
            for ins in instructions:
                ins.then_inc(self.s, 1)
            self.n += len(instructions)
            steps[0] = self.n
            self.eng.wait_ge(self.s, self.n)

    ca = sb(top, "ca", [P, CA.shape[1]])
    cols = sb(top, "cols", [P, 4 * KT])
    n1c, mnc, n2c, n3c = (cols[:, i * KT:(i + 1) * KT] for i in range(4))
    h = sb(top, "h", [P, 3, D])
    s_stored = sem(top, "s_stored")
    s_shift = sem(top, "s_shift")
    n_stored = [0]
    s_hload = sem(top, "s_hload")

    def CAc(name):
        o, n = CA_AT[name]
        return ca[:, o:o + n]

    ident, ones = CAc("ident"), CAc("ones")

    def store(eng, dst, src):
        eng.dma_start(dst, src).then_inc(s_stored, 16)
        n_stored[0] += 16

    pieces = []
    for g in range(3):
        for c in range(2):
            step = NB // max(1, WB[g] // 256)
            for b in range(0, NB, step):
                pieces.append((g, c, b, step))

    def shift_piece(eng):
        if pieces:
            g, c, b, n = pieces.pop(0)
            eng.dma_start(outs_s[g][c][0, b:b + n, 0:WB[g] - NT].rearrange("b r h e -> b r (h e)"),
                          caches[g][c][0, b:b + n, NT:WB[g]].rearrange("b r h e -> b r (h e)")).then_inc(s_shift, 16)
    n_shift = 16 * len(pieces)

    front = ExitStack()
    zg = sb(front, "zg", [P, 2, 2 * D])
    zgw = sb(front, "zgw", [P, 2, D // 4])
    xT = sb(front, "xT", [P, KT, TOK])
    hAT = xT
    hBT = sb(front, "hBT", [P, AH, TOK])
    mid = ExitStack()
    zm = sb(mid, "zm", [P, 2, 3, MW])
    vaug = sb(mid, "vaug", [P, 2, MH, MD + 1])
    za = sb(mid, "za", [P, 2, 3 * AW])
    zw = sb(mid, "zw", [P, 4, MD])
    zaw = sb(mid, "zaw", [P, 9, AD])
    grow = sb(mid, "grow", [MH, 2, TOK])

    st = ExitStack()
    wbuf = sb(st, "wbuf", [P, 2, KT, MW])
    wif = sb(st, "wif", [P, KT, 2 * MH])
    bif = sb(st, "bif", [MH, 2])
    xn = wbuf[:, 1, 0:3, :]
    sq = wbuf[:, 1, 4, :]
    ss = sb(st, "ss", [P, 3])
    rs = sb(st, "rs", [P, 3])
    rope = sb(st, "rope", [P, 4, 2 * 12, RH])
    psT0, psT1 = pb(st, "psT0", [P, 2, 512]), pb(st, "psT1", [P, 2, 512])
    psT2 = pb(st, "psT2", [P, 512])
    psG = pb(st, "psG", [P, 2, 512])
    s_c = sem(st, "s_consts")
    s_w = [sem(st, "s_w0"), sem(st, "s_w1")]
    s_small = sem(st, "s_small")
    s_ss, s_ms, s_rt, s_rs, s_xn, s_tr, s_xT = (sem(st, n) for n in (
        "s_sumsq", "s_meansq", "s_root", "s_rstd", "s_xn", "s_xtrans", "s_xT"))
    s_gp = sem(st, "s_gate_product")
    s_p0, s_p1, s_p2 = sem(st, "s_prod0"), sem(st, "s_prod1"), sem(st, "s_prod2")
    s_e0, s_e1, s_e2 = sem(st, "s_out0"), sem(st, "s_out1"), sem(st, "s_out2")
    s_aug = sem(st, "s_aug")
    s_rope = sem(st, "s_rope")

    def wcol(z):
        return z if z < GATE0 else z + 2 * MH

    with nc.Block() as block:
        NBLK = len(BLOCKS)

        @block.sync
        def _(sp):
            for t, src in enumerate((x_prompt[0, 0:P], x_prompt[0, P:SEQ], x_sample.rearrange("b t d -> (b t) d"))):
                sp.dma_start(h[0:ROWS[t], t, :], src).then_inc(s_hload, 16)
            sp.dma_start(ca[:, :], ca_in).then_inc(s_c, 16)
            sp.dma_start(cols[:, :], norm_cols).then_inc(s_small, 16)
            sp.dma_start(wif[:, :, :], w_gates).then_inc(s_small, 16)
            sp.dma_start(bif[:, :], b_gates).then_inc(s_small, 16)
            for i, (z0, w) in enumerate(BLOCKS):
                if i == 1:
                    sp.wait_ge(s_tr, 6)
                if i >= 2:
                    sp.wait_ge(s_p2, i - 1)
                sp.dma_start(wbuf[:, i % 2, :, 0:w],
                             w_in[0].rearrange("(k p) n -> p k n", p=P)[:, :, wcol(z0):wcol(z0) + w]).then_inc(s_w[i % 2], 16)
                if i >= 3:
                    shift_piece(sp)
            sp.wait_ge(s_rope, 3)
            sp.wait_ge(s_e0, NBLK)
            sp.wait_ge(s_e1, NBLK)
            sp.wait_ge(s_e2, NBLK)
            for g in range(3):
                for c in range(2):
                    z0 = (1 + c) * AW + g * GW
                    dst = outs_p[g][c][0, 0].rearrange("r h e -> r (h e)")
                    keep = dst.shape[0]
                    for t in range(2):
                        if t * P >= SEQ - keep:
                            r = t * P - (SEQ - keep)
                            store(sp, dst[r:r + P], za[:, t, z0:z0 + GW])
                    for j in range(AH):
                        store(sp, outs_s[g][c][0, :, WB[g] - NT:WB[g], j, :],
                              zaw[NS * j:NS * (j + 1), 3 * (1 + c) + g, :])
            sp.wait_ge(s_stored, n_stored[0])

        @block.gpsimd
        def _(pool):
            pool.memset(vaug[:, :, :, MD:MD + 1], 1.0).then_inc(s_aug, 1)
            pool.wait_ge(s_aug, 1)

        @block.tensor
        def _(pe):
            pe.wait_ge(s_c, 16)
            for t in range(3):
                pe.wait_ge(s_xn, t + 1)
                for half in range(2):
                    if t >= 1:
                        pe.wait_ge(s_xT, 2 * (t - 1) + half + 1)
                    for q in range(4):
                        k = 4 * half + q
                        last = pe.transpose(psG[:, half, q * P:q * P + ROWS[t]], xn[0:ROWS[t], t, k * P:(k + 1) * P],
                                            ident[0:ROWS[t], 0:ROWS[t]])
                    last.then_inc(s_tr, 1)
            pe.wait_ge(s_xT, 6)
            pe.wait_ge(s_small, 48)
            for c in range(2):
                for k in range(KT):
                    last = pe.matmul(psG[0:MH, c, 0:TOK], wif[:, k, c * MH:(c + 1) * MH], xT[:, k, :],
                                     start=(k == 0), stop=(k == KT - 1))
                last.then_inc(s_gp, 1)
            for i, (z0, w) in enumerate(BLOCKS):
                pe.wait_ge(s_w[i % 2], 16 * (i // 2 + 1))
                wb = wbuf[:, i % 2]
                for t, (ps, sp_, se) in enumerate(((psT0, s_p0, s_e0), (psT1, s_p1, s_e1))):
                    if i >= 1:
                        pe.wait_ge(se, i)
                    for c in range(w // 512):
                        for k in range(KT):
                            last = pe.matmul(ps[:, c, :], xT[:, k, t * P:(t + 1) * P], wb[:, k, c * 512:(c + 1) * 512],
                                             start=(k == 0), stop=(k == KT - 1))
                    last.then_inc(sp_, 1)
                if i >= 1:
                    pe.wait_ge(s_e2, i)
                q = w // 4
                for k in range(KT):
                    for g in range(4):
                        last = pe.matmul(psT2[32 * g:32 * g + 32, 0:q], xT[:, k, SEQ:TOK], wb[:, k, g * q:(g + 1) * q],
                                         start=(k == 0), stop=(k == KT - 1))
                last.then_inc(s_p2, 1)

        def dest(z0, t):
            if z0 < ZAQ:
                j = z0 // MW
                if t == 2:
                    return zw[:, j, :]
                if j == 2:
                    return vaug[:, t, :, 0:MD]
                return zm[:, t, min(j, 2), :]
            if z0 < ZGA:
                j = (z0 - ZAQ) // GW
                return zaw[:, j, :] if t == 2 else za[:, t, j * GW:(j + 1) * GW]
            j = (z0 - ZGA) // D
            return zgw[:, j, :] if t == 2 else zg[:, t, j * D:(j + 1) * D]

        def source(z0, w, t):
            if t == 2:
                return psT2[:, 0:w // 4]
            s_ = (psT0, psT1)[t][:, 0:w // 512, :].rearrange("p c n -> p (c n)")
            return s_.rearrange("p (h n) -> p h n", h=MH) if z0 == ZV else s_

        @block.scalar
        def _(act):
            for t in range(3):
                act.wait_ge(s_hload, 48)
                R = ROWS[t]
                if t >= 1:
                    act.wait_ge(s_ss, t)
                act.activation(sq[0:R], h[0:R, t, :], ACT.Square, accum_out=ss[0:R, t:t + 1]).then_inc(s_ss, 1)
                act.wait_ge(s_ms, t + 1)
                act.activation(ss[0:R, t:t + 1], ss[0:R, t:t + 1], ACT.Sqrt).then_inc(s_rt, 1)
            for i, (z0, w) in enumerate(BLOCKS):
                sig = z0 == ZO or z0 >= ZGA
                act.wait_ge(s_p0, i + 1)
                if z0 == ZV:
                    act.wait_ge(s_aug, 1)
                act.activation(dest(z0, 0), source(z0, w, 0), ACT.Sigmoid if sig else ACT.Copy).then_inc(s_e0, 1)
                if sig:
                    act.wait_ge(s_p1, i + 1)
                    act.activation(dest(z0, 1), source(z0, w, 1), ACT.Sigmoid).then_inc(s_e1, 1)
                    act.wait_ge(s_p2, i + 1)
                    act.activation(dest(z0, 2), source(z0, w, 2), ACT.Sigmoid).then_inc(s_e2, 1)

        @block.vector
        def _(dve):
            for t in range(3):
                R = ROWS[t]
                dve.wait_ge(s_ss, t + 1)
                dve.tensor_scalar(ss[0:R, t:t + 1], ss[0:R, t:t + 1], 1.0 / D, EPS, ALU.mult, ALU.add).then_inc(s_ms, 1)
                dve.wait_ge(s_rt, t + 1)
                dve.reciprocal(rs[0:R, t:t + 1], ss[0:R, t:t + 1]).then_inc(s_rs, 1)
                dve.wait_ge(s_rs, t + 1)
                dve.tensor_scalar(xn[0:R, t, :], h[0:R, t, :], rs[0:R, t:t + 1], None, ALU.mult).then_inc(s_xn, 1)
            dve.wait_ge(s_small, 48)
            for t in range(3):
                R = ROWS[t]
                for half in range(2):
                    dve.wait_ge(s_tr, 2 * t + half + 1)
                    dve.tensor_tensor(xT[:, 4 * half:4 * half + 4, t * P:t * P + R],
                                      psG[:, half, :].rearrange("p (q n) -> p q n", q=4)[:, :, 0:R],
                                      n1c[:, 4 * half:4 * half + 4].unsqueeze(2).to_broadcast([P, 4, R]),
                                      ALU.mult).then_inc(s_xT, 1)
            for c in range(2):
                dve.wait_ge(s_gp, c + 1)
                dve.tensor_scalar(grow[:, c, :], psG[0:MH, c, 0:TOK], bif[:, c:c + 1], None, ALU.add)
            for i, (z0, w) in enumerate(BLOCKS):
                if z0 == ZO or z0 >= ZGA:
                    continue
                dve.wait_ge(s_p1, i + 1)
                dve.tensor_copy(dest(z0, 1), source(z0, w, 1)).then_inc(s_e1, 1)
                dve.wait_ge(s_p2, i + 1)
                dve.tensor_copy(dest(z0, 2), source(z0, w, 2)).then_inc(s_e2, 1)
            nb = 4 + 9
            dve.wait_ge(s_e0, nb)
            dve.wait_ge(s_e1, nb)
            dve.wait_ge(s_e2, nb)
            dve.wait_ge(s_c, 16)
            link = Chain(dve)
            for t, (v, n, tab) in enumerate(((za[:, 0, 0:2 * AW], 24, "p0"), (za[:, 1, 0:2 * AW], 24, "p1"),
                                             (zaw[:, 0:6, :].rearrange("p a b -> p (a b)"), 6, "s"))):
                v = v.rearrange("p (n e) -> p n e", e=AD)
                x1, x2 = v[:, :, 0:RH], v[:, :, RH:2 * RH]
                cos = CAc("cos" + tab).unsqueeze(1).to_broadcast([P, n, RH])
                sin = CAc("sin" + tab).unsqueeze(1).to_broadcast([P, n, RH])
                link.many(dve.tensor_tensor(rope[:, 0, 0:n, :], x1, cos, ALU.mult),
                          dve.tensor_tensor(rope[:, 1, 0:n, :], x2, sin, ALU.mult),
                          dve.tensor_tensor(rope[:, 2, 0:n, :], x2, cos, ALU.mult),
                          dve.tensor_tensor(rope[:, 3, 0:n, :], x1, sin, ALU.mult))
                link(dve.tensor_tensor(x1, rope[:, 0, 0:n, :], rope[:, 1, 0:n, :], ALU.subtract))
                dve.tensor_tensor(x2, rope[:, 2, 0:n, :], rope[:, 3, 0:n, :], ALU.add).then_inc(s_rope, 1)
                dve.wait_ge(s_rope, t + 1)
    st.close()
    ap = ExitStack()
    cb = sb(mid, "cb", [P, CB.shape[1]])

    def CBc(name):
        o, n = CB_AT[name]
        return cb[:, o:o + n]

    s_cb = sem(mid, "s_cb")
    qkT = sb(ap, "qkT", [P, 12, 4 * P])
    sS = sb(ap, "sS", [P, 2, 3 * SEQ])
    pS = sb(ap, "pS", [P, 2, 3 * SEQ])
    pT = sb(ap, "pT", [P, 2, 3 * SEQ])
    nmx, lsum, rl = sb(ap, "nmx", [P, 8]), sb(ap, "lsum", [P, 8]), sb(ap, "rl", [P, 8])
    psTR = pb(ap, "psTR", [P, 2, 512])
    psS = pb(ap, "psS", [P, 2, 1024])
    psO = pb(ap, "psO", [P, 2, 512])
    s_qt, s_qe = sem(ap, "s_qk_trans"), sem(ap, "s_qk_out")
    s_sc, s_sm, s_nm, s_ex, s_rl, s_pn = (sem(ap, n) for n in (
        "s_scores", "s_masked", "s_negmax", "s_exp", "s_rsum", "s_pnorm"))
    s_pt, s_pe, s_ov, s_oe = (sem(ap, n) for n in ("s_p_trans", "s_p_out", "s_pv", "s_pv_out"))
    UNITS = [(hs, jt) for hs in range(AH) for jt in range(2)]
    SCALE = AD ** -0.5

    with nc.Block() as block:
        @block.sync
        def _(sp):
            sp.dma_start(cb[:, :], cb_in).then_inc(s_cb, 16)
            for _ in range(2):
                shift_piece(sp)

        @block.tensor
        def _(pe):
            for hd in range(12):
                if hd >= 2:
                    pe.wait_ge(s_qe, hd - 1)
                for c in range(2):
                    for t in range(2):
                        last = pe.transpose(psTR[:, hd % 2, (2 * c + t) * P:(2 * c + t + 1) * P],
                                            za[:, t, c * AW + hd * AD:c * AW + (hd + 1) * AD], ident)
                last.then_inc(s_qt, 1)
            pe.wait_ge(s_qe, 12)

            def scores(i):
                hs, jt = UNITS[i]
                if i >= 2:
                    pe.wait_ge(s_sm, i - 1)
                for g in range(3):
                    last = pe.matmul(psS[:, i % 2, g * SEQ:(g + 1) * SEQ], qkT[:, 4 * g + hs, jt * P:(jt + 1) * P],
                                     qkT[:, 4 * g + hs, 2 * P:4 * P], start=True, stop=True)
                last.then_inc(s_sc, 1)

            def values(i):
                hs, jt = UNITS[i]
                pe.wait_ge(s_pn, i + 1)
                if i >= 1:
                    pe.wait_ge(s_pe, i)
                for g in range(3):
                    for s in range(jt + 1):
                        a = g * SEQ + s * P
                        last = pe.transpose(psTR[:, :, :].rearrange("p a b -> p (a b)")[:, a:a + P], pS[:, i % 2, a:a + P], ident)
                last.then_inc(s_pt, 1)
                pe.wait_ge(s_pe, i + 1)
                if i >= 2:
                    pe.wait_ge(s_oe, i - 1)
                for g in range(3):
                    for s in range(jt + 1):
                        a = g * SEQ + s * P
                        last = pe.matmul(psO[:, i % 2, 0:P], za[:, s, 2 * AW + (4 * g + hs) * AD:2 * AW + (4 * g + hs + 1) * AD],
                                         pT[:, i % 2, a:a + P], start=(g == 0 and s == 0), stop=(g == 2 and s == jt))
                last.then_inc(s_ov, 1)

            for i in range(len(UNITS) + 1):
                if i < len(UNITS):
                    scores(i)
                if i >= 1:
                    values(i - 1)

        def part(x, jt):
            return x.rearrange("p (g s) -> p g s", g=3)[:, :, 0:(jt + 1) * P]

        def evac(act, i):
            jt = UNITS[i][1]
            act.wait_ge(s_pt, i + 1)
            if i >= 2:
                act.wait_ge(s_ov, i - 1)
            act.activation(part(pT[:, i % 2, :], jt), part(psTR[:, :, :].rearrange("p a b -> p (a b)")[:, 0:3 * SEQ], jt),
                           ACT.Copy).then_inc(s_pe, 1)

        @block.scalar
        def _(act):
            for hd in range(0, 12, 2):
                act.wait_ge(s_qt, hd + 1)
                if hd >= 2:
                    act.wait_ge(s_qe, hd)
                act.activation(qkT[:, hd, :], psTR[:, hd % 2, :], ACT.Copy).then_inc(s_qe, 1)
            for i, (hs, jt) in enumerate(UNITS):
                act.wait_ge(s_nm, i + 1)
                if i >= 2:
                    act.wait_ge(s_pt, i - 1)
                act.activation(pS[:, i % 2, :], sS[:, i % 2, :], ACT.Exp, bias=nmx[:, i:i + 1],
                               accum_out=lsum[:, i:i + 1]).then_inc(s_ex, 1)
                if i >= 1:
                    evac(act, i - 1)
            evac(act, len(UNITS) - 1)

        @block.vector
        def _(dve):
            for hd in range(1, 12, 2):
                dve.wait_ge(s_qt, hd + 1)
                dve.wait_ge(s_qe, hd)
                dve.tensor_copy(qkT[:, hd, :], psTR[:, hd % 2, :]).then_inc(s_qe, 1)
            dve.wait_ge(s_cb, 16)

            def out(i):
                hs, jt = UNITS[i]
                dve.wait_ge(s_ov, i + 1)
                dve.tensor_copy(hBT[:, hs, jt * P:(jt + 1) * P], psO[:, i % 2, 0:P]).then_inc(s_oe, 1)

            for i, (hs, jt) in enumerate(UNITS):
                dve.wait_ge(s_sc, i + 1)
                if i >= 2:
                    dve.wait_ge(s_ex, i - 1)
                dve.scalar_tensor_tensor(out=sS[:, i % 2, :], in0=psS[:, i % 2, 0:3 * SEQ], scalar=SCALE,
                                         in1=CBc("amask")[:, jt * 3 * SEQ:(jt + 1) * 3 * SEQ],
                                         op0=ALU.mult, op1=ALU.add).then_inc(s_sm, 1)
                dve.wait_ge(s_sm, i + 1)
                dve.tensor_reduce(nmx[:, i:i + 1], sS[:, i % 2, :], AX.X, ALU.max, negate=True).then_inc(s_nm, 1)
                dve.wait_ge(s_ex, i + 1)
                dve.reciprocal(rl[:, i:i + 1], lsum[:, i:i + 1]).then_inc(s_rl, 1)
                dve.wait_ge(s_rl, i + 1)
                dve.tensor_scalar(pS[:, i % 2, :], pS[:, i % 2, :], rl[:, i:i + 1], None, ALU.mult).then_inc(s_pn, 1)
                if i >= 1:
                    out(i - 1)
            out(len(UNITS) - 1)
    ap.close()

    ap = ExitStack()
    kv = sb(ap, "kv", [P, 3, AH * NKEY])
    sqk = sb(ap, "sqk", [P, 6, P])
    qmask = sb(ap, "qmask", [P, 3, NB, P])
    ssS = sb(ap, "ssS", [P, SKEY])
    spT = qmask[:, 1:3, :, :].rearrange("p g b n -> p (g b) n")[:, 0:10, :]
    own = qmask[:, 0, :, :]
    hBs = sb(ap, "hBs", [P, AD])
    sst = sb(ap, "sst", [P, 3])
    psA = pb(ap, "psA", [P, 4, 512])
    psV = pb(ap, "psV", [P, NB, AD])
    psR = pb(ap, "psR", [P, 512])
    psN = pb(ap, "psN", [P, 512])
    s_kv = [sem(ap, f"s_kv{i}") for i in range(3)]
    s_used = sem(ap, "s_kv_used")
    s_t, s_te, s_qm, s_new = (sem(ap, n) for n in ("s_trans", "s_trans_out", "s_qmask", "s_newscores"))
    s_pr = sem(ap, "s_probs")
    s_pt, s_pe, s_nv, s_hb = (sem(ap, n) for n in ("s_sp_trans", "s_sp_out", "s_new_values", "s_hBs"))
    s_ex = sem(ap, "s_sexp")
    s_nm = sem(ap, "s_snegmax")
    SEGS = ((0, 0, 1, 0), (1, 1, 4, 1), (2, 5, 2, 2))

    with nc.Block() as block:
        @block.sync
        def _(sp):
            for i in range(2 * NB):
                if i >= 3:
                    sp.wait_ge(s_used, i - 2)
                src = KT_cache[i].rearrange("d h k -> d (h k)") if i < NB else VK[i - NB].rearrange("k t n -> k (t n)")
                sp.dma_start(kv[:, i % 3], src).then_inc(s_kv[i % 3], 16)

        @block.tensor
        def _(pe):
            for n in range(6):
                if n == 3:
                    pe.wait_ge(s_te, 1)
                last = pe.transpose(psR[:, (n % 3) * P:(n % 3 + 1) * P], zaw[:, n, :], ident)
                if n % 3 == 2:
                    last.then_inc(s_t, 1)
            pe.wait_ge(s_te, 2)
            for g in range(3):
                last = pe.matmul(psA[:, 3, g * P:(g + 1) * P], sqk[:, g, :], sqk[:, 3 + g, :], start=True, stop=True)
            last.then_inc(s_new, 1)
            pe.wait_ge(s_qm, 3)
            for b in range(NB):
                pe.wait_ge(s_kv[b % 3], 16 * (b // 3 + 1))
                keys = kv[:, b % 3].rearrange("p (h k) -> p h k", h=AH)
                for bank, t0, nt, g in SEGS:
                    for j in range(AH):
                        last = pe.matmul(psA[32 * j:32 * j + 32, bank, 0:nt * P], qmask[:, g, b, 32 * j:32 * j + 32],
                                         keys[:, j, t0 * P:(t0 + nt) * P], start=(b == 0), stop=(b == NB - 1))
                last.then_inc(s_used, 1)
            pe.wait_ge(s_pr, 1)
            for n in range(10):
                if n % 4 == 0 and n:
                    pe.wait_ge(s_pe, n // 4)
                last = pe.transpose(psR[:, (n % 4) * P:(n % 4 + 1) * P], ssS[:, n * P:(n + 1) * P], ident)
                if n % 4 == 3 or n == 9:
                    last.then_inc(s_pt, 1)
            pe.wait_ge(s_pe, 3)
            for b in range(NB):
                i = NB + b
                pe.wait_ge(s_kv[i % 3], 16 * (i // 3 + 1))
                values_ = kv[:, i % 3].rearrange("p (t n) -> p t n", t=7)
                for n in range(7):
                    for j in range(AH):
                        last = pe.matmul(psV[32 * j:32 * j + 32, b, :], spT[:, n, 32 * j:32 * j + 32],
                                         values_[:, n, j * AD:(j + 1) * AD], start=(n == 0), stop=(n == 6))
                last.then_inc(s_used, 1)
            for g in range(3):
                last = pe.matmul(psN[:, 0:AD], spT[:, 7 + g, :], zaw[:, 6 + g, :], start=(g == 0), stop=(g == 2))
            last.then_inc(s_nv, 1)
            pe.wait_ge(s_hb, 1)
            pe.transpose(psR[:, 0:P], hBs[:, :], ident).then_inc(s_t, 1)

        @block.scalar
        def _(act):
            act.wait_ge(s_nm, 1)
            act.activation(ssS[:, :], ssS[:, :], ACT.Exp, bias=sst[:, 0:1], accum_out=sst[:, 1:2]).then_inc(s_ex, 1)
            for n in range(3):
                act.wait_ge(s_pt, n + 1)
                c = min(4, 10 - 4 * n)
                act.activation(spT[:, 4 * n:4 * n + c, :].rearrange("p a b -> p (a b)"), psR[:, 0:c * P], ACT.Copy).then_inc(s_pe, 1)

        @block.vector
        def _(dve):
            link = Chain(dve)
            for n in range(2):
                dve.wait_ge(s_t, n + 1)
                dve.tensor_copy(sqk[:, 3 * n:3 * n + 3, :].rearrange("p a b -> p (a b)"), psR[:, 0:3 * P]).then_inc(s_te, 1)
            dve.wait_ge(s_te, 2)
            for g in range(3):
                dve.tensor_tensor(qmask[:, g, :, :], sqk[:, g, :].unsqueeze(1).to_broadcast([P, NB, P]),
                                  CBc("bcol").rearrange("p (b f) -> p b f", b=NB), ALU.mult).then_inc(s_qm, 1)
            dve.wait_ge(s_new, 1)
            dve.wait_ge(s_used, NB)
            sm = CBc("smask")
            parts = [dve.scalar_tensor_tensor(out=ssS[:, a:a + n], in0=psA[:, bank, 0:n], scalar=SCALE, in1=sm[:, a:a + n],
                                              op0=ALU.mult, op1=ALU.add)
                     for bank, a, n in ((0, 0, P), (1, P, 4 * P), (2, 5 * P, 2 * P), (3, NKEY, 3 * P))]
            link.many(*parts)
            dve.tensor_reduce(sst[:, 0:1], ssS[:, :], AX.X, ALU.max, negate=True).then_inc(s_nm, 1)
            dve.wait_ge(s_ex, 1)
            link(dve.reciprocal(sst[:, 2:3], sst[:, 1:2]))
            dve.tensor_scalar(ssS[:, :], ssS[:, :], sst[:, 2:3], None, ALU.mult).then_inc(s_pr, 1)
            dve.wait_ge(s_used, 2 * NB)
            link(dve.tensor_tensor(own, psV[:, :, :], CBc("brow").unsqueeze(2).to_broadcast([P, NB, AD]), ALU.mult))
            link(dve.tensor_reduce(hBs[:, :], own.rearrange("p b e -> p e b"), AX.X, ALU.add))
            dve.wait_ge(s_nv, 1)
            dve.tensor_tensor(hBs[:, :], psN[:, 0:AD], hBs[:, :], ALU.add).then_inc(s_hb, 1)
            dve.wait_ge(s_t, 3)
            link(dve.tensor_copy(hBT[:, :, SEQ:TOK], psR[:, 0:P].rearrange("p (h n) -> p h n", h=AH)))
    ap.close()
    ap = ExitStack()
    def rowbuf(name, n=TOK):
        return sb(ap, name, [MH, n])
    lf, bsum, cg, mx, tmp, emj, ws, aint = (rowbuf(n) for n in ("lf", "bsum", "cg", "mx", "tmp", "emj", "ws", "aint"))
    m0 = rowbuf("m0", NB)
    mnew = rowbuf("mnew", 1 + NB)
    xrow = sb(ap, "xrow", [MH, 6, P])
    qT_, kT_ = sb(ap, "mqT", [P, 2, SEQ]), sb(ap, "mkT", [P, 2, SEQ])
    arg, ex, wt = sb(ap, "arg", [P, 3 * P]), sb(ap, "ex", [P, 3 * P]), sb(ap, "wt", [P, 3 * P])
    wk = sb(ap, "wk", [P, 2, MD])
    colsb = sb(ap, "colsb", [P, 64])
    sm1 = sb(ap, "sm1", [P, 4])
    ssq = sb(ap, "ssq", [P, 10])
    rsq = sb(ap, "rsq", [P, 10])
    cst = sb(ap, "cst", [P, 2, 2 * MD])
    nst = sb(ap, "nst", [1, 2, MD])
    ct = sb(ap, "ct", [P, 2, MH, 2 * MD])
    sv = sb(ap, "sv", [P, MD + 1])
    sT = sb(ap, "sT", [P, 4, P])
    qmm = sb(ap, "qmm", [P, 2, NB, P])
    wv = sb(ap, "wv", [P, MD])
    km = sb(ap, "km", [P, 2, MD])
    nrow = sb(ap, "nrow", [NS, MD])
    ntok = sb(ap, "ntok", [P, MD])
    scr = sb(ap, "scr", [P, MD])
    psTR = pb(ap, "mTR", [P, 2, 512])
    psS_, psM = pb(ap, "mS", [P, 512]), pb(ap, "mM", [P, 512])
    psN_ = pb(ap, "mN", [P, 2, 512])
    psC, psX = pb(ap, "mC", [P, 512]), pb(ap, "mX", [P, 512])
    KS = MD ** -0.5
    s_ld, s_ac = sem(ap, "s_mload"), sem(ap, "s_mact")
    s_rowd, s_bc, s_colp, s_col, s_xr = (sem(ap, n) for n in ("s_rowargs", "s_rowact", "s_colsp", "s_cols", "s_xrow"))
    s_mt, s_mte, s_mts, s_mtse = (sem(ap, n) for n in ("s_mtrans", "s_mtq_out", "s_mtrans2", "s_mtk_out"))
    s_ms_, s_mm = sem(ap, "s_mscores"), sem(ap, "s_mmax")
    s_arg, s_e, s_w_, s_wk, s_num, s_hh, s_cp, s_co, s_sq = (sem(ap, n) for n in (
        "s_arg", "s_mexp", "s_mw", "s_wk", "s_num", "s_hh", "s_cprod", "s_cout", "s_msq"))
    s_sqd = sem(ap, "s_meansqs")
    s_ha, s_hat, s_hae = sem(ap, "s_ha"), sem(ap, "s_hatrans"), sem(ap, "s_haout")
    s_cst = [sem(ap, "s_cstored0"), sem(ap, "s_cstored1")]
    s_ct = [sem(ap, "s_ct0"), sem(ap, "s_ct1")]
    s_cts = [sem(ap, "s_cts0"), sem(ap, "s_cts1")]
    s_cq, s_km, s_up, s_upd = (sem(ap, n) for n in ("s_cq", "s_km", "s_update", "s_updated"))
    s_sv, s_nn, s_nno, s_qmm, s_wv = (sem(ap, n) for n in ("s_sv", "s_nnew", "s_nnew_out", "s_qmm", "s_wv"))

    PC_ = lambda q, t, hd: colsb[:, 8 * q + 4 * t + hd:8 * q + 4 * t + hd + 1]
    SC_ = lambda q: colsb[:, 24 + q:25 + q]
    AC = colsb[:, 28:60]
    ACC = colsb[0:NS, 60:61]

    with nc.Block() as block:
        @block.sync
        def _(sp):
            sp.dma_start(m0[:, :], m_rows).then_inc(s_ld, 16)
            sp.dma_start(nrow[:, :], n_rows).then_inc(s_ld, 16)
            sp.dma_start(ntok[:, :], n_tok).then_inc(s_ld, 16)
            for hd in range(MH):
                sp.wait_ge(s_co, 2 * hd + 2)
                sp.dma_start(C_p[hd].rearrange("(a p) e -> p a e", p=P), cst[:, hd % 2].rearrange("p (a e) -> p a e", a=2)).then_inc(s_cst[hd % 2], 16)
                sp.dma_start(n_p[hd:hd + 1], nst[:, hd % 2]).then_inc(s_cst[hd % 2], 16)
                if hd == 0:
                    for b in range(2):
                        sp.dma_start(ct[:, b], CT[:, :, b].rearrange("p h k v -> p h (k v)")).then_inc(s_ct[b], 16)
                shift_piece(sp)
            for b in range(NB):
                sp.wait_ge(s_upd, MH * (b + 1))
                sp.dma_start(C_s[:, :, b].rearrange("p h k v -> p h (k v)"), ct[:, b % 2]).then_inc(s_cts[b % 2], 16)
                if b + 2 < NB:
                    sp.wait_ge(s_cts[b % 2], 16 * (b // 2 + 1))
                    sp.dma_start(ct[:, b % 2], CT[:, :, b + 2].rearrange("p h k v -> p h (k v)")).then_inc(s_ct[b % 2], 16)
            sp.wait_ge(s_nno, 1)
            store(sp, n_s, nrow[:, :])
            store(sp, m_p, mnew[:, 0:1])
            store(sp, m_s, mnew[:, 1:1 + NB])
            for i in range(2):
                sp.wait_ge(s_cts[i], 16 * NB // 2)
            for i in range(2):
                sp.wait_ge(s_cst[i], 32 * MH // 2)
            sp.wait_ge(s_stored, n_stored[0])

        @block.tensor
        def _(pe):
            def trans(hd):
                if hd >= 1:
                    pe.wait_ge(s_mte, hd)
                for c in range(2):
                    if c == 1 and hd >= 1:
                        pe.wait_ge(s_mtse, hd)
                    for half in range(2):
                        for t in range(2):
                            a = hd * MD + half * P
                            last = pe.transpose(psTR[:, c, (2 * half + t) * P:(2 * half + t + 1) * P], zm[:, t, c, a:a + P], ident)
                    last.then_inc((s_mt, s_mts)[c], 1)

            trans(0)
            pe.wait_ge(s_xr, 6)
            for q, r in enumerate((cg, emj, ws)):
                for t in range(2):
                    pe.transpose(psX[:, 8 * q + 4 * t:8 * q + 4 * t + 4], r[:, t * P:(t + 1) * P], ident[0:MH, 0:MH])
            for q in range(4):
                pe.matmul(psX[:, 24 + q:25 + q], xrow[:, 1 + q, :], ones[0:MH, 0:1], start=True, stop=True)
            pe.matmul(psX[:, 28:60], ones[0:MH, :], xrow[:, 5, 0:NS], start=True, stop=True)
            pe.matmul(psX[0:NS, 60:61], xrow[:, 5, 0:NS], ones[0:MH, 0:1], start=True, stop=True).then_inc(s_colp, 1)
            for hd in range(MH):
                if hd >= 1:
                    pe.wait_ge(s_w_, hd)
                    pe.wait_ge(s_arg, 3 * hd)
                pe.wait_ge(s_mte, hd + 1)
                pe.wait_ge(s_mtse, hd + 1)
                for half in range(2):
                    pe.matmul(psS_[:, 0:SEQ], kT_[:, half, 0:P], qT_[:, half, :], start=(half == 0), stop=(half == 1))
                for half in range(2):
                    last = pe.matmul(psS_[:, SEQ:3 * P], kT_[:, half, P:SEQ], qT_[:, half, P:SEQ], start=(half == 0), stop=(half == 1))
                last.then_inc(s_ms_, 1)
                pe.matmul(psM[:, 0:SEQ], CBc("hsel")[0:MH, hd * P:(hd + 1) * P], mx[:, 0:SEQ], start=True, stop=True).then_inc(s_mm, 1)
                if hd + 1 < MH:
                    trans(hd + 1)
                pe.wait_ge(s_wk, 2 * hd + 2)
                if hd >= 1:
                    pe.wait_ge(s_co, 2 * hd)
                for dh in range(2):
                    for t in range(2):
                        pe.matmul(psC[:, dh * MD:(dh + 1) * MD], vaug[:, t, hd, dh * P:(dh + 1) * P], wk[:, t, :],
                                  start=(t == 0), stop=(t == 1))
                for t in range(2):
                    last = pe.matmul(psX[0:1, 0:MD], vaug[:, t, hd, MD:MD + 1], wk[:, t, :], start=(t == 0), stop=(t == 1))
                last.then_inc(s_cp, 1)
                pe.wait_ge(s_w_, hd + 1)
                if hd >= 1:
                    pe.wait_ge(s_hh, 2 * hd)
                pe.matmul(psN_[:, 0, 0:MD + 1], wt[:, 0:P], vaug[:, 0, hd, :], start=True, stop=True)
                pe.matmul(psN_[:, 1, 0:MD + 1], wt[:, P:2 * P], vaug[:, 0, hd, :], start=True, stop=False)
                pe.matmul(psN_[:, 1, 0:MD + 1], wt[:, 2 * P:3 * P], vaug[:, 1, hd, :], start=False, stop=True).then_inc(s_num, 1)
            pe.wait_ge(s_mte, MH)
            for n in range(4):
                last = pe.transpose(psTR[:, 0, n * P:(n + 1) * P], zw[:, n // 2, (n % 2) * P:(n % 2 + 1) * P], ident)
            last.then_inc(s_mt, 1)
            pe.wait_ge(s_mte, MH + 1)
            pe.wait_ge(s_w_, MH)
            for half in range(2):
                last = pe.matmul(psS_[:, 0:P], sT[:, 2 + half, :], sT[:, half, :], start=(half == 0), stop=(half == 1))
            last.then_inc(s_ms_, 1)
            pe.wait_ge(s_arg, 3 * MH)
            pe.matmul(psM[:, 0:P], ones[0:MH, :], xrow[:, 0, :], start=True, stop=True).then_inc(s_mm, 1)
            pe.wait_ge(s_w_, MH + 1)
            pe.wait_ge(s_hh, 2 * MH)
            pe.matmul(psN_[:, 0, 0:MD + 1], wt[:, 0:P], sv[:, :], start=True, stop=True).then_inc(s_num, 1)
            pe.wait_ge(s_wk, 2 * MH + 1)
            pe.wait_ge(s_co, 2 * MH)
            pe.matmul(psX[0:NS, 0:MD], CBc("bhsel"), wk[:, 0, :], start=True, stop=True).then_inc(s_nn, 1)
            pe.wait_ge(s_qmm, 2)
            pe.wait_ge(s_wv, 1)
            for b in range(NB):
                pe.wait_ge(s_ct[b % 2], 16 * (b // 2 + 1))
                for half in range(2):
                    for j in range(MH):
                        last = pe.matmul(psN_[32 * j:32 * j + 32, 1, 0:MD], qmm[:, half, b, 32 * j:32 * j + 32],
                                         ct[:, b % 2, j, half * MD:(half + 1) * MD],
                                         start=(b == 0 and half == 0), stop=(b == NB - 1 and half == 1))
                last.then_inc(s_cq, 1)
                pe.wait_ge(s_km, b + 1)
                for j in range(MH):
                    n = MH * b + j
                    ps = (psTR[:, 0], psTR[:, 1], psS_[:, :], psC[:, :])[j]
                    if n >= MH:
                        pe.wait_ge(s_upd, n - MH + 1)
                    elif j == 2:
                        pe.wait_ge(s_w_, MH + 1)
                    elif j == 3:
                        pe.wait_ge(s_co, 2 * MH)
                    elif j == 0:
                        pe.wait_ge(s_mte, MH + 1)
                        pe.wait_ge(s_mtse, MH)
                    for half in range(2):
                        last = pe.matmul(ps[:, half * MD:(half + 1) * MD], km[32 * j:32 * j + 32, b % 2, half * P:(half + 1) * P],
                                         wv[32 * j:32 * j + 32, :], start=True, stop=True)
                    last.then_inc(s_up, 1)
            pe.wait_ge(s_ha, 8)
            pe.wait_ge(s_upd, MH * NB)
            for n in range(4):
                if n >= 2:
                    pe.wait_ge(s_hae, n - 1)
                t, half = n // 2, n % 2
                for q in range(4):
                    k = 4 * half + q
                    last = pe.transpose(psTR[:, n % 2, q * P:(q + 1) * P], zm[:, t, 2, k * P:(k + 1) * P], ident)
                last.then_inc(s_hat, 1)
            pe.wait_ge(s_ha, 9)
            for half in range(2):
                pe.wait_ge(s_hae, 3 + half)
                pe.transpose(psTR[:, half, 0:P], zw[:, 3, half * P:(half + 1) * P], ident).then_inc(s_hat, 1)

        @block.scalar
        def _(act):
            act.wait_ge(s_steps, steps[0] + 2)
            act.activation(tmp[:, :], tmp[:, :], ACT.Exp).then_inc(s_bc, 1)
            act.wait_ge(s_bc, 1)
            act.activation(tmp[:, :], tmp[:, :], ACT.Ln, bias=1.0).then_inc(s_bc, 1)
            act.wait_ge(s_rowd, 1)
            act.activation(emj[:, :], emj[:, :], ACT.Exp).then_inc(s_bc, 1)
            act.activation(ws[:, :], ws[:, :], ACT.Exp).then_inc(s_bc, 1)
            act.activation(aint[:, 0:NS], aint[:, 0:NS], ACT.Exp).then_inc(s_bc, 1)
            for hd in range(MH):
                act.wait_ge(s_mt, hd + 1)
                if hd >= 1:
                    act.wait_ge(s_ms_, hd)
                act.activation(qT_[:, :, :].rearrange("p a b -> p (a b)"), psTR[:, 0, :], ACT.Copy).then_inc(s_mte, 1)
                act.wait_ge(s_col, 1)
                act.wait_ge(s_arg, 3 * hd + 3)
                if hd >= 1:
                    act.wait_ge(s_w_, hd)
                act.activation(ex[:, 0:SEQ], arg[:, 0:SEQ], ACT.Exp, bias=PC_(0, 0, hd)).then_inc(s_e, 1)
                act.activation(ex[:, SEQ:3 * P], arg[:, SEQ:3 * P], ACT.Exp, bias=PC_(0, 1, hd)).then_inc(s_e, 1)
                act.wait_ge(s_cp, hd + 1)
                if hd >= 2:
                    act.wait_ge(s_cst[hd % 2], 32 * (hd // 2))
                act.activation(cst[:, hd % 2], psC[:, :], ACT.Copy).then_inc(s_co, 1)
                act.activation(nst[:, hd % 2], psX[0:1, 0:MD], ACT.Copy).then_inc(s_co, 1)
                for t in range(2):
                    n = 2 * hd + t
                    act.wait_ge(s_hh, n + 1)
                    if n:
                        act.wait_ge(s_sq, n)
                    act.activation(scr[:, :], zm[:, t, 2, hd * MD:(hd + 1) * MD], ACT.Square, accum_out=ssq[:, n:n + 1]).then_inc(s_sq, 1)
            act.wait_ge(s_mt, MH + 1)
            act.activation(sT[:, :, :].rearrange("p a b -> p (a b)"), psTR[:, 0, :], ACT.Copy).then_inc(s_mte, 1)
            act.wait_ge(s_arg, 3 * MH + 1)
            act.activation(ex[:, 0:P], arg[:, 0:P], ACT.Exp, bias=SC_(0)).then_inc(s_e, 1)
            act.wait_ge(s_sqd, 1)
            act.activation(ssq[:, 0:8], ssq[:, 0:8], ACT.Sqrt).then_inc(s_ac, 1)
            act.wait_ge(s_hh, 2 * MH + 1)
            act.wait_ge(s_sq, 8)
            act.activation(scr[:, :], zw[:, 3, :], ACT.Square, accum_out=ssq[:, 8:9]).then_inc(s_sq, 1)
            act.wait_ge(s_sqd, 2)
            act.activation(ssq[:, 8:9], ssq[:, 8:9], ACT.Sqrt).then_inc(s_ac, 1)

        @block.vector
        def _(dve):
            link = Chain(dve)
            f = grow[:, 1, :]
            link(dve.tensor_scalar(tmp[:, :], f, -1.0, None, ALU.mult))
            link(dve.tensor_tensor(tmp[:, :], f, tmp[:, :], ALU.min))
            link(dve.tensor_scalar(lf[:, :], f, 0.0, None, ALU.min))
            dve.wait_ge(s_bc, 2)
            link(dve.tensor_tensor(lf[:, :], lf[:, :], tmp[:, :], ALU.subtract))

            def scan(src, dst, op):
                bufs = [src, dst]
                d, i = 1, 0
                while d < SEQ:
                    a, b = bufs[i % 2], bufs[(i + 1) % 2]
                    todo = [dve.tensor_tensor(b[:, d:SEQ], a[:, d:SEQ], a[:, 0:SEQ - d], op),
                            dve.tensor_copy(b[:, 0:d], a[:, 0:d])]
                    av, bv = (x[:, SEQ:TOK].rearrange("p (b t) -> p b t", t=NT) for x in (a, b))
                    if d < NT:
                        todo += [dve.tensor_tensor(bv[:, :, d:NT], av[:, :, d:NT], av[:, :, 0:NT - d], op),
                                 dve.tensor_copy(bv[:, :, 0:d], av[:, :, 0:d])]
                    link.many(*todo)
                    d, i = 2 * d, i + 1
                return src

            scan(lf, tmp, ALU.add)
            link(dve.tensor_copy(bsum[:, :], lf[:, :]))
            link(dve.tensor_tensor(cg[:, :], grow[:, 0, :], bsum[:, :], ALU.subtract))
            link(dve.tensor_copy(mx[:, :], cg[:, :]))
            scan(mx, tmp, ALU.max)
            dve.wait_ge(s_ld, 48)
            samp = lambda x: x[:, SEQ:TOK].rearrange("p (b t) -> p b t", t=NT)
            m0b = m0[:, :].unsqueeze(2).to_broadcast([MH, NB, NT])
            link.many(dve.tensor_scalar(mx[:, 0:SEQ], mx[:, 0:SEQ], 0.0, None, ALU.max),
                      dve.tensor_tensor(samp(mx), samp(mx), m0b, ALU.max))
            link(dve.tensor_tensor(tmp[:, :], bsum[:, :], mx[:, :], ALU.add))
            link.many(dve.tensor_copy(mnew[:, 0:1], tmp[:, SEQ - 1:SEQ]),
                      dve.tensor_copy(mnew[:, 1:1 + NB], samp(tmp)[:, :, NT - 1]),
                      dve.tensor_scalar(emj[:, :], tmp[:, :], -1.0, None, ALU.mult),
                      dve.tensor_scalar(ws[:, 0:SEQ], cg[:, 0:SEQ], mx[:, SEQ - 1:SEQ], None, ALU.subtract),
                      dve.tensor_tensor(samp(ws), samp(cg), samp(mx)[:, :, NT - 1:NT].to_broadcast([MH, NB, NT]), ALU.subtract))
            dve.tensor_tensor(aint[:, 0:NS].rearrange("p (b t) -> p b t", t=NT), m0b, samp(mx), ALU.subtract).then_inc(s_rowd, 1)
            dve.wait_ge(s_bc, 5)
            own4 = CBc("hsel")[0:MH].rearrange("p (h n) -> p h n", h=MH)
            for q, r in enumerate((samp(mx), samp(cg), samp(emj), samp(ws), aint[:, 0:NS])):
                r = r if q == 4 else (mx, cg, emj, ws)[q][:, SEQ:TOK]
                dve.tensor_tensor(xrow[:, q, :].rearrange("p (h n) -> p h n", h=MH), r.unsqueeze(1).to_broadcast([MH, MH, NS]),
                                  own4[:, :, 0:NS], ALU.mult).then_inc(s_xr, 1)
            decay = aint[:, 0:NS].rearrange("p (b t) -> p b t", t=NT)[:, :, NT - 1]
            dve.tensor_tensor(xrow[:, 5, 0:NS].rearrange("p (h b) -> p h b", h=MH), decay.unsqueeze(1).to_broadcast([MH, MH, NB]),
                              own4[:, :, 0:NB], ALU.mult).then_inc(s_xr, 1)
            dve.wait_ge(s_colp, 1)
            dve.tensor_copy(colsb[:, 0:60], psX[:, 0:60]).then_inc(s_col, 1)
            dve.tensor_copy(ACC, psX[0:NS, 60:61]).then_inc(s_col, 1)
            dve.wait_ge(s_col, 2)

            def finish(n, num, den, rden, e, gate):
                link(dve.tensor_scalar(sm1[:, 0:1], den, -1.0, None, ALU.mult))
                link(dve.scalar_tensor_tensor(out=sm1[:, 0:1], in0=sm1[:, 0:1], scalar=e, in1=den, op0=ALU.max, op1=ALU.max))
                link(dve.reciprocal(sm1[:, 1:2], sm1[:, 0:1]))
                dve.scalar_tensor_tensor(out=gate, in0=num, scalar=sm1[:, 1:2], in1=gate, op0=ALU.mult, op1=ALU.mult).then_inc(s_hh, 1)

            for hd in range(MH):
                dve.wait_ge(s_mts, hd + 1)
                if hd >= 1:
                    dve.wait_ge(s_ms_, hd)
                dve.tensor_copy(kT_[:, :, :].rearrange("p a b -> p (a b)"), psTR[:, 1, :]).then_inc(s_mtse, 1)
                if hd >= 1:
                    dve.wait_ge(s_cp, hd)
                for t in range(2):
                    dve.tensor_scalar(wk[:, t, :], zm[:, t, 1, hd * MD:(hd + 1) * MD], PC_(2, t, hd), KS, ALU.mult, ALU.mult).then_inc(s_wk, 1)
                dve.wait_ge(s_mm, hd + 1)
                if hd >= 1:
                    dve.wait_ge(s_e, 2 * hd)
                dve.tensor_tensor(arg[:, 0:P], CBc("causal"), psM[:, 0:P], ALU.subtract).then_inc(s_arg, 1)
                dve.tensor_scalar(arg[:, P:SEQ], psM[:, P:SEQ], -1.0, None, ALU.mult).then_inc(s_arg, 1)
                dve.tensor_tensor(arg[:, SEQ:3 * P], CBc("causal"), psM[:, P:SEQ], ALU.subtract).then_inc(s_arg, 1)
                dve.wait_ge(s_e, 2 * hd + 2)
                dve.wait_ge(s_ms_, hd + 1)
                if hd >= 1:
                    dve.wait_ge(s_num, hd)
                dve.scalar_tensor_tensor(out=wt[:, :], in0=psS_[:, 0:3 * P], scalar=KS, in1=ex[:, :], op0=ALU.mult, op1=ALU.mult).then_inc(s_w_, 1)
                dve.wait_ge(s_num, hd + 1)
                for t in range(2):
                    finish(2 * hd + t, psN_[:, t, 0:MD], psN_[:, t, MD:MD + 1], None, PC_(1, t, hd), zm[:, t, 2, hd * MD:(hd + 1) * MD])
            dve.tensor_copy(sv[:, 0:MD], zw[:, 2, :]).then_inc(s_sv, 1)
            dve.tensor_copy(sv[:, MD:MD + 1], ones[:, 0:1]).then_inc(s_sv, 1)
            dve.wait_ge(s_cp, MH)
            dve.tensor_scalar(wk[:, 0, :], zw[:, 1, :], SC_(2), KS, ALU.mult, ALU.mult).then_inc(s_wk, 1)
            dve.tensor_scalar(wv[:, :], zw[:, 2, :], SC_(2), None, ALU.mult).then_inc(s_wv, 1)
            dve.wait_ge(s_mte, MH + 1)
            for half in range(2):
                dve.tensor_tensor(qmm[:, half], sT[:, half, :].unsqueeze(1).to_broadcast([P, NB, P]),
                                  CBc("bcol").rearrange("p (b f) -> p b f", b=NB), ALU.mult).then_inc(s_qmm, 1)
            dve.wait_ge(s_mm, MH + 1)
            dve.wait_ge(s_e, 2 * MH)
            dve.tensor_tensor(arg[:, 0:P], CBc("scausal"), psM[:, 0:P], ALU.subtract).then_inc(s_arg, 1)
            dve.wait_ge(s_e, 2 * MH + 1)
            dve.wait_ge(s_ms_, MH + 1)
            dve.wait_ge(s_num, MH)
            dve.wait_ge(s_sv, 2)
            dve.scalar_tensor_tensor(out=wt[:, 0:P], in0=psS_[:, 0:P], scalar=KS, in1=ex[:, 0:P], op0=ALU.mult, op1=ALU.mult).then_inc(s_w_, 1)
            dve.wait_ge(s_sq, 8)
            dve.tensor_scalar(ssq[:, 0:8], ssq[:, 0:8], 1.0 / MD, EPS, ALU.mult, ALU.add).then_inc(s_sqd, 1)
            dve.wait_ge(s_ac, 1)
            link(dve.reciprocal(rsq[:, 0:8], ssq[:, 0:8]))
            for n in range(8):
                x = zm[:, n % 2, 2, (n // 2) * MD:(n // 2 + 1) * MD]
                dve.tensor_scalar(x, x, rsq[:, n:n + 1], None, ALU.mult).then_inc(s_ha, 1)
            dve.wait_ge(s_nn, 1)
            dve.scalar_tensor_tensor(out=nrow[:, :], in0=nrow[:, :], scalar=ACC, in1=psX[0:NS, 0:MD], op0=ALU.mult, op1=ALU.add).then_inc(s_nno, 1)
            for b in range(NB):
                if b >= 2:
                    dve.wait_ge(s_up, MH * (b - 1))
                dve.tensor_scalar(km[:, b % 2, :], zw[:, 1, :], CBc("brow")[:, b:b + 1], KS, ALU.mult, ALU.mult).then_inc(s_km, 1)
                dve.wait_ge(s_cq, b + 1)
                for j in range(MH):
                    dve.wait_ge(s_up, MH * b + j + 1)
                    ps = (psTR[:, 0], psTR[:, 1], psS_[:, :], psC[:, :])[j]
                    x = ct[:, b % 2, j, :]
                    n = j * NB + b
                    dve.scalar_tensor_tensor(out=x, in0=x, scalar=AC[:, n:n + 1], in1=ps, op0=ALU.mult, op1=ALU.add).then_inc(s_upd, 1)
            link(dve.tensor_tensor(ntok[:, :], ntok[:, :], zw[:, 0, :], ALU.mult))
            link(dve.tensor_reduce(sm1[:, 2:3], ntok[:, :], AX.X, ALU.add))
            dve.wait_ge(s_num, MH + 1)
            link(dve.scalar_tensor_tensor(out=sm1[:, 3:4], in0=sm1[:, 2:3], scalar=SC_(3), in1=psN_[:, 0, MD:MD + 1], op0=ALU.mult, op1=ALU.add))
            link(dve.tensor_scalar(ntok[:, :], psN_[:, 1, 0:MD], SC_(3), None, ALU.mult))
            link(dve.tensor_tensor(ntok[:, :], ntok[:, :], psN_[:, 0, 0:MD], ALU.add))
            finish(8, ntok[:, :], sm1[:, 3:4], None, SC_(1), zw[:, 3, :])
            dve.wait_ge(s_sq, 9)
            dve.tensor_scalar(ssq[:, 8:9], ssq[:, 8:9], 1.0 / MD, EPS, ALU.mult, ALU.add).then_inc(s_sqd, 1)
            dve.wait_ge(s_ac, 2)
            link(dve.reciprocal(rsq[:, 8:9], ssq[:, 8:9]))
            dve.tensor_scalar(zw[:, 3, :], zw[:, 3, :], rsq[:, 8:9], None, ALU.mult).then_inc(s_ha, 1)
            for n in range(4):
                dve.wait_ge(s_hat, n + 1)
                t, half = n // 2, n % 2
                dve.tensor_tensor(hAT[:, 4 * half:4 * half + 4, t * P:(t + 1) * P], psTR[:, n % 2, :].rearrange("p (q n) -> p q n", q=4),
                                  mnc[:, 4 * half:4 * half + 4].unsqueeze(2).to_broadcast([P, 4, P]), ALU.mult).then_inc(s_hae, 1)
            for half in range(2):
                dve.wait_ge(s_hat, 5 + half)
                dve.tensor_tensor(hAT[:, half:KT:2, SEQ:TOK], psTR[:, half, 0:P].rearrange("p (h n) -> p h n", h=MH),
                                  mnc[:, half:KT:2].unsqueeze(2).to_broadcast([P, MH, NS]), ALU.mult).then_inc(s_hae, 1)
    ap.close()
    mid.close()
    ring = sb(front, "ring", [P, 6, 4096])
    wa = sb(front, "wa", [P, KT, D])
    wb_ = sb(front, "wb", [P, 4096])
    wpb = wb_[:, :].rearrange("p (k n) -> p k n", k=4)
    b2s = wb_[0:E, 0:D]
    wple = wb_[:, D:3 * D].rearrange("p (k n) -> p k n", k=2)
    prow = wb_[:, 3 * D:3 * D + 3 * PLE].rearrange("p (t n) -> p t n", t=3)
    uT = xT
    zflat = zg[:, :, :].rearrange("p t n -> p (t n)")
    x2 = zflat[:, 0:3 * D].rearrange("p (t n) -> p t n", t=3)
    acc2 = zflat[0:2 * NS, 3 * D:3 * D + 512]
    ysb = zflat[:, 3 * D + 512:4 * D]
    xflat = xT[:, :, :].rearrange("p k n -> p (k n)")
    glu, lin, sg, xg = (xflat[:, 512 * i:512 * (i + 1)] for i in range(4))
    hflat = hBT[:, :, :].rearrange("p k n -> p (k n)")
    xgT = hflat[:, 0:512].rearrange("p (j n) -> p j n", j=4)
    acT = hflat[:, 512:1024].rearrange("p (j n) -> p j n", j=4)
    wr = sb(front, "wr", [P, KT, E])
    RG = sb(front, "RG", [P, E + 1, 6])
    selU, selG = sb(front, "selU", [P, 3, P]), sb(front, "selG", [P, 3, P])
    GAB = sb(front, "GAB", [P, 2, TOK])
    b1s = sb(front, "b1s", [2, 2 * 512])
    rg6 = sb(front, "rg6", [P, 6])
    nmax = sb(front, "nmax", [P, 1], I32)
    st3 = sb(front, "st3", [P, 12])
    s_ring = [sem(front, f"s_ring{c}") for c in range(6)]
    w1v = w1[0].rearrange("e (c k p) n -> e c p k n", c=4, p=P)
    w2v = w2[0].rearrange("e (c k p) n -> e c p k n", c=2, p=P)

    def load_chunk(sp, e, c):
        if c < 4:
            src, k = w1v[e, c], 2
        else:
            src, k = w2v[e, c - 4], 4
        if not isinstance(e, int):
            src = (w1v[bass.ds(e, 1), c, :, :, :] if c < 4 else w2v[bass.ds(e, 1), c - 4, :, :, :]).rearrange("a p k n -> (a p) k n")
        sp.dma_start(ring[:, c, :].rearrange("p (k n) -> p k n", k=k), src).then_inc(s_ring[c], 16)

    ap = ExitStack()
    Lg = sb(ap, "Lg", [P, 3, E])
    work = [sb(ap, f"rw{i}", [P, 3, E]) for i in range(4)]
    mask = sb(ap, "mask", [P, 3, E])
    m8 = sb(ap, "m8", [P, 3, 8])
    brb = sb(ap, "brb", [P, E])
    gT = GAB[0:E, :, :].rearrange("p a b -> p (a b)")[:, 0:TOK]
    pX = [pb(ap, "pX0", [P, 2, 512]), pb(ap, "pX1", [P, 2, 512])]
    pX2 = pb(ap, "pX2", [P, 512])
    pT = pb(ap, "pT_", [P, 2, 512])
    pR = pb(ap, "pR", [P, 512])
    s_wa, s_wb, s_sm, s_b2 = sem(ap, "s_wa"), sem(ap, "s_wb"), sem(ap, "s_smallw"), sem(ap, "s_b2")
    s_pa, s_pe_, s_u = sem(ap, "s_products"), sem(ap, "s_products_out"), sem(ap, "s_u")
    s_ut, s_ute = sem(ap, "s_utrans"), sem(ap, "s_utrans_out")
    s_h1, s_sq, s_mq, s_rt, s_x2, s_x2t, s_x2e = (sem(front, "s_" + n) for n in (
        "residual", "sumsq2", "meansq2", "root2", "xn2", "xn2_trans", "xn2_T"))
    s_lg, s_mask, s_rk, s_gt, s_gte, s_bb, s_ex = (sem(ap, n) for n in (
        "s_logits", "s_mask", "s_rank", "s_gtrans", "s_gT", "s_bias2", "s_gexp"))
    s_nx = sem(ap, "s_nextweights")

    def xs_products(pe, xt, kt, wts, first_wait, n0, pX, pX2, s_pa, s_pe_):
        for t in range(3):
            if n0 + t >= 3:
                pe.wait_ge(s_pe_, n0 + t - 2)
            for ready in (first_wait if t == 0 else ()):
                pe.wait_ge(*ready)
            if t < 2:
                for c in range(2):
                    for k in range(kt):
                        last = pe.matmul(pX[t][:, c, :], xt[:, k, t * P:(t + 1) * P], wts[:, k, c * 512:(c + 1) * 512],
                                         start=(k == 0), stop=(k == kt - 1))
            else:
                for k in range(kt):
                    for g in range(4):
                        last = pe.matmul(pX2[32 * g:32 * g + 32, 0:D // 4], xt[:, k, SEQ:TOK], wts[:, k, g * 256:(g + 1) * 256],
                                         start=(k == 0), stop=(k == kt - 1))
            last.then_inc(s_pa, 1)

    with nc.Block() as block:
        @block.sync
        def _(sp):
            sp.dma_start(wa[:, :, :], w_pa[0].rearrange("(k p) n -> p k n", p=P)).then_inc(s_wa, 16)
            sp.dma_start(wpb, w_pb[0].rearrange("(k p) n -> p k n", p=P)).then_inc(s_wb, 16)
            sp.dma_start(wr[:, :, :], w_router).then_inc(s_sm, 16)
            sp.dma_start(brb[:, :], b_router[0].partition_broadcast(P)).then_inc(s_sm, 16)
            sp.dma_start(b1s[:, :], b1[0].rearrange("a b n -> a (b n)")).then_inc(s_sm, 16)
            for c in range(3):
                load_chunk(sp, 0, c)
            sp.wait_ge(s_pa, 3)
            sp.dma_start(wa[:, :, :], w_o[0].rearrange("(k p) n -> p k n", p=P)).then_inc(s_wa, 16)
            sp.wait_ge(s_pa, 6)
            sp.dma_start(b2s, b2[0]).then_inc(s_b2, 16)
            sp.dma_start(wple, w_ple[0].rearrange("(k p) n -> p k n", p=P)).then_inc(s_nx, 16)
            for t, src in enumerate((p_prompt[0:P], p_prompt[P:SEQ], p_sample)):
                sp.dma_start(prow[0:ROWS[t], t, :], src).then_inc(s_nx, 16)
            for c in range(3, 6):
                load_chunk(sp, 0, c)
            sp.wait_ge(s_pa, 9)
            sp.dma_start(wa[:, :, :], w_ple_gate[0].rearrange("(k p) n -> p k n", p=P)).then_inc(s_nx, 16)
            while pieces:
                shift_piece(sp)

        @block.tensor
        def _(pe):
            xs_products(pe, hAT, KT, wa, [(s_wa, 16)], 0, pX, pX2, s_pa, s_pe_)
            xs_products(pe, hBT, 4, wpb, [(s_wb, 16)], 3, pX, pX2, s_pa, s_pe_)
            for t in range(2):
                pe.wait_ge(s_u, t + 1)
                for half in range(2):
                    if t:
                        pe.wait_ge(s_ute, half + 1)
                    for q in range(4):
                        k = 4 * half + q
                        last = pe.transpose(pT[:, half, q * P:(q + 1) * P], zg[:, t, k * P:(k + 1) * P], ident)
                    last.then_inc(s_ut, 1)
            pe.wait_ge(s_u, 3)
            for half in range(2):
                pe.wait_ge(s_ute, 3 + half)
                pe.transpose(pT[:, half, 0:P], zgw[:, 0, half * P:(half + 1) * P], ident).then_inc(s_ut, 1)
            xs_products(pe, uT, KT, wa, [(s_wa, 32), (s_ute, 6)], 6, pX, pX2, s_pa, s_pe_)
            for t in range(3):
                pe.wait_ge(s_x2, t + 1)
                for half in range(2):
                    if t:
                        pe.wait_ge(s_x2e, 2 * (t - 1) + half + 1)
                    for q in range(4):
                        k = 4 * half + q
                        last = pe.transpose(pT[:, half, q * P:q * P + ROWS[t]], x2[0:ROWS[t], t, k * P:(k + 1) * P],
                                            ident[0:ROWS[t], 0:ROWS[t]])
                    last.then_inc(s_x2t, 1)
            pe.wait_ge(s_sm, 48)
            pe.wait_ge(s_x2e, 6)
            for t in range(3):
                for k in range(KT):
                    last = pe.matmul(pR[0:ROWS[t], t * E:(t + 1) * E], uT[:, k, t * P:t * P + ROWS[t]], wr[:, k, :],
                                     start=(k == 0), stop=(k == KT - 1))
            last.then_inc(s_lg, 1)
            pe.wait_ge(s_mask, 1)
            for t in range(3):
                for s in range(t + 1):
                    pe.matmul(pR[:, 128 + t * E:128 + (t + 1) * E], CAc("before") if s == t else ones, mask[:, s, :],
                              start=(s == 0), stop=(s == t))
            for t in range(3):
                last = pe.matmul(pR[:, 256:256 + E], ones, mask[:, t, :], start=(t == 0), stop=(t == 2))
            last.then_inc(s_rk, 1)
            pe.wait_ge(s_mask, 2)
            for t in range(3):
                last = pe.transpose(pT[0:E, 0, t * P:t * P + ROWS[t]], work[0][0:ROWS[t], t, :], ident[0:ROWS[t], 0:ROWS[t]])
            last.then_inc(s_gt, 1)
            pe.wait_ge(s_gte, 1)
            pe.wait_ge(s_b2, 16)
            for t in range(2):
                for c in range(2):
                    last = pe.matmul(pX[t][:, c, :], gT[:, t * P:(t + 1) * P], b2s[:, c * 512:(c + 1) * 512], start=True, stop=True)
                last.then_inc(s_bb, 1)
            for c in range(2):
                last = pe.matmul(pX2[32 * c:32 * c + 32, :], gT[:, SEQ:TOK], b2s[:, c * 512:(c + 1) * 512], start=True, stop=True)
            last.then_inc(s_bb, 1)

        @block.scalar
        def _(act):
            for t in range(2):
                for half in range(2):
                    n = 2 * t + half
                    act.wait_ge(s_ut, n + 1)
                    act.wait_ge(s_pa, 6)
                    act.activation(uT[:, 4 * half:4 * half + 4, t * P:(t + 1) * P], pT[:, half, :].rearrange("p (q n) -> p q n", q=4),
                                   ACT.Copy).then_inc(s_ute, 1)
            for half in range(2):
                act.wait_ge(s_ut, 5 + half)
                act.activation(uT[:, half:KT:2, SEQ:TOK], pT[:, half, 0:P].rearrange("p (g n) -> p g n", g=4), ACT.Copy).then_inc(s_ute, 1)
            for t in range(3):
                R = ROWS[t]
                act.wait_ge(s_h1, t + 1)
                act.activation(x2[0:R, t, :], h[0:R, t, :], ACT.Square, accum_out=st3[0:R, t:t + 1]).then_inc(s_sq, 1)
                act.wait_ge(s_mq, t + 1)
                act.activation(st3[0:R, t:t + 1], st3[0:R, t:t + 1], ACT.Sqrt).then_inc(s_rt, 1)
            act.wait_ge(s_mask, 1)
            act.activation(work[0][:, :, :], work[0][:, :, :], ACT.Exp).then_inc(s_ex, 1)
            act.wait_ge(s_gt, 1)
            act.activation(gT[:, :], pT[0:E, 0, 0:TOK], ACT.Copy).then_inc(s_gte, 1)

        @block.vector
        def _(dve):
            link = Chain(dve)
            flat = lambda x: x[:, :, :].rearrange("p c n -> p (c n)")
            src = (flat(pX[0]), flat(pX[1]), pX2[:, 0:D // 4])
            ga = (zg[:, 0, 0:D], zg[:, 1, 0:D], zgw[:, 0, :])
            gb = (zg[:, 0, D:2 * D], zg[:, 1, D:2 * D], zgw[:, 1, :])
            for n in range(6):
                dve.wait_ge(s_pa, n + 1)
                z = (ga, gb)[n // 3][n % 3]
                dve.tensor_tensor(z, src[n % 3], z, ALU.mult).then_inc(s_pe_, 1)
                if n >= 3:
                    dve.wait_ge(s_pe_, n + 1)
                    dve.tensor_tensor(ga[n % 3], ga[n % 3], gb[n % 3], ALU.add).then_inc(s_u, 1)
            for t in range(2):
                dve.wait_ge(s_pa, 7 + t)
                dve.tensor_tensor(h[:, t, :], src[t], h[:, t, :], ALU.add).then_inc(s_h1, 1)
            dve.wait_ge(s_pa, 9)
            for g in range(4):
                ins = dve.tensor_tensor(h[0:NS, 2, g * 256:(g + 1) * 256], pX2[32 * g:32 * g + 32, 0:256],
                                        h[0:NS, 2, g * 256:(g + 1) * 256], ALU.add)
                if g < 3:
                    ins.then_inc(s_steps, 1)
                    link.n += 1
            ins.then_inc(s_h1, 1)
            dve.wait_ge(s_steps, link.n)
            for t in range(3):
                R = ROWS[t]
                dve.wait_ge(s_sq, t + 1)
                dve.tensor_scalar(st3[0:R, t:t + 1], st3[0:R, t:t + 1], 1.0 / D, EPS, ALU.mult, ALU.add).then_inc(s_mq, 1)
                dve.wait_ge(s_rt, t + 1)
                link(dve.reciprocal(st3[0:R, 3 + t:4 + t], st3[0:R, t:t + 1]))
                if t == 2:
                    link(dve.memset(x2[:, 2, :], 0.0))
                dve.tensor_scalar(x2[0:R, t, :], h[0:R, t, :], st3[0:R, 3 + t:4 + t], None, ALU.mult).then_inc(s_x2, 1)
            for t in range(3):
                R = ROWS[t]
                for half in range(2):
                    dve.wait_ge(s_x2t, 2 * t + half + 1)
                    dve.tensor_tensor(uT[:, 4 * half:4 * half + 4, t * P:t * P + R],
                                      pT[:, half, :].rearrange("p (q n) -> p q n", q=4)[:, :, 0:R],
                                      n2c[:, 4 * half:4 * half + 4].unsqueeze(2).to_broadcast([P, 4, R]), ALU.mult).then_inc(s_x2e, 1)
            link(dve.memset(Lg[:, :, :], 0.0))
            dve.wait_ge(s_lg, 1)
            link.many(*[dve.tensor_tensor(Lg[0:ROWS[t], t, :], pR[0:ROWS[t], t * E:(t + 1) * E], brb[0:ROWS[t], :], ALU.add) for t in range(3)])
            link.many(*[dve.max(m8[:, t, :], Lg[:, t, :]) for t in range(3)])
            wide = lambda x, n: x.to_broadcast([P, 3, n])
            v4 = wide(m8[:, :, TOPK - 1:TOPK], E)
            ex, gt, eq, pc = work
            link.many(dve.tensor_tensor(gt[:, :, :], Lg[:, :, :], v4, ALU.is_gt),
                      dve.tensor_tensor(eq[:, :, :], Lg[:, :, :], v4, ALU.is_equal),
                      dve.tensor_tensor(ex[:, :, :], Lg[:, :, :], wide(m8[:, :, 0:1], E), ALU.subtract))
            link.many(dve.tensor_copy(pc[:, :, :], eq[:, :, :]),
                      dve.tensor_reduce(st3[:, 6:9], gt[:, :, :], AX.X, ALU.add))
            a, b, d = pc, mask, 1
            while d < E:
                link.many(dve.tensor_tensor(b[:, :, d:E], a[:, :, d:E], a[:, :, 0:E - d], ALU.add),
                          dve.tensor_copy(b[:, :, 0:d], a[:, :, 0:d]))
                a, b, d = b, a, 2 * d
            link(dve.tensor_tensor(b[:, :, :], a[:, :, :], wide(st3[:, 6:9].unsqueeze(2), E), ALU.add))
            link(dve.tensor_scalar(b[:, :, :], b[:, :, :], TOPK + 0.5, None, ALU.is_lt))
            link(dve.tensor_tensor(b[:, :, :], b[:, :, :], eq[:, :, :], ALU.mult))
            link(dve.tensor_tensor(gt[:, :, :], gt[:, :, :], b[:, :, :], ALU.add))
            dve.tensor_tensor(mask[:, :, :], gt[:, :, :], wide(CAc("valid").unsqueeze(2), E), ALU.mult).then_inc(s_mask, 1)
            dve.wait_ge(s_mask, 1)
            dve.wait_ge(s_ex, 1)
            link(dve.tensor_tensor(ex[:, :, :], ex[:, :, :], mask[:, :, :], ALU.mult))
            link(dve.tensor_reduce(st3[:, 6:9], ex[:, :, :], AX.X, ALU.add))
            link(dve.tensor_scalar(st3[:, 6:9], st3[:, 6:9], 1e-30, None, ALU.max))
            link(dve.reciprocal(st3[:, 9:12], st3[:, 6:9]))
            dve.tensor_tensor(ex[:, :, :], ex[:, :, :], wide(st3[:, 9:12].unsqueeze(2), E), ALU.mult).then_inc(s_mask, 1)
            dve.wait_ge(s_mask, 2)
            FAR = 4096.0
            link(dve.memset(RG[:, E:E + 1, :], -FAR))
            link(dve.tensor_copy(RG[:, 0:E, 3:6], ex[:, :, :].rearrange("p t e -> p e t")))
            dve.wait_ge(s_rk, 1)
            link(dve.tensor_scalar(eq[:, :, :], pR[:, 128:128 + 3 * E].rearrange("p (t e) -> p t e", t=3), FAR, None, ALU.add))
            link(dve.tensor_tensor(eq[:, :, :], eq[:, :, :], mask[:, :, :], ALU.mult))
            link(dve.tensor_scalar(RG[:, 0:E, 0:3], eq[:, :, :].rearrange("p t e -> p e t"), -FAR, None, ALU.add))
            link(dve.tensor_reduce(st3[:, 6:7], pR[:, 256:256 + E], AX.X, ALU.max))
            link(dve.tensor_copy(nmax[:, :], st3[:, 6:7]))
            for t in range(2):
                dve.wait_ge(s_bb, t + 1)
                link(dve.tensor_tensor(h[:, t, :], src[t], h[:, t, :], ALU.add))
            dve.wait_ge(s_bb, 3)
            link.many(*[dve.tensor_tensor(acc2[32 * c:32 * c + 32, :], pX2[32 * c:32 * c + 32, :], h[0:NS, 2, c * 512:(c + 1) * 512], ALU.add)
                        for c in range(2)])
            link(dve.memset(GAB[:, :, :], 0.0))
    ap.close()

    ap = ExitStack()
    pG, pL, pY = pb(ap, "eG", [P, 512]), pb(ap, "eL", [P, 512]), pb(ap, "eY", [P, 512])
    pSc = [pb(ap, f"eS{i}", [P, 512]) for i in range(3)]
    pA, pB = pb(ap, "eA", [P, 512]), pb(ap, "eB", [P, 512])
    names = ("used", "b1", "col", "selU", "selG", "g1", "xg", "g2", "xgT", "h", "glu", "lin", "sg", "prod", "act",
             "at", "acT", "ysb", "gt", "gab", "sc", "acc", "rank")
    S = {n: sem(ap, "e_" + n) for n in names}
    OUT5 = 5

    def experts(p, pe=None, act=None, dve=None, sp=None):
        def w(eng, name, value, per):
            eng.wait_ge(S[name], value + per * p)

        def first(e, p):
            return isinstance(e, int) and isinstance(p, int) and e == 0 and p == 0

        def each(eng, body, start=1):
            with eng.Fori(start, E) as e:
                body(e)

        if sp is not None:
            def loads(e):
                w(sp, "h", e, E)
                sp.dma_start(b1s[:, :], b1[bass.ds(e, 1), :, :, :].rearrange("x a b n -> (x a) (b n)")).then_inc(S["b1"], 16)
                for c in range(6):
                    w(sp, "used", 6 * e - 5 + c, 6 * E)
                    load_chunk(sp, e, c)
            if not isinstance(p, int):
                w(sp, "h", 0, E)
                sp.dma_start(b1s[:, :], b1[0].rearrange("a b n -> a (b n)")).then_inc(S["b1"], 16)
                w(sp, "used", 0, 6 * E)
                for c in range(6):
                    load_chunk(sp, 0, c)
            each(sp, loads)

        if pe is not None:
            def gather(e):
                w(pe, "selU", e + 1, E + 1)
                for t in range(3):
                    for c in range(2):
                        last = pe.matmul(pA[64 * c:64 * c + 64, :], selU[:, t, 0:CAP], x2[:, t, c * 512:(c + 1) * 512],
                                         start=(t == 0), stop=(t == 2))
                last.then_inc(S["g1"], 1)
                w(pe, "xg", e + 1, E + 1)
                if not isinstance(e, int) or e:
                    w(pe, "gab", 2 * e, 2 * E)
                for j in range(4):
                    last = pe.transpose(pB[:, j * P:(j + 1) * P], xg[:, j * P:(j + 1) * P], ident)
                last.then_inc(S["g2"], 1)

            def up(e):
                w(pe, "xgT", e + 1, E + 1)
                if not first(e, p):
                    w(pe, "b1", 16 * e, 16 * E)
                for i, ps in enumerate((pG, pL)):
                    last = pe.matmul(ps[:, :], CAc("halves")[0:2], b1s[:, i * 512:(i + 1) * 512], start=True, stop=False,
                                     skip_group_check=True)
                last.then_inc(S["h"], 1)
                for k in range(KT):
                    c = k // 2
                    if k % 2 == 0:
                        pe.wait_ge(s_ring[c], 16 * (e + 1) + 16 * E * p)
                    for i, ps in enumerate((pG, pL)):
                        for hh in range(2):
                            col = (k % 2) * 2 * FF + i * FF + hh * 512
                            last = pe.matmul(ps[64 * hh:64 * hh + 64, :], xgT[:, k % 4, (k // 4) * CAP:(k // 4 + 1) * CAP],
                                             ring[:, c, col:col + 512], start=False, stop=(k == KT - 1), skip_group_check=True)
                    if k % 2:
                        last.then_inc(S["used"], 1)

            def gates_t(e):
                w(pe, "selG", e + 1, E + 1)
                w(pe, "xgT", e + 1, E + 1)
                for t in range(3):
                    last = pe.transpose(pB[:, t * P:t * P + ROWS[t]], selG[0:ROWS[t], t, :], ident[0:ROWS[t], 0:ROWS[t]])
                last.then_inc(S["gt"], 1)

            def scatter(e):
                w(pe, "ysb", e + 1, E)
                w(pe, "gab", 2 * e + 2, 2 * E)
                for n in range(OUT5):
                    if not first(e, p) or n >= 3:
                        w(pe, "acc", OUT5 * e + (-1, 0, -2, 1, 2)[n], OUT5 * E)
                    ps = pSc[n % 3]
                    if n < 4:
                        t, c = n // 2, n % 2
                        last = pe.matmul(ps[:, :], GAB[:, c, t * P:(t + 1) * P], ysb, start=True, stop=True)
                    else:
                        for c in range(2):
                            last = pe.matmul(ps[32 * c:32 * c + 32, :], GAB[:, c, SEQ:TOK], ysb, start=True, stop=True)
                    last.then_inc(S["sc"], 1)

            def down(e):
                w(pe, "act", e + 1, E)
                w(pe, "xgT", e + 2, E + 1)
                for j in range(4):
                    last = pe.transpose(pB[:, j * P:(j + 1) * P], sg[:, j * P:(j + 1) * P], ident)
                last.then_inc(S["at"], 1)
                w(pe, "acT", e + 1, E)
                for k in range(KT):
                    c = 4 + k // 4
                    if k % 4 == 0:
                        pe.wait_ge(s_ring[c], 16 * (e + 1) + 16 * E * p)
                    for hh in range(2):
                        col = (k % 4) * D + hh * 512
                        last = pe.matmul(pY[64 * hh:64 * hh + 64, :], acT[:, k % 4, (k // 4) * CAP:(k // 4 + 1) * CAP],
                                         ring[:, c, col:col + 512], start=(k == 0), stop=(k == KT - 1))
                    if k % 4 == 3:
                        last.then_inc(S["used"], 1)

            gather(0)
            up(0)
            gates_t(0)
            gather(1)
            down(0)
            up(1)
            gates_t(1)
            scatter(0)
            gather(2)
            down(1)

            def body(e):
                up(e)
                gates_t(e)
                scatter(e - 1)
                gather(e + 1)
                down(e)
            each(pe, body, 2)
            scatter(E - 1)

        if act is not None:
            def rows(e):
                w(act, "g1", e + 1, E + 1)
                act.activation(xg, pA[:, :], ACT.Copy).then_inc(S["xg"], 1)

            def gates_out(e):
                w(act, "gt", e + 1, E)
                if not first(e, p):
                    w(act, "sc", OUT5 * e, OUT5 * E)
                act.activation(GAB[0:64, 0, :], pB[0:64, 0:TOK], ACT.Copy).then_inc(S["gab"], 1)
                act.activation(GAB[64:P, 1, :], pB[64:P, 0:TOK], ACT.Copy).then_inc(S["gab"], 1)

            def ffn(e):
                w(act, "at", e + 1, E)
                act.activation(acT.rearrange("p j n -> p (j n)"), pB[:, :], ACT.Copy).then_inc(S["acT"], 1)
                w(act, "used", 6 * (e + 1), 6 * E)
                act.activation(ysb, pY[:, :], ACT.Copy).then_inc(S["ysb"], 1)

            def sigm(e):
                w(act, "glu", e + 1, E)
                act.activation(sg, glu, ACT.Sigmoid, scale=ALPHA).then_inc(S["sg"], 1)

            rows(0)
            sigm(0)
            gates_out(0)
            rows(1)
            ffn(0)

            def body(e):
                sigm(e)
                gates_out(e)
                rows(e + 1)
                ffn(e)
            each(act, body)

        if dve is not None:
            def select(e):
                if not first(e, p):
                    w(dve, "g1", e, E + 1)
                    w(dve, "gt", e, E)
                dve.tensor_copy(rg6[:, :], RG[:, bass.ds(e, 1), :].rearrange("p a b -> p (a b)")).then_inc(S["col"], 1)
                w(dve, "col", e + 1, E + 1)
                slot = CAc("slot").unsqueeze(1).to_broadcast([P, 3, P])
                dve.tensor_tensor(selU[:, :, :], slot, rg6[:, 0:3].unsqueeze(2).to_broadcast([P, 3, P]), ALU.is_equal).then_inc(S["selU"], 1)
                w(dve, "selU", e + 1, E + 1)
                dve.tensor_tensor(selG[:, :, :], selU[:, :, :], rg6[:, 3:6].unsqueeze(2).to_broadcast([P, 3, P]), ALU.mult).then_inc(S["selG"], 1)

            def rows_t(e):
                w(dve, "g2", e + 1, E + 1)
                dve.tensor_tensor(xgT.rearrange("p j (c n) -> p j c n", c=2), pB[:, :].rearrange("p (j c n) -> p j c n", j=4, c=2),
                                  n2c.rearrange("p (c j) -> p j c", c=2).unsqueeze(3).to_broadcast([P, 4, 2, CAP]),
                                  ALU.mult).then_inc(S["xgT"], 1)

            def swiglu(e):
                w(dve, "used", 6 * e + 4, 6 * E)
                dve.tensor_scalar(glu, pG[:, :], LIMIT, None, ALU.min).then_inc(S["glu"], 1)
                dve.tensor_scalar(lin, pL[:, :], LIMIT, -LIMIT, ALU.min, ALU.max).then_inc(S["lin"], 1)
                w(dve, "lin", e + 1, E)
                dve.scalar_tensor_tensor(out=lin, in0=lin, scalar=1.0, in1=glu, op0=ALU.add, op1=ALU.mult).then_inc(S["prod"], 1)
                w(dve, "prod", e + 1, E)
                w(dve, "sg", e + 1, E)
                dve.tensor_tensor(sg, sg, lin, ALU.mult).then_inc(S["act"], 1)

            def add(e):
                for n in range(OUT5):
                    w(dve, "sc", OUT5 * e + n + 1, OUT5 * E)
                    ps = pSc[n % 3]
                    if n < 4:
                        x = h[:, n // 2, (n % 2) * 512:(n % 2 + 1) * 512]
                        dve.tensor_tensor(x, ps[:, :], x, ALU.add).then_inc(S["acc"], 1)
                    else:
                        dve.tensor_tensor(acc2, ps[0:2 * NS, :], acc2, ALU.add).then_inc(S["acc"], 1)

            if not isinstance(p, int):
                w(dve, "acc", 0, OUT5 * E)
                dve.tensor_scalar(RG[:, :, 0:3], RG[:, :, 0:3], -float(CAP), None, ALU.add).then_inc(S["rank"], 1)
                dve.wait_ge(S["rank"], p)
            select(0)
            rows_t(0)
            swiglu(0)
            select(1)
            rows_t(1)

            def body(e):
                swiglu(e)
                select(e + 1)
                add(e - 1)
                rows_t(e + 1)
            each(dve, body)
            add(E - 1)

    with nc.Block() as block:
        def passes(eng, **kw):
            experts(0, **kw)
            most = eng.value_load(nmax[0:1, 0:1], min_val=0, max_val=TOK)
            with eng.If(most > CAP):
                with eng.Fori(1, PASSES) as p:
                    experts(p, **kw)

        @block.sync
        def _(sp):
            passes(sp, sp=sp)

        @block.tensor
        def _(pe):
            passes(pe, pe=pe)

        @block.scalar
        def _(act):
            passes(act, act=act)

        @block.vector
        def _(dve):
            passes(dve, dve=dve)
    ap.close()
    ap = ExitStack()
    pX = [pb(ap, "fX0", [P, 2, 512]), pb(ap, "fX1", [P, 2, 512])]
    pX2 = pb(ap, "fX2", [P, 512])
    pT = pb(ap, "fT", [P, 2, 512])
    rflat = ring[:, :, :].rearrange("p c n -> p (c n)")
    sgp = rflat[:, 0:2 * D].rearrange("p (t n) -> p t n", t=2)
    sgw = rflat[:, 2 * D:2 * D + 256]
    tmp2 = rflat[0:NS, 3 * D:4 * D]
    nfb = rflat[:, 4 * D:5 * D]
    y = rflat[:, 5 * D:8 * D].rearrange("p (t n) -> p t n", t=3)
    prT = hflat[:, 0:2 * TOK].rearrange("p (k n) -> p k n", k=2)
    s_nf = sem(ap, "s_normf")
    s_pa, s_pe_ = sem(ap, "f_products"), sem(ap, "f_products_out")
    s_pt, s_pte, s_h3, s_y = (sem(ap, "f_" + n) for n in ("ptrans", "pT", "h3", "y"))

    with nc.Block() as block:
        @block.sync
        def _(sp):
            sp.dma_start(nfb, norm_f.partition_broadcast(P)).then_inc(s_nf, 16)
            for t, dst in enumerate((y_prompt[0:P], y_prompt[P:SEQ], y_sample)):
                sp.wait_ge(s_y, t + 1)
                store(sp, dst, y[0:ROWS[t], t, :])
            sp.wait_ge(s_shift, n_shift)
            sp.wait_ge(s_stored, n_stored[0])

        @block.tensor
        def _(pe):
            pe.wait_ge(s_nx, 80)
            for q in range(2):
                for t in (2, 0, 1):
                    last = pe.transpose(pX[0][:, q, t * P:t * P + ROWS[t]], prow[0:ROWS[t], t, q * P:(q + 1) * P],
                                        ident[0:ROWS[t], 0:ROWS[t]])
                last.then_inc(s_pt, 1)
            for t in range(3):
                pe.wait_ge(s_x2, 4 + t)
                for half in range(2):
                    if t:
                        pe.wait_ge(s_x2e, 6 + 2 * (t - 1) + half + 1)
                    for q in range(4):
                        k = 4 * half + q
                        last = pe.transpose(pT[:, half, q * P:q * P + ROWS[t]], x2[0:ROWS[t], t, k * P:(k + 1) * P],
                                            ident[0:ROWS[t], 0:ROWS[t]])
                    last.then_inc(s_x2t, 1)
            xs_products(pe, uT, KT, wa, [(s_x2e, 12), (s_pte, 1)], 0, pX, pX2, s_pa, s_pe_)
            xs_products(pe, prT, 2, wple, [], 3, pX, pX2, s_pa, s_pe_)

        @block.scalar
        def _(act):
            act.wait_ge(s_pt, 2)
            act.activation(prT, pX[0][:, :, 0:TOK], ACT.Copy).then_inc(s_pte, 1)
            for t in range(3):
                R = ROWS[t]
                act.wait_ge(s_h1, 4 + t)
                act.activation(x2[0:R, t, :], h[0:R, t, :], ACT.Square, accum_out=st3[0:R, t:t + 1]).then_inc(s_sq, 1)
            for t in range(3):
                R = ROWS[t]
                act.wait_ge(s_mq, 4 + t)
                act.activation(st3[0:R, t:t + 1], st3[0:R, t:t + 1], ACT.Sqrt).then_inc(s_rt, 1)
            src = (pX[0][:, :, :].rearrange("p c n -> p (c n)"), pX[1][:, :, :].rearrange("p c n -> p (c n)"), pX2[:, 0:D // 4])
            for t, dst in enumerate((sgp[:, 0, :], sgp[:, 1, :], sgw)):
                act.wait_ge(s_pa, t + 1)
                act.activation(dst, src[t], ACT.Sigmoid).then_inc(s_pe_, 1)
            for t in range(3):
                R = ROWS[t]
                act.wait_ge(s_h3, t + 1)
                act.activation(y[0:R, t, :], h[0:R, t, :], ACT.Square, accum_out=st3[0:R, 6 + t:7 + t]).then_inc(s_sq, 1)
            for t in range(3):
                R = ROWS[t]
                act.wait_ge(s_mq, 7 + t)
                act.activation(st3[0:R, 6 + t:7 + t], st3[0:R, 6 + t:7 + t], ACT.Sqrt).then_inc(s_rt, 1)

        @block.vector
        def _(dve):
            link = Chain(dve)

            def rstd(n, c, t):
                R = ROWS[t]
                dve.wait_ge(s_sq, n + t + 1)
                dve.tensor_scalar(st3[0:R, c + t:c + t + 1], st3[0:R, c + t:c + t + 1], 1.0 / D, EPS, ALU.mult, ALU.add).then_inc(s_mq, 1)

            link(dve.tensor_copy(h[0:NS, 2, 0:512], acc2[0:NS, :]))
            link(dve.tensor_copy(h[0:NS, 2, 512:D], acc2[NS:2 * NS, :]))
            for t in range(3):
                dve.tensor_copy(rg6[:, t:t + 1], nmax[:, :]).then_inc(s_h1, 1)
            for t in range(3):
                rstd(3, 0, t)
            for t in range(3):
                R = ROWS[t]
                dve.wait_ge(s_rt, 4 + t)
                link(dve.reciprocal(st3[0:R, 3 + t:4 + t], st3[0:R, t:t + 1]))
                dve.tensor_scalar(x2[0:R, t, :], h[0:R, t, :], st3[0:R, 3 + t:4 + t], None, ALU.mult).then_inc(s_x2, 1)
            for t in range(3):
                R = ROWS[t]
                for half in range(2):
                    dve.wait_ge(s_x2t, 6 + 2 * t + half + 1)
                    dve.tensor_tensor(uT[:, 4 * half:4 * half + 4, t * P:t * P + R],
                                      pT[:, half, :].rearrange("p (q n) -> p q n", q=4)[:, :, 0:R],
                                      n3c[:, 4 * half:4 * half + 4].unsqueeze(2).to_broadcast([P, 4, R]), ALU.mult).then_inc(s_x2e, 1)
            src = (pX[0][:, :, :].rearrange("p c n -> p (c n)"), pX[1][:, :, :].rearrange("p c n -> p (c n)"), pX2[:, 0:D // 4])
            dve.wait_ge(s_pe_, 3)
            for t, g in enumerate((sgp[:, 0, :], sgp[:, 1, :], sgw)):
                dve.wait_ge(s_pa, 4 + t)
                link(dve.tensor_tensor(g, src[t], g, ALU.mult))
                if t < 2:
                    dve.tensor_tensor(h[:, t, :], h[:, t, :], g, ALU.add).then_inc(s_h3, 1)
                else:
                    link.many(*[dve.tensor_copy(tmp2[:, k * 256:(k + 1) * 256], sgw[32 * k:32 * k + 32, :]) for k in range(4)])
                    dve.tensor_tensor(h[0:NS, 2, :], h[0:NS, 2, :], tmp2, ALU.add).then_inc(s_h3, 1)
            for t in range(3):
                rstd(6, 6, t)
            dve.wait_ge(s_nf, 16)
            for t in range(3):
                R = ROWS[t]
                dve.wait_ge(s_rt, 7 + t)
                link(dve.reciprocal(st3[0:R, 9 + t:10 + t], st3[0:R, 6 + t:7 + t]))
                dve.scalar_tensor_tensor(out=y[0:R, t, :], in0=h[0:R, t, :], scalar=st3[0:R, 9 + t:10 + t], in1=nfb[0:R],
                                         op0=ALU.mult, op1=ALU.mult).then_inc(s_y, 1)
    ap.close()
    front.close()
    top.close()


def kernel(**inputs):
    import concourse.bacc as _bacc
    from concourse.bass_utils import run_bass_kernel_spmd as _run

    nc = _bacc.Bacc("TRN2", target_bir_lowering=False, num_devices=1)
    arrays = lay_out(inputs)
    args = {n: nc.dram_tensor(n, a.shape, mybir.dt.from_np(a.dtype), kind="ExternalInput").ap() for n, a in arrays.items()}
    for n, shape in OUT_SHAPES.items():
        args[n] = nc.dram_tensor(n, shape, F32, kind="ExternalOutput").ap()
    layer(nc, **args)
    r = _run(nc, [arrays], core_ids=[0])
    return arrange({n: r.results[0][n] for n in OUT_SHAPES})
```

```python
from contextlib import ExitStack

import numpy as np
import concourse.bass as bass
from concourse import mybir

F32 = mybir.dt.float32
F32R = mybir.dt.float32r
I32 = mybir.dt.int32
ALU = mybir.AluOpType
ACT = mybir.ActivationFunctionType
AX = mybir.AxisListType

P = 128
D = 1024
KT = D // P
SEQ = 256
NB, NT = 8, 4
NS = NB * NT
TOK = SEQ + NS
ROWS = (P, P, NS)
MH, MD = 4, 256
MW = MH * MD
AH, AD = 4, 128
GW = AH * AD
AW = 3 * GW
RH = AD // 8
PAST = 1024
GROUPS = ((128, 1), (512, 4), (2048, 16))
WB = tuple(min(w, PAST) for w, _ in GROUPS)
E = 32
TOPK = 4
FF = 1024
ALPHA, LIMIT = 1.702, 7.0
PLE = 256
EPS = 1e-6
NEG = -1e30
CAP = 64
PASSES = -(-TOK // CAP)

ZQ, ZK, ZV, ZO = 0, MW, 2 * MW, 3 * MW
ZAQ = 4 * MW
ZAK, ZAV = ZAQ + AW, ZAQ + 2 * AW
ZGA = ZAQ + 3 * AW
ZGB = ZGA + D
NZ = ZGB + D
GATE0 = 4 * MW
NKEY = P * 7
SKEY = NKEY + 3 * P


def constants():
    p = np.arange(P)[:, None]
    f = np.arange(P)[None, :]
    a = {}
    a["ident"] = (p == f)
    a["ones"] = np.ones((P, P))
    a["before"] = (p < f)
    a["halves"] = (p == f // CAP)
    a["valid"] = np.stack([np.ones(P), np.ones(P), np.arange(P) < NS], 1)
    a["slot"] = np.broadcast_to(f % CAP, (P, P))
    b = {}
    b["causal"] = np.where(p <= f, 0, NEG)
    am = np.full((P, 2, 3, SEQ), NEG)
    s = np.arange(SEQ)[None, :]
    for jt in range(2):
        for g, (win, dil) in enumerate(GROUPS):
            d = jt * P + p - s
            am[:, jt, g] = np.where((d >= 0) & (d % dil == 0) & (d <= win), 0, NEG)
    b["amask"] = am.reshape(P, -1)
    t = p % NT
    sm = np.full((P, SKEY), NEG)
    sm[:, 0:P] = np.where(f >= t, 0, NEG)
    for u in range(4):
        sm[:, (1 + u) * P:(2 + u) * P] = np.where(t == u, 0, NEG)
    for v in range(2):
        sm[:, (5 + v) * P:(6 + v) * P] = np.where(t == 2 * v + f // 64, 0, NEG)
    own = (p // NT == f // NT)
    sm[:, NKEY:NKEY + P] = np.where(own & (f <= p), 0, NEG)
    for g in (1, 2):
        sm[:, NKEY + g * P:NKEY + (g + 1) * P] = np.where(p == f, 0, NEG)
    b["smask"] = sm
    b["scausal"] = np.where(own & (p <= f), 0, NEG)
    bf = (np.arange(P) // NT) % NB
    b["bcol"] = np.broadcast_to((np.arange(NB)[:, None] == bf[None, :]).reshape(1, -1), (P, NB * P))
    b["brow"] = (bf[:, None] == np.arange(NB)[None, :])
    b["hcol"] = (p // NS == np.arange(MH)[None, :])
    b["bhsel"] = (p // NT == np.arange(NS)[None, :])
    hs = np.zeros((P, MH, P))
    for h in range(MH):
        hs[h, h] = 1
    b["hsel"] = hs.reshape(P, -1)
    half = RH
    inv = (1.0 / (np.float32(500000.0) ** (np.arange(0, 2 * half, 2, dtype=np.float32) / np.float32(2 * half)))).astype(np.float32)
    for name, pos in (("p0", np.arange(P)), ("p1", P + np.arange(P)), ("s", PAST + np.arange(P) % NT)):
        ang = pos.astype(np.float32)[:, None] * inv[None, :]
        a["cos" + name] = np.cos(ang)
        a["sin" + name] = np.sin(ang)
    out = []
    for d in (a, b):
        at, place = 0, {}
        for k, v in d.items():
            place[k] = (at, v.shape[1])
            at += v.shape[1]
        out += [np.concatenate([np.asarray(v, np.float32) for v in d.values()], 1), place]
    return out


CA, CA_AT, CB, CB_AT = constants()

CHUNK = 2 * MW
BLOCKS = ([(i * MW, MW) for i in range(4)] + [(ZAQ + i * GW, GW) for i in range(9)] + [(ZGA, D), (ZGB, D)])


def lay_out(x):
    x = {k: np.ascontiguousarray(v) for k, v in x.items()}
    a = {k: x[k] for k in ("x_prompt", "x_sample", "cache_k0", "cache_v0", "cache_k1", "cache_v1", "cache_k2",
                           "cache_v2", "w_in", "w_pa", "w_pb", "w_o", "w1", "w2", "b2", "w_ple",
                           "w_ple_gate", "norm_f", "b_router")}
    a["ca_in"], a["cb_in"] = CA, CB
    col = lambda v: v.reshape(-1, P).T
    a["norm_cols"] = np.concatenate([col(x[k][0]) for k in ("norm1", "m_norm", "norm2", "norm3")], 1)
    a["w_gates"] = x["w_in"][0][:, GATE0:GATE0 + 2 * MH].reshape(KT, P, 2 * MH).transpose(1, 0, 2)
    a["b_gates"] = np.stack([x["b_igate"][0], x["b_fgate"][0]], 1)
    a["b1"] = x["b1"].reshape(E, 2, 2, 512).transpose(0, 2, 1, 3)
    a["w_router"] = x["w_router"][0].reshape(KT, P, E).transpose(1, 0, 2)
    a["p_prompt"], a["p_sample"] = x["p_prompt"][0, 0], x["p_sample"][0].reshape(NS, PLE)
    C = x["state_C"][0].transpose(1, 0, 3, 2).reshape(MH, NB, 2, P, MD)
    a["CT"] = C.transpose(3, 0, 1, 2, 4)
    n = x["state_n"][0].transpose(1, 0, 2)
    a["n_rows"] = n.reshape(MH * NB, MD)
    a["n_tok"] = np.repeat(n.reshape(MH * NB, MD), NT, 0)
    a["m_rows"] = x["state_m"][0].T
    def keys(c):
        t = [x[f"cache_{c}{g}"][0] for g in range(3)]
        g1 = t[1].reshape(NB, P, 4, AH, AD).transpose(0, 2, 1, 3, 4)
        g2 = t[2].reshape(NB, 64, 16, AH, AD)[:, :, 0:4].transpose(0, 2, 1, 3, 4).reshape(NB, 2, 2, 64, AH, AD)
        return np.concatenate([t[0], g1.reshape(NB, 4 * P, AH, AD), g2.reshape(NB, 2 * P, AH, AD)], 1)
    a["KT_cache"] = keys("k").transpose(0, 3, 2, 1)
    a["VK"] = keys("v").reshape(NB, 7, P, GW).transpose(0, 2, 1, 3)
    return {k: np.ascontiguousarray(v) for k, v in a.items()}


OUT_SHAPES = dict(
    y_prompt=(SEQ, D), y_sample=(NS, D), C_p=(MH, MD, MD), n_p=(MH, MD), m_p=(MH, 1),
    k0_p=(1, 1, 128, AH, AD), v0_p=(1, 1, 128, AH, AD), k1_p=(1, 1, 256, AH, AD), v1_p=(1, 1, 256, AH, AD),
    k2_p=(1, 1, 256, AH, AD), v2_p=(1, 1, 256, AH, AD),
    C_s=(P, MH, NB, 2, MD), n_s=(MH * NB, MD), m_s=(MH, NB),
    k0_s=(1, NB, 128, AH, AD), v0_s=(1, NB, 128, AH, AD), k1_s=(1, NB, 512, AH, AD), v1_s=(1, NB, 512, AH, AD),
    k2_s=(1, NB, 1024, AH, AD), v2_s=(1, NB, 1024, AH, AD))


def arrange(r):
    r = {k: np.asarray(v) for k, v in r.items()}
    r["y_prompt"] = r["y_prompt"].reshape(1, SEQ, D)
    r["y_sample"] = r["y_sample"].reshape(NB, NT, D)
    r["C_p"] = r["C_p"].reshape(1, 1, MH, MD, MD)
    r["n_p"] = r["n_p"].reshape(1, 1, MH, MD)
    r["m_p"] = r["m_p"].reshape(1, 1, MH)
    r["C_s"] = np.ascontiguousarray(r["C_s"].transpose(2, 1, 4, 3, 0).reshape(1, NB, MH, MD, MD))
    r["n_s"] = np.ascontiguousarray(r["n_s"].reshape(MH, NB, MD).transpose(1, 0, 2))[None]
    r["m_s"] = np.ascontiguousarray(r["m_s"].T)[None]
    return tuple(r[k] for k in OUT_SHAPES)


def layer(nc, x_prompt, x_sample, cache_k0, cache_v0, cache_k1, cache_v1, cache_k2, cache_v2, w_in, w_pa, w_pb,
          w_o, w1, w2, b2, w_ple, w_ple_gate, norm_f, b_router, ca_in, cb_in, norm_cols, w_gates, b_gates, b1,
          w_router, p_prompt, p_sample, CT, n_rows, n_tok, m_rows, KT_cache, VK,
          y_prompt, y_sample, C_p, n_p, m_p, k0_p, v0_p, k1_p, v1_p, k2_p, v2_p,
          C_s, n_s, m_s, k0_s, v0_s, k1_s, v1_s, k2_s, v2_s):
    caches = ((cache_k0, cache_v0), (cache_k1, cache_v1), (cache_k2, cache_v2))
    outs_p = ((k0_p, v0_p), (k1_p, v1_p), (k2_p, v2_p))
    outs_s = ((k0_s, v0_s), (k1_s, v1_s), (k2_s, v2_s))
    top = ExitStack()

    def sem(stack, name):
        return stack.enter_context(nc.semaphore(name))

    def sb(stack, name, shape, dt=F32):
        return stack.enter_context(nc.sbuf_tensor(name, shape, dt))

    def pb(stack, name, shape):
        return stack.enter_context(nc.psum_tensor(name, shape, F32))

    s_steps = sem(top, "s_steps")
    steps = [0]

    class Chain:

        def __init__(self, eng):
            self.eng, self.s, self.n = eng, s_steps, steps[0]

        def __call__(self, ins):
            ins.then_inc(self.s, 1)
            self.n += 1
            steps[0] = self.n
            self.eng.wait_ge(self.s, self.n)

        def many(self, *instructions):
            for ins in instructions:
                ins.then_inc(self.s, 1)
            self.n += len(instructions)
            steps[0] = self.n
            self.eng.wait_ge(self.s, self.n)

    ca = sb(top, "ca", [P, CA.shape[1]])
    cols = sb(top, "cols", [P, 4 * KT])
    n1c, mnc, n2c, n3c = (cols[:, i * KT:(i + 1) * KT] for i in range(4))
    h = sb(top, "h", [P, 3, D])
    s_stored = sem(top, "s_stored")
    s_shift = sem(top, "s_shift")
    n_stored = [0]
    s_hload = sem(top, "s_hload")

    def CAc(name):
        o, n = CA_AT[name]
        return ca[:, o:o + n]

    ident, ones = CAc("ident"), CAc("ones")

    def store(eng, dst, src):
        eng.dma_start(dst, src).then_inc(s_stored, 16)
        n_stored[0] += 16

    pieces = []
    for g in range(3):
        for c in range(2):
            step = NB // max(1, WB[g] // 256)
            for b in range(0, NB, step):
                pieces.append((g, c, b, step))

    def shift_piece(eng):
        if pieces:
            g, c, b, n = pieces.pop(0)
            eng.dma_start(outs_s[g][c][0, b:b + n, 0:WB[g] - NT].rearrange("b r h e -> b r (h e)"),
                          caches[g][c][0, b:b + n, NT:WB[g]].rearrange("b r h e -> b r (h e)")).then_inc(s_shift, 16)
    n_shift = 16 * len(pieces)

    front = ExitStack()
    zg = sb(front, "zg", [P, 2, 2 * D])
    zgw = sb(front, "zgw", [P, 2, D // 4])
    xT = sb(front, "xT", [P, KT, TOK])
    hAT = xT
    hBT = sb(front, "hBT", [P, AH, TOK])
    za = sb(front, "za", [P, 2, 3 * AW])
    zaflat = za[:, :, :].rearrange("p t n -> p (t n)")
    wa = zaflat[:, 0:KT * D].rearrange("p (k n) -> p k n", k=KT)
    s_wa = sem(front, "s_wa")
    mid = ExitStack()
    zm = sb(mid, "zm", [P, 2, 3, MW])
    vaug = sb(mid, "vaug", [P, 2, MH, MD + 1])
    zw = sb(mid, "zw", [P, 4, MD])
    zaw = sb(mid, "zaw", [P, 9, AD])
    grow = sb(mid, "grow", [MH, 2, TOK])

    st = ExitStack()
    NW, NR = 2, 4
    wraw = sb(st, "wraw", [P, NR, CHUNK])
    whi = sb(st, "whi", [P, NW, CHUNK], F32R)
    wlo = sb(st, "wlo", [P, NW, CHUNK], F32R)
    xhi = sb(st, "xhi", [P, KT, TOK], F32R)
    xlo = sb(st, "xlo", [P, KT, TOK], F32R)
    wif = sb(st, "wif", [P, KT, 2 * MH])
    bif = sb(st, "bif", [MH, 2])
    xn = zaflat[:, 0:3 * D].rearrange("p (t n) -> p t n", t=3)
    sq = zaflat[:, 3 * D:4 * D]
    ss = sb(st, "ss", [P, 3])
    rs = sb(st, "rs", [P, 3])
    rope = zg[:, 0, 0:4 * 2 * 12 * RH].rearrange("p (a n e) -> p a n e", a=4, e=RH)
    psT0, psT1 = pb(st, "psT0", [P, 2, 512]), pb(st, "psT1", [P, 2, 512])
    psT2 = pb(st, "psT2", [P, 512])
    psG = pb(st, "psG", [P, 2, 512])
    s_c = sem(st, "s_consts")
    s_w = [sem(st, f"s_w{i}") for i in range(NR)]
    s_lo, s_free, s_xs = sem(st, "s_wlow"), sem(st, "s_wfree"), sem(st, "s_xsplit")
    s_small = sem(st, "s_small")
    s_ss, s_ms, s_rt, s_xn, s_tr, s_xT = (sem(st, n) for n in (
        "s_sumsq", "s_meansq", "s_root", "s_xn", "s_xtrans", "s_xT"))
    s_gp = sem(st, "s_gate_product")
    s_p0, s_p1, s_p2 = sem(st, "s_prod0"), sem(st, "s_prod1"), sem(st, "s_prod2")
    s_e0, s_e1, s_e2 = sem(st, "s_out0"), sem(st, "s_out1"), sem(st, "s_out2")
    s_aug = sem(st, "s_aug")
    s_rope = sem(st, "s_rope")

    def wcol(z):
        return z if z < GATE0 else z + 2 * MH

    NBLK = len(BLOCKS)
    CHUNKS = []
    for i, (z0, w_) in enumerate(BLOCKS):
        nk = CHUNK // w_
        CHUNKS += [(i, z0, w_, k, nk) for k in range(0, KT, nk)]

    def multiplied(eng, n):
        i, _, _, k0, nk = CHUNKS[n]
        if k0 + nk == KT:
            eng.wait_ge(s_p2, i + 1)
        else:
            eng.wait_ge(s_free, sum(c[3] + c[4] < KT for c in CHUNKS[:n + 1]))

    def split(dve, raw, high, low):
        return (lambda: dve.tensor_copy(high, raw),
                lambda: dve.tensor_tensor(low, raw, high.bitcast(F32), ALU.subtract))

    with nc.Block() as block:

        @block.sync
        def _(sp):
            for t, src in enumerate((x_prompt[0, 0:P], x_prompt[0, P:SEQ], x_sample.rearrange("b t d -> (b t) d"))):
                sp.dma_start(h[0:ROWS[t], t, :], src).then_inc(s_hload, 16)
            sp.dma_start(ca[:, :], ca_in).then_inc(s_c, 16)
            sp.dma_start(cols[:, :], norm_cols).then_inc(s_small, 16)
            sp.dma_start(wif[:, :, :], w_gates).then_inc(s_small, 16)
            sp.dma_start(bif[:, :], b_gates).then_inc(s_small, 16)

            for n, (i, z0, w, k, nk) in enumerate(CHUNKS):
                if n >= NR:
                    multiplied(sp, n - NR)
                sp.dma_start(wraw[:, n % NR, :].rearrange("p (k n) -> p k n", k=nk),
                             w_in[0].rearrange("(k p) n -> p k n", p=P)[:, k:k + nk, wcol(z0):wcol(z0) + w]).then_inc(s_w[n % NR], 16)
                if n % 4 == 3 and n >= 7:
                    shift_piece(sp)

        @block.gpsimd
        def _(pool):
            pool.memset(vaug[:, :, :, MD:MD + 1], 1.0).then_inc(s_aug, 1)
            pool.wait_ge(s_aug, 1)

        @block.tensor
        def _(pe):
            pe.wait_ge(s_c, 16)
            for t in range(3):
                pe.wait_ge(s_xn, t + 1)
                for half in range(2):
                    if t >= 1:
                        pe.wait_ge(s_xT, 2 * (t - 1) + half + 1)
                    for q in range(4):
                        k = 4 * half + q
                        last = pe.transpose(psG[:, half, q * P:q * P + ROWS[t]], xn[0:ROWS[t], t, k * P:(k + 1) * P],
                                            ident[0:ROWS[t], 0:ROWS[t]])
                    last.then_inc(s_tr, 1)
            pe.wait_ge(s_xT, 6)
            pe.wait_ge(s_small, 48)
            for c in range(2):
                for k in range(KT):
                    last = pe.matmul(psG[0:MH, c, 0:TOK], wif[:, k, c * MH:(c + 1) * MH], xT[:, k, :],
                                     start=(k == 0), stop=(k == KT - 1))
                last.then_inc(s_gp, 1)
            pe.wait_ge(s_xs, 2)
            for n, (i, z0, w, k0, nk) in enumerate(CHUNKS):
                pe.wait_ge(s_lo, n + 1)
                wh = whi[:, n % NW, :].rearrange("p (k n) -> p k n", k=nk)
                wl = wlo[:, n % NW, :].rearrange("p (k n) -> p k n", k=nk)
                wr_ = wraw[:, n % NR, :].rearrange("p (k n) -> p k n", k=nk)
                xh, xl = xhi[:, :, :], xlo[:, :, :]
                for t, (ps, sp_, se) in enumerate(((psT0, s_p0, s_e0), (psT1, s_p1, s_e1), (psT2, s_p2, s_e2))):
                    if k0 == 0 and i >= 1:
                        pe.wait_ge(se, i)
                    for c in range(w // 512 if t < 2 else 0):
                        for k in range(nk):
                            for a, b in ((xh, wh), (xh, wl), (xl, wh)):
                                last = pe.matmul(ps[:, c, :], a[:, k0 + k, t * P:(t + 1) * P], b[:, k, c * 512:(c + 1) * 512],
                                                 start=(k0 + k == 0 and a is xh and b is wh), stop=(k0 + k == KT - 1 and a is xl))
                    for k in range(nk if t == 2 else 0):
                        for g in range(4):
                            last = pe.matmul(ps[32 * g:32 * g + 32, 0:w // 4], xT[:, k0 + k, SEQ:TOK],
                                             wr_[:, k, g * w // 4:(g + 1) * w // 4],
                                             start=(k0 + k == 0), stop=(k0 + k == KT - 1))
                    if k0 + nk == KT:
                        last.then_inc(sp_, 1)
                if k0 + nk < KT:
                    last.then_inc(s_free, 1)

        def dest(z0, t):
            if z0 < ZAQ:
                j = z0 // MW
                if t == 2:
                    return zw[:, j, :]
                if j == 2:
                    return vaug[:, t, :, 0:MD]
                return zm[:, t, min(j, 2), :]
            if z0 < ZGA:
                j = (z0 - ZAQ) // GW
                return zaw[:, j, :] if t == 2 else za[:, t, j * GW:(j + 1) * GW]
            j = (z0 - ZGA) // D
            return zgw[:, j, :] if t == 2 else zg[:, t, j * D:(j + 1) * D]

        def source(z0, w, t):
            if t == 2:
                return psT2[:, 0:w // 4]
            s_ = (psT0, psT1)[t][:, 0:w // 512, :].rearrange("p c n -> p (c n)")
            return s_.rearrange("p (h n) -> p h n", h=MH) if z0 == ZV else s_

        @block.scalar
        def _(act):
            for t in range(3):
                act.wait_ge(s_hload, 48)
                R = ROWS[t]
                if t >= 1:
                    act.wait_ge(s_ss, t)
                act.activation(sq[0:R], h[0:R, t, :], ACT.Square, accum_out=ss[0:R, t:t + 1]).then_inc(s_ss, 1)
                act.wait_ge(s_ms, t + 1)
                act.activation(ss[0:R, t:t + 1], ss[0:R, t:t + 1], ACT.Sqrt).then_inc(s_rt, 1)
            def stores():
                nb = 4 + 9
                act.wait_ge(s_rope, 3)
                for out in (s_e0, s_e1, s_e2):
                    act.wait_ge(out, nb)
                for g in range(3):
                    for c in range(2):
                        z0 = (1 + c) * AW + g * GW
                        dst = outs_p[g][c][0, 0].rearrange("r h e -> r (h e)")
                        keep = dst.shape[0]
                        for t in range(2):
                            if t * P >= SEQ - keep:
                                r = t * P - (SEQ - keep)
                                store(act, dst[r:r + P], za[:, t, z0:z0 + GW])
                        for j in range(AH):
                            store(act, outs_s[g][c][0, :, WB[g] - NT:WB[g], j, :],
                                  zaw[NS * j:NS * (j + 1), 3 * (1 + c) + g, :])

            for i, (z0, w) in enumerate(BLOCKS):
                if z0 == ZGA:
                    stores()
                way = ACT.Sigmoid if z0 == ZO or z0 >= ZGA else ACT.Copy
                act.wait_ge(s_p0, i + 1)
                if z0 == ZV:
                    act.wait_ge(s_aug, 1)
                act.activation(dest(z0, 0), source(z0, w, 0), way).then_inc(s_e0, 1)
                act.wait_ge(s_p1, i + 1)
                act.activation(dest(z0, 1), source(z0, w, 1), way).then_inc(s_e1, 1)
                act.wait_ge(s_p2, i + 1)
                act.activation(dest(z0, 2), source(z0, w, 2), way).then_inc(s_e2, 1)

        @block.vector
        def _(dve):
            link = Chain(dve)
            for t in range(3):
                R = ROWS[t]
                dve.wait_ge(s_ss, t + 1)
                dve.tensor_scalar(ss[0:R, t:t + 1], ss[0:R, t:t + 1], 1.0 / D, EPS, ALU.mult, ALU.add).then_inc(s_ms, 1)
                dve.wait_ge(s_rt, t + 1)
                link(dve.reciprocal(rs[0:R, t:t + 1], ss[0:R, t:t + 1]))
                dve.tensor_scalar(xn[0:R, t, :], h[0:R, t, :], rs[0:R, t:t + 1], None, ALU.mult).then_inc(s_xn, 1)
            dve.wait_ge(s_small, 48)
            for t in range(3):
                R = ROWS[t]
                for half in range(2):
                    dve.wait_ge(s_tr, 2 * t + half + 1)
                    dve.tensor_tensor(xT[:, 4 * half:4 * half + 4, t * P:t * P + R],
                                      psG[:, half, :].rearrange("p (q n) -> p q n", q=4)[:, :, 0:R],
                                      n1c[:, 4 * half:4 * half + 4].unsqueeze(2).to_broadcast([P, 4, R]),
                                      ALU.mult).then_inc(s_xT, 1)
            high_x, low_x = split(dve, xT[:, :, :], xhi[:, :, :], xlo[:, :, :])
            dve.wait_ge(s_xT, 6)
            high_x().then_inc(s_xs, 1)
            dve.wait_ge(s_xs, 1)
            low_x().then_inc(s_xs, 1)

            def prepare(n):
                high_w, low_w = split(dve, wraw[:, n % NR, :], whi[:, n % NW, :], wlo[:, n % NW, :])
                dve.wait_ge(s_w[n % NR], 16 * (n // NR + 1))
                if n >= NW:
                    multiplied(dve, n - NW)
                link(high_w())
                low_w().then_inc(s_lo, 1)

            def rotate(t):
                v, n, tab = ((za[:, 0, 0:2 * AW], 24, "p0"), (za[:, 1, 0:2 * AW], 24, "p1"),
                             (zaw[:, 0:6, :].rearrange("p a b -> p (a b)"), 6, "s"))[t]
                dve.wait_ge((s_e0, s_e1, s_e2)[t], 4 + 6)
                v = v.rearrange("p (n e) -> p n e", e=AD)
                x1, x2 = v[:, :, 0:RH], v[:, :, RH:2 * RH]
                cos = CAc("cos" + tab).unsqueeze(1).to_broadcast([P, n, RH])
                sin = CAc("sin" + tab).unsqueeze(1).to_broadcast([P, n, RH])
                link.many(dve.tensor_tensor(rope[:, 0, 0:n, :], x1, cos, ALU.mult),
                          dve.tensor_tensor(rope[:, 1, 0:n, :], x2, sin, ALU.mult),
                          dve.tensor_tensor(rope[:, 2, 0:n, :], x2, cos, ALU.mult),
                          dve.tensor_tensor(rope[:, 3, 0:n, :], x1, sin, ALU.mult))
                link(dve.tensor_tensor(x1, rope[:, 0, 0:n, :], rope[:, 1, 0:n, :], ALU.subtract))
                dve.tensor_tensor(x2, rope[:, 2, 0:n, :], rope[:, 3, 0:n, :], ALU.add).then_inc(s_rope, 1)
                dve.wait_ge(s_rope, t + 1)

            AHEAD = NW - 1
            for n in range(AHEAD):
                prepare(n)
            for c in range(2):
                dve.wait_ge(s_gp, c + 1)
                dve.tensor_scalar(grow[:, c, :], psG[0:MH, c, 0:TOK], bif[:, c:c + 1], None, ALU.add)
            dve.wait_ge(s_c, 16)
            for n, (i, z0, w, k0, nk) in enumerate(CHUNKS):
                if n + AHEAD < len(CHUNKS):
                    prepare(n + AHEAD)
                if i in (10, 11, 12) and k0 + nk == KT:
                    rotate(i - 10)
    st.close()
    ap = ExitStack()
    cb = sb(mid, "cb", [P, CB.shape[1]])

    def CBc(name):
        o, n = CB_AT[name]
        return cb[:, o:o + n]

    s_cb = sem(mid, "s_cb")
    def rowbuf(name, n=TOK):
        return sb(mid, name, [MH, n])
    lf, bsum, cg, mx, tmp, emj, ws, aint = (rowbuf(n) for n in ("lf", "bsum", "cg", "mx", "tmp", "emj", "ws", "aint"))
    m0 = rowbuf("m0", NB)
    mnew = rowbuf("mnew", 1 + NB)
    xrow = sb(mid, "xrow", [MH, 6, P])
    kvs = ExitStack()
    kv0 = sb(kvs, "kv0", [P, AH * NKEY])
    s_kv = [sem(kvs, f"s_kv{i}") for i in range(4)]
    qkT = sb(ap, "qkT", [P, 12, 4 * P])
    sS = sb(ap, "sS", [P, 2, 3 * SEQ])
    pS = sb(ap, "pS", [P, 2, 3 * SEQ])
    pT = xT[:, :, :].rearrange("p k n -> p (k n)")[:, 0:6 * SEQ].rearrange("p (a n) -> p a n", a=2)
    nmx, lsum, rl = sb(ap, "nmx", [P, 8]), sb(ap, "lsum", [P, 8]), sb(ap, "rl", [P, 8])
    psTR = pb(ap, "psTR", [P, 2, 512])
    psS = pb(ap, "psS", [P, 2, 1024])
    psO = pb(ap, "psO", [P, 2, 512])
    s_qt, s_qe = sem(ap, "s_qk_trans"), sem(ap, "s_qk_out")
    s_sc, s_sm, s_nm, s_ex, s_pn = (sem(ap, n) for n in (
        "s_scores", "s_masked", "s_negmax", "s_exp", "s_pnorm"))
    s_pt, s_pe, s_ov, s_oe = (sem(ap, n) for n in ("s_p_trans", "s_p_out", "s_pv", "s_pv_out"))
    UNITS = [(hs, jt) for hs in range(AH) for jt in range(2)]
    SCALE = AD ** -0.5

    with nc.Block() as block:
        @block.sync
        def _(sp):
            sp.dma_start(cb[:, :], cb_in).then_inc(s_cb, 16)
            sp.dma_start(kv0[:, :], KT_cache[0].rearrange("d h k -> d (h k)")).then_inc(s_kv[0], 16)
            for _ in range(2):
                shift_piece(sp)

        @block.tensor
        def _(pe):
            for hd in range(12):
                if hd >= 2:
                    pe.wait_ge(s_qe, hd - 1)
                for c in range(2):
                    for t in range(2):
                        last = pe.transpose(psTR[:, hd % 2, (2 * c + t) * P:(2 * c + t + 1) * P],
                                            za[:, t, c * AW + hd * AD:c * AW + (hd + 1) * AD], ident)
                last.then_inc(s_qt, 1)
            pe.wait_ge(s_qe, 12)

            def scores(i):
                hs, jt = UNITS[i]
                if i >= 2:
                    pe.wait_ge(s_sm, i - 1)
                for g in range(3):
                    last = pe.matmul(psS[:, i % 2, g * SEQ:(g + 1) * SEQ], qkT[:, 4 * g + hs, jt * P:(jt + 1) * P],
                                     qkT[:, 4 * g + hs, 2 * P:4 * P], start=True, stop=True)
                last.then_inc(s_sc, 1)

            def values(i):
                hs, jt = UNITS[i]
                pe.wait_ge(s_pn, i + 1)
                if i >= 1:
                    pe.wait_ge(s_pe, i)
                for g in range(3):
                    for s in range(jt + 1):
                        a = g * SEQ + s * P
                        last = pe.transpose(psTR[:, :, :].rearrange("p a b -> p (a b)")[:, a:a + P], pS[:, i % 2, a:a + P], ident)
                last.then_inc(s_pt, 1)
                if i + 2 < len(UNITS):
                    scores(i + 2)
                pe.wait_ge(s_pe, i + 1)
                if i >= 2:
                    pe.wait_ge(s_oe, i - 1)
                for g in range(3):
                    for s in range(jt + 1):
                        a = g * SEQ + s * P
                        last = pe.matmul(psO[:, i % 2, 0:P], za[:, s, 2 * AW + (4 * g + hs) * AD:2 * AW + (4 * g + hs + 1) * AD],
                                         pT[:, i % 2, a:a + P], start=(g == 0 and s == 0), stop=(g == 2 and s == jt))
                last.then_inc(s_ov, 1)

            scores(0)
            scores(1)
            for i in range(len(UNITS)):
                values(i)

        def part(x, jt):
            return x.rearrange("p (g s) -> p g s", g=3)[:, :, 0:(jt + 1) * P]

        def evac(act, i):
            jt = UNITS[i][1]
            act.wait_ge(s_pt, i + 1)
            if i >= 2:
                act.wait_ge(s_ov, i - 1)
            act.activation(part(pT[:, i % 2, :], jt), part(psTR[:, :, :].rearrange("p a b -> p (a b)")[:, 0:3 * SEQ], jt),
                           ACT.Copy).then_inc(s_pe, 1)

        @block.scalar
        def _(act):
            for hd in range(0, 12, 2):
                act.wait_ge(s_qt, hd + 1)
                if hd >= 2:
                    act.wait_ge(s_qe, hd)
                act.activation(qkT[:, hd, :], psTR[:, hd % 2, :], ACT.Copy).then_inc(s_qe, 1)
            def exps(i):
                act.wait_ge(s_nm, i + 1)
                if i >= 2:
                    act.wait_ge(s_pt, i - 1)
                act.activation(pS[:, i % 2, :], sS[:, i % 2, :], ACT.Exp, bias=nmx[:, i:i + 1],
                               accum_out=lsum[:, i:i + 1]).then_inc(s_ex, 1)

            exps(0)
            exps(1)
            for i in range(len(UNITS)):
                evac(act, i)
                if i + 2 < len(UNITS):
                    exps(i + 2)

        @block.vector
        def _(dve):
            for hd in range(1, 12, 2):
                dve.wait_ge(s_qt, hd + 1)
                dve.wait_ge(s_qe, hd)
                dve.tensor_copy(qkT[:, hd, :], psTR[:, hd % 2, :]).then_inc(s_qe, 1)
            dve.wait_ge(s_cb, 16)

            def out(i):
                hs, jt = UNITS[i]
                dve.wait_ge(s_ov, i + 1)
                dve.tensor_copy(hBT[:, hs, jt * P:(jt + 1) * P], psO[:, i % 2, 0:P]).then_inc(s_oe, 1)

            link = Chain(dve)

            def masked(i):
                jt = UNITS[i][1]
                dve.wait_ge(s_sc, i + 1)
                if i >= 2:
                    dve.wait_ge(s_ex, i - 1)
                dve.scalar_tensor_tensor(out=sS[:, i % 2, :], in0=psS[:, i % 2, 0:3 * SEQ], scalar=SCALE,
                                         in1=CBc("amask")[:, jt * 3 * SEQ:(jt + 1) * 3 * SEQ],
                                         op0=ALU.mult, op1=ALU.add).then_inc(s_sm, 1)
                dve.wait_ge(s_sm, i + 1)
                dve.tensor_reduce(nmx[:, i:i + 1], sS[:, i % 2, :], AX.X, ALU.max, negate=True).then_inc(s_nm, 1)

            masked(0)
            masked(1)
            for i in range(len(UNITS)):
                dve.wait_ge(s_ex, i + 1)
                link(dve.reciprocal(rl[:, i:i + 1], lsum[:, i:i + 1]))
                dve.tensor_scalar(pS[:, i % 2, :], pS[:, i % 2, :], rl[:, i:i + 1], None, ALU.mult).then_inc(s_pn, 1)
                if i >= 1:
                    out(i - 1)
                if i + 2 < len(UNITS):
                    masked(i + 2)
            out(len(UNITS) - 1)
    ap.close()

    s_ld = sem(mid, "s_mload")
    s_rowd, s_bc, s_xr = (sem(mid, n) for n in ("s_rowargs", "s_rowact", "s_xrow"))
    ap = ExitStack()
    kv1 = sb(ap, "kv1", [P, AH * NKEY])
    KV = (kv0[:, :], kv1[:, :], zaflat[:, 0:AH * NKEY], zaflat[:, AH * NKEY:2 * AH * NKEY])
    sqk = sb(ap, "sqk", [P, 6, P])
    qmask = sb(ap, "qmask", [P, 3, NB, P])
    ssS = sb(ap, "ssS", [P, SKEY])
    spT = qmask[:, 1:3, :, :].rearrange("p g b n -> p (g b) n")[:, 0:10, :]
    own = qmask[:, 0, :, :]
    hBs = sb(ap, "hBs", [P, AD])
    sst = sb(ap, "sst", [P, 3])
    psA = pb(ap, "psA", [P, 4, 512])
    psV = pb(ap, "psV", [P, NB, AD])
    psR = pb(ap, "psR", [P, 512])
    psN = pb(ap, "psN", [P, 512])
    s_used = sem(ap, "s_kv_used")
    s_t, s_te, s_qm, s_new = (sem(ap, n) for n in ("s_trans", "s_trans_out", "s_qmask", "s_newscores"))
    s_pr = sem(ap, "s_probs")
    s_pt, s_pe, s_nv, s_hb = (sem(ap, n) for n in ("s_sp_trans", "s_sp_out", "s_new_values", "s_hBs"))
    s_ex = sem(ap, "s_sexp")
    s_nm = sem(ap, "s_snegmax")
    SEGS = ((0, 0, 1, 0), (1, 1, 4, 1), (2, 5, 2, 2))

    with nc.Block() as block:
        @block.sync
        def _(sp):
            sp.dma_start(m0[:, :], m_rows).then_inc(s_ld, 16)
            sp.wait_ge(s_stored, n_stored[0])
            for i in range(1, 2 * NB):
                if i >= 4:
                    sp.wait_ge(s_used, i - 3)
                src = KT_cache[i].rearrange("d h k -> d (h k)") if i < NB else VK[i - NB].rearrange("k t n -> k (t n)")
                sp.dma_start(KV[i % 4], src).then_inc(s_kv[i % 4], 16)

        @block.tensor
        def _(pe):
            for n in range(6):
                if n == 3:
                    pe.wait_ge(s_te, 1)
                last = pe.transpose(psR[:, (n % 3) * P:(n % 3 + 1) * P], zaw[:, n, :], ident)
                if n % 3 == 2:
                    last.then_inc(s_t, 1)
            pe.wait_ge(s_te, 2)
            for g in range(3):
                last = pe.matmul(psA[:, 3, g * P:(g + 1) * P], sqk[:, g, :], sqk[:, 3 + g, :], start=True, stop=True)
            last.then_inc(s_new, 1)
            pe.wait_ge(s_qm, 3)
            for b in range(NB):
                pe.wait_ge(s_kv[b % 4], 16 * (b // 4 + 1))
                keys = KV[b % 4].rearrange("p (h k) -> p h k", h=AH)
                for bank, t0, nt, g in SEGS:
                    for j in range(AH):
                        last = pe.matmul(psA[32 * j:32 * j + 32, bank, 0:nt * P], qmask[:, g, b, 32 * j:32 * j + 32],
                                         keys[:, j, t0 * P:(t0 + nt) * P], start=(b == 0), stop=(b == NB - 1))
                last.then_inc(s_used, 1)
            pe.wait_ge(s_pr, 1)
            for n in range(10):
                if n % 4 == 0 and n:
                    pe.wait_ge(s_pe, n // 4)
                last = pe.transpose(psR[:, (n % 4) * P:(n % 4 + 1) * P], ssS[:, n * P:(n + 1) * P], ident)
                if n % 4 == 3 or n == 9:
                    last.then_inc(s_pt, 1)
            pe.wait_ge(s_pe, 3)
            for b in range(NB):
                i = NB + b
                pe.wait_ge(s_kv[i % 4], 16 * (i // 4 + 1))
                values_ = KV[i % 4].rearrange("p (t n) -> p t n", t=7)
                for n in range(7):
                    for j in range(AH):
                        last = pe.matmul(psV[32 * j:32 * j + 32, b, :], spT[:, n, 32 * j:32 * j + 32],
                                         values_[:, n, j * AD:(j + 1) * AD], start=(n == 0), stop=(n == 6))
                last.then_inc(s_used, 1)
            for g in range(3):
                last = pe.matmul(psN[:, 0:AD], spT[:, 7 + g, :], zaw[:, 6 + g, :], start=(g == 0), stop=(g == 2))
            last.then_inc(s_nv, 1)
            pe.wait_ge(s_hb, 1)
            pe.transpose(psR[:, 0:P], hBs[:, :], ident).then_inc(s_t, 1)

        @block.scalar
        def _(act):
            act.wait_ge(s_steps, steps[0] + 2)
            act.activation(tmp[:, :], tmp[:, :], ACT.Exp).then_inc(s_bc, 1)
            act.wait_ge(s_bc, 1)
            act.activation(tmp[:, :], tmp[:, :], ACT.Ln, bias=1.0).then_inc(s_bc, 1)
            act.wait_ge(s_rowd, 1)
            act.activation(emj[:, :], emj[:, :], ACT.Exp).then_inc(s_bc, 1)
            act.activation(ws[:, :], ws[:, :], ACT.Exp).then_inc(s_bc, 1)
            act.activation(aint[:, 0:NS], aint[:, 0:NS], ACT.Exp).then_inc(s_bc, 1)
            act.wait_ge(s_nm, 1)
            act.activation(ssS[:, :], ssS[:, :], ACT.Exp, bias=sst[:, 0:1], accum_out=sst[:, 1:2]).then_inc(s_ex, 1)
            for n in range(3):
                act.wait_ge(s_pt, n + 1)
                c = min(4, 10 - 4 * n)
                act.activation(spT[:, 4 * n:4 * n + c, :].rearrange("p a b -> p (a b)"), psR[:, 0:c * P], ACT.Copy).then_inc(s_pe, 1)

        @block.vector
        def _(dve):
            link = Chain(dve)
            for n in range(2):
                dve.wait_ge(s_t, n + 1)
                dve.tensor_copy(sqk[:, 3 * n:3 * n + 3, :].rearrange("p a b -> p (a b)"), psR[:, 0:3 * P]).then_inc(s_te, 1)
            dve.wait_ge(s_te, 2)
            for g in range(3):
                dve.tensor_tensor(qmask[:, g, :, :], sqk[:, g, :].unsqueeze(1).to_broadcast([P, NB, P]),
                                  CBc("bcol").rearrange("p (b f) -> p b f", b=NB), ALU.mult).then_inc(s_qm, 1)
            f = grow[:, 1, :]
            link(dve.tensor_scalar(tmp[:, :], f, -1.0, None, ALU.mult))
            link(dve.tensor_tensor(tmp[:, :], f, tmp[:, :], ALU.min))
            link(dve.tensor_scalar(lf[:, :], f, 0.0, None, ALU.min))
            dve.wait_ge(s_bc, 2)
            link(dve.tensor_tensor(lf[:, :], lf[:, :], tmp[:, :], ALU.subtract))

            def scan(src, dst, op):
                bufs = [src, dst]
                d, i = 1, 0
                while d < SEQ:
                    a, b = bufs[i % 2], bufs[(i + 1) % 2]
                    todo = [dve.tensor_tensor(b[:, d:SEQ], a[:, d:SEQ], a[:, 0:SEQ - d], op),
                            dve.tensor_copy(b[:, 0:d], a[:, 0:d])]
                    av, bv = (x[:, SEQ:TOK].rearrange("p (b t) -> p b t", t=NT) for x in (a, b))
                    if d < NT:
                        todo += [dve.tensor_tensor(bv[:, :, d:NT], av[:, :, d:NT], av[:, :, 0:NT - d], op),
                                 dve.tensor_copy(bv[:, :, 0:d], av[:, :, 0:d])]
                    link.many(*todo)
                    d, i = 2 * d, i + 1
                return src

            scan(lf, tmp, ALU.add)
            link(dve.tensor_copy(bsum[:, :], lf[:, :]))
            link(dve.tensor_tensor(cg[:, :], grow[:, 0, :], bsum[:, :], ALU.subtract))
            link(dve.tensor_copy(mx[:, :], cg[:, :]))
            scan(mx, tmp, ALU.max)
            dve.wait_ge(s_ld, 16)
            samp = lambda x: x[:, SEQ:TOK].rearrange("p (b t) -> p b t", t=NT)
            m0b = m0[:, :].unsqueeze(2).to_broadcast([MH, NB, NT])
            link.many(dve.tensor_scalar(mx[:, 0:SEQ], mx[:, 0:SEQ], 0.0, None, ALU.max),
                      dve.tensor_tensor(samp(mx), samp(mx), m0b, ALU.max))
            link(dve.tensor_tensor(tmp[:, :], bsum[:, :], mx[:, :], ALU.add))
            link.many(dve.tensor_copy(mnew[:, 0:1], tmp[:, SEQ - 1:SEQ]),
                      dve.tensor_copy(mnew[:, 1:1 + NB], samp(tmp)[:, :, NT - 1]),
                      dve.tensor_scalar(emj[:, :], tmp[:, :], -1.0, None, ALU.mult),
                      dve.tensor_scalar(ws[:, 0:SEQ], cg[:, 0:SEQ], mx[:, SEQ - 1:SEQ], None, ALU.subtract),
                      dve.tensor_tensor(samp(ws), samp(cg), samp(mx)[:, :, NT - 1:NT].to_broadcast([MH, NB, NT]), ALU.subtract))
            dve.tensor_tensor(aint[:, 0:NS].rearrange("p (b t) -> p b t", t=NT), m0b, samp(mx), ALU.subtract).then_inc(s_rowd, 1)
            dve.wait_ge(s_bc, 5)
            own4 = CBc("hsel")[0:MH].rearrange("p (h n) -> p h n", h=MH)
            for q, r in enumerate((samp(mx), samp(cg), samp(emj), samp(ws), aint[:, 0:NS])):
                r = r if q == 4 else (mx, cg, emj, ws)[q][:, SEQ:TOK]
                dve.tensor_tensor(xrow[:, q, :].rearrange("p (h n) -> p h n", h=MH), r.unsqueeze(1).to_broadcast([MH, MH, NS]),
                                  own4[:, :, 0:NS], ALU.mult).then_inc(s_xr, 1)
            decay = aint[:, 0:NS].rearrange("p (b t) -> p b t", t=NT)[:, :, NT - 1]
            dve.tensor_tensor(xrow[:, 5, 0:NS].rearrange("p (h b) -> p h b", h=MH), decay.unsqueeze(1).to_broadcast([MH, MH, NB]),
                              own4[:, :, 0:NB], ALU.mult).then_inc(s_xr, 1)
            dve.wait_ge(s_new, 1)
            dve.wait_ge(s_used, NB)
            sm = CBc("smask")
            parts = [dve.scalar_tensor_tensor(out=ssS[:, a:a + n], in0=psA[:, bank, 0:n], scalar=SCALE, in1=sm[:, a:a + n],
                                              op0=ALU.mult, op1=ALU.add)
                     for bank, a, n in ((0, 0, P), (1, P, 4 * P), (2, 5 * P, 2 * P), (3, NKEY, 3 * P))]
            link.many(*parts)
            dve.tensor_reduce(sst[:, 0:1], ssS[:, :], AX.X, ALU.max, negate=True).then_inc(s_nm, 1)
            dve.wait_ge(s_ex, 1)
            link(dve.reciprocal(sst[:, 2:3], sst[:, 1:2]))
            dve.tensor_scalar(ssS[:, :], ssS[:, :], sst[:, 2:3], None, ALU.mult).then_inc(s_pr, 1)
            dve.wait_ge(s_used, 2 * NB)
            link(dve.tensor_tensor(own, psV[:, :, :], CBc("brow").unsqueeze(2).to_broadcast([P, NB, AD]), ALU.mult))
            link(dve.tensor_reduce(hBs[:, :], own.rearrange("p b e -> p e b"), AX.X, ALU.add))
            dve.wait_ge(s_nv, 1)
            dve.tensor_tensor(hBs[:, :], psN[:, 0:AD], hBs[:, :], ALU.add).then_inc(s_hb, 1)
            dve.wait_ge(s_t, 3)
            link(dve.tensor_copy(hBT[:, :, SEQ:TOK], psR[:, 0:P].rearrange("p (h n) -> p h n", h=AH)))
    ap.close()
    kvs.close()
    ap = ExitStack()
    qkT_ = sb(ap, "mqkT", [P, 4, SEQ])
    qT_, kT_ = qkT_[:, 0:2, :], qkT_[:, 2:4, :]
    arg, ex, wt = sb(ap, "arg", [P, 3 * P]), sb(ap, "ex", [P, 3 * P]), sb(ap, "wt", [P, 3 * P])
    wk = sb(ap, "wk", [P, 2, MD])
    colsb = sb(ap, "colsb", [P, 64])
    sm1 = sb(ap, "sm1", [P, 4])
    ssq = sb(ap, "ssq", [P, 10])
    rsq = sb(ap, "rsq", [P, 10])
    cst = sb(ap, "cst", [P, 2, 2 * MD])
    nst = sb(ap, "nst", [1, 2, MD])
    ct2 = sb(ap, "ct", [P, 2, MH, 2 * MD])
    ct = (ct2[:, 0], ct2[:, 1], xT[:, :, :].rearrange("p k n -> p (k n)")[:, 0:MH * 2 * MD].rearrange("p (h n) -> p h n", h=MH))
    sv = sb(ap, "sv", [P, MD + 1])
    sT = sb(ap, "sT", [P, 4, P])
    qmm = sb(ap, "qmm", [P, 2, NB, P])
    wv = qkT_
    km = sb(ap, "km", [P, 2, MD])
    nrow = sb(ap, "nrow", [NS, MD])
    ntok = sb(ap, "ntok", [P, MD])
    scr = sb(ap, "scr", [P, MD])
    psTR = pb(ap, "mTR", [P, 2, 512])
    psSC = pb(ap, "mSC", [P, 2, 512])
    psS_, psC = psSC[:, 0, :], psSC[:, 1, :]
    psM = pb(ap, "mM", [P, 512])
    psN_ = pb(ap, "mN", [P, 2, 512])
    psX = pb(ap, "mX", [P, 512])
    KS = MD ** -0.5
    s_ac = sem(ap, "s_mact")
    s_colp, s_col = (sem(ap, n) for n in ("s_colsp", "s_cols"))
    s_mt, s_mte, s_mts, s_mtse = (sem(ap, n) for n in ("s_mtrans", "s_mtq_out", "s_mtrans2", "s_mtk_out"))
    s_ms_, s_mm = sem(ap, "s_mscores"), sem(ap, "s_mmax")
    s_arg, s_e, s_w_, s_wk, s_num, s_hh, s_cp, s_co, s_sq = (sem(ap, n) for n in (
        "s_arg", "s_mexp", "s_mw", "s_wk", "s_num", "s_hh", "s_cprod", "s_cout", "s_msq"))
    s_sqd = sem(ap, "s_meansqs")
    s_ha, s_hat, s_hae = sem(ap, "s_ha"), sem(ap, "s_hatrans"), sem(ap, "s_haout")
    s_cst = [sem(ap, "s_cstored0"), sem(ap, "s_cstored1")]
    s_ct = [sem(ap, f"s_ct{i}") for i in range(3)]
    s_cts = [sem(ap, f"s_cts{i}") for i in range(3)]
    s_cq, s_km, s_up, s_upd = (sem(ap, n) for n in ("s_cq", "s_km", "s_update", "s_updated"))
    s_sv, s_nn, s_nno, s_qmm = (sem(ap, n) for n in ("s_sv", "s_nnew", "s_nnew_out", "s_qmm"))

    PC_ = lambda q, t, hd: colsb[:, 8 * q + 4 * t + hd:8 * q + 4 * t + hd + 1]
    SC_ = lambda q: colsb[:, 24 + q:25 + q]
    AC = colsb[:, 28:60]
    ACC = colsb[0:NS, 60:61]

    with nc.Block() as block:
        @block.sync
        def _(sp):
            sp.dma_start(nrow[:, :], n_rows).then_inc(s_ld, 16)
            sp.dma_start(ntok[:, :], n_tok).then_inc(s_ld, 16)
            for b in range(3):
                sp.dma_start(ct[b], CT[:, :, b].rearrange("p h k v -> p h (k v)")).then_inc(s_ct[b], 16)
            sp.wait_ge(s_stored, n_stored[0])
            sp.dma_start(wa, w_pa[0].rearrange("(k p) n -> p k n", p=P)).then_inc(s_wa, 16)
            for hd in range(MH):
                sp.wait_ge(s_co, 2 * hd + 2)
                sp.dma_start(C_p[hd].rearrange("(a p) e -> p a e", p=P), cst[:, hd % 2].rearrange("p (a e) -> p a e", a=2)).then_inc(s_cst[hd % 2], 16)
                sp.dma_start(n_p[hd:hd + 1], nst[:, hd % 2]).then_inc(s_cst[hd % 2], 16)
            for b in range(NB):
                sp.wait_ge(s_upd, MH * (b + 1))
                sp.dma_start(C_s[:, :, b].rearrange("p h k v -> p h (k v)"), ct[b % 3]).then_inc(s_cts[b % 3], 16)
            sp.wait_ge(s_nno, 1)
            store(sp, n_s, nrow[:, :])
            store(sp, m_p, mnew[:, 0:1])
            store(sp, m_s, mnew[:, 1:1 + NB])
            for i in range(3):
                sp.wait_ge(s_cts[i], 16 * len(range(i, NB, 3)))
            for i in range(2):
                sp.wait_ge(s_cst[i], 32 * MH // 2)
            sp.wait_ge(s_stored, n_stored[0])

        @block.tensor
        def _(pe):
            def trans(hd):
                if hd >= 1:
                    pe.wait_ge(s_mte, hd)
                for c in range(2):
                    if c == 1 and hd >= 1:
                        pe.wait_ge(s_mtse, hd)
                    for half in range(2):
                        for t in range(2):
                            a = hd * MD + half * P
                            last = pe.transpose(psTR[:, c, (2 * half + t) * P:(2 * half + t + 1) * P], zm[:, t, c, a:a + P], ident)
                    last.then_inc((s_mt, s_mts)[c], 1)

            trans(0)
            pe.wait_ge(s_xr, 6)
            for q, r in enumerate((cg, emj, ws)):
                for t in range(2):
                    pe.transpose(psX[:, 8 * q + 4 * t:8 * q + 4 * t + 4], r[:, t * P:(t + 1) * P], ident[0:MH, 0:MH])
            for q in range(4):
                pe.matmul(psX[:, 24 + q:25 + q], xrow[:, 1 + q, :], ones[0:MH, 0:1], start=True, stop=True)
            pe.matmul(psX[:, 28:60], ones[0:MH, :], xrow[:, 5, 0:NS], start=True, stop=True)
            pe.matmul(psX[0:NS, 60:61], xrow[:, 5, 0:NS], ones[0:MH, 0:1], start=True, stop=True).then_inc(s_colp, 1)
            for hd in range(MH):
                if hd >= 1:
                    pe.wait_ge(s_w_, hd)
                    pe.wait_ge(s_arg, 3 * hd)
                pe.wait_ge(s_mte, hd + 1)
                pe.wait_ge(s_mtse, hd + 1)
                for half in range(2):
                    pe.matmul(psS_[:, 0:SEQ], kT_[:, half, 0:P], qT_[:, half, :], start=(half == 0), stop=(half == 1))
                for half in range(2):
                    last = pe.matmul(psS_[:, SEQ:3 * P], kT_[:, half, P:SEQ], qT_[:, half, P:SEQ], start=(half == 0), stop=(half == 1))
                last.then_inc(s_ms_, 1)
                pe.matmul(psM[:, 0:SEQ], CBc("hsel")[0:MH, hd * P:(hd + 1) * P], mx[:, 0:SEQ], start=True, stop=True).then_inc(s_mm, 1)
                if hd + 1 < MH:
                    trans(hd + 1)
                pe.wait_ge(s_wk, 2 * hd + 2)
                if hd >= 1:
                    pe.wait_ge(s_co, 2 * hd)
                for dh in range(2):
                    for t in range(2):
                        pe.matmul(psC[:, dh * MD:(dh + 1) * MD], vaug[:, t, hd, dh * P:(dh + 1) * P], wk[:, t, :],
                                  start=(t == 0), stop=(t == 1))
                for t in range(2):
                    last = pe.matmul(psX[0:1, 0:MD], vaug[:, t, hd, MD:MD + 1], wk[:, t, :], start=(t == 0), stop=(t == 1))
                last.then_inc(s_cp, 1)
                pe.wait_ge(s_w_, hd + 1)
                if hd >= 1:
                    pe.wait_ge(s_hh, 2 * hd)
                pe.matmul(psN_[:, 0, 0:MD + 1], wt[:, 0:P], vaug[:, 0, hd, :], start=True, stop=True)
                pe.matmul(psN_[:, 1, 0:MD + 1], wt[:, P:2 * P], vaug[:, 0, hd, :], start=True, stop=False)
                pe.matmul(psN_[:, 1, 0:MD + 1], wt[:, 2 * P:3 * P], vaug[:, 1, hd, :], start=False, stop=True).then_inc(s_num, 1)
            pe.wait_ge(s_mte, MH)
            for n in range(4):
                last = pe.transpose(psTR[:, 0, n * P:(n + 1) * P], zw[:, n // 2, (n % 2) * P:(n % 2 + 1) * P], ident)
            last.then_inc(s_mt, 1)
            pe.wait_ge(s_mte, MH + 1)
            pe.wait_ge(s_w_, MH)
            for half in range(2):
                last = pe.matmul(psS_[:, 0:P], sT[:, 2 + half, :], sT[:, half, :], start=(half == 0), stop=(half == 1))
            last.then_inc(s_ms_, 1)
            pe.wait_ge(s_arg, 3 * MH)
            pe.matmul(psM[:, 0:P], ones[0:MH, :], xrow[:, 0, :], start=True, stop=True).then_inc(s_mm, 1)
            pe.wait_ge(s_w_, MH + 1)
            pe.wait_ge(s_hh, 2 * MH)
            pe.matmul(psN_[:, 0, 0:MD + 1], wt[:, 0:P], sv[:, :], start=True, stop=True).then_inc(s_num, 1)
            pe.wait_ge(s_wk, 2 * MH + 1)
            pe.wait_ge(s_co, 2 * MH)
            pe.matmul(psX[0:NS, 0:MD], CBc("bhsel"), wk[:, 0, :], start=True, stop=True).then_inc(s_nn, 1)
            pe.wait_ge(s_qmm, 2 + MH)
            for b in range(NB):
                pe.wait_ge(s_ct[b % 3], 16 * (b // 3 + 1))
                for half in range(2):
                    for j in range(MH):
                        last = pe.matmul(psN_[32 * j:32 * j + 32, 1, 0:MD], qmm[:, half, b, 32 * j:32 * j + 32],
                                         ct[b % 3][:, j, half * MD:(half + 1) * MD],
                                         start=(b == 0 and half == 0), stop=(b == NB - 1 and half == 1))
                last.then_inc(s_cq, 1)
                pe.wait_ge(s_km, b + 1)
                for q, ps in enumerate((psTR, psSC)):
                    if b:
                        pe.wait_ge(s_upd, MH * (b - 1) + 2 * q + 2)
                    elif q == 0:
                        pe.wait_ge(s_mte, MH + 1)
                        pe.wait_ge(s_mtse, MH)
                    else:
                        pe.wait_ge(s_w_, MH + 1)
                        pe.wait_ge(s_co, 2 * MH)
                    for half in range(2):
                        last = pe.matmul(ps[:, half, :], km[:, b % 2, half * P:(half + 1) * P],
                                         wv[:, 2 * q:2 * q + 2, :].rearrange("p a n -> p (a n)"), start=True, stop=True)
                    last.then_inc(s_up, 1)
            pe.wait_ge(s_ha, 8)
            pe.wait_ge(s_upd, MH * NB)
            for n in range(4):
                if n >= 2:
                    pe.wait_ge(s_hae, n - 1)
                t, half = n // 2, n % 2
                for q in range(4):
                    k = 4 * half + q
                    last = pe.transpose(psTR[:, n % 2, q * P:(q + 1) * P], zm[:, t, 2, k * P:(k + 1) * P], ident)
                last.then_inc(s_hat, 1)
            pe.wait_ge(s_ha, 9)
            for half in range(2):
                pe.wait_ge(s_hae, 3 + half)
                pe.transpose(psTR[:, half, 0:P], zw[:, 3, half * P:(half + 1) * P], ident).then_inc(s_hat, 1)

        @block.scalar
        def _(act):
            def squares(hd):
                for t in range(2):
                    n = 2 * hd + t
                    act.wait_ge(s_hh, n + 1)
                    if n:
                        act.wait_ge(s_sq, n)
                    act.activation(scr[:, :], zm[:, t, 2, hd * MD:(hd + 1) * MD], ACT.Square, accum_out=ssq[:, n:n + 1]).then_inc(s_sq, 1)

            for hd in range(MH):
                act.wait_ge(s_mt, hd + 1)
                if hd >= 1:
                    act.wait_ge(s_ms_, hd)
                act.activation(qT_[:, :, :].rearrange("p a b -> p (a b)"), psTR[:, 0, :], ACT.Copy).then_inc(s_mte, 1)
                act.wait_ge(s_col, 1)
                act.wait_ge(s_arg, 3 * hd + 3)
                if hd >= 1:
                    act.wait_ge(s_w_, hd)
                act.activation(ex[:, 0:SEQ], arg[:, 0:SEQ], ACT.Exp, bias=PC_(0, 0, hd)).then_inc(s_e, 1)
                act.activation(ex[:, SEQ:3 * P], arg[:, SEQ:3 * P], ACT.Exp, bias=PC_(0, 1, hd)).then_inc(s_e, 1)
                act.wait_ge(s_cp, hd + 1)
                if hd >= 2:
                    act.wait_ge(s_cst[hd % 2], 32 * (hd // 2))
                act.activation(cst[:, hd % 2], psC, ACT.Copy).then_inc(s_co, 1)
                act.activation(nst[:, hd % 2], psX[0:1, 0:MD], ACT.Copy).then_inc(s_co, 1)
                if hd:
                    squares(hd - 1)
            squares(MH - 1)
            act.wait_ge(s_mt, MH + 1)
            act.activation(sT[:, :, :].rearrange("p a b -> p (a b)"), psTR[:, 0, :], ACT.Copy).then_inc(s_mte, 1)
            act.wait_ge(s_arg, 3 * MH + 1)
            act.activation(ex[:, 0:P], arg[:, 0:P], ACT.Exp, bias=SC_(0)).then_inc(s_e, 1)
            act.wait_ge(s_sqd, 1)
            act.activation(ssq[:, 0:8], ssq[:, 0:8], ACT.Sqrt).then_inc(s_ac, 1)
            for b in range(3, NB):
                act.wait_ge(s_cts[b % 3], 16 * (b // 3))
                act.dma_start(ct[b % 3], CT[:, :, b].rearrange("p h k v -> p h (k v)")).then_inc(s_ct[b % 3], 16)
            act.wait_ge(s_hh, 2 * MH + 1)
            act.wait_ge(s_sq, 8)
            act.activation(scr[:, :], zw[:, 3, :], ACT.Square, accum_out=ssq[:, 8:9]).then_inc(s_sq, 1)
            act.wait_ge(s_sqd, 2)
            act.activation(ssq[:, 8:9], ssq[:, 8:9], ACT.Sqrt).then_inc(s_ac, 1)

        @block.vector
        def _(dve):
            link = Chain(dve)
            dve.wait_ge(s_colp, 1)
            dve.tensor_copy(colsb[:, 0:60], psX[:, 0:60]).then_inc(s_col, 1)
            dve.tensor_copy(ACC, psX[0:NS, 60:61]).then_inc(s_col, 1)
            dve.wait_ge(s_col, 2)

            def finish(num, den, e, gate):
                link(dve.tensor_scalar(sm1[:, 0:1], den, -1.0, None, ALU.mult))
                link(dve.scalar_tensor_tensor(out=sm1[:, 0:1], in0=sm1[:, 0:1], scalar=e, in1=den, op0=ALU.max, op1=ALU.max))
                link(dve.reciprocal(sm1[:, 1:2], sm1[:, 0:1]))
                dve.scalar_tensor_tensor(out=gate, in0=num, scalar=sm1[:, 1:2], in1=gate, op0=ALU.mult, op1=ALU.mult).then_inc(s_hh, 1)

            def head_keys(hd):
                dve.wait_ge(s_mts, hd + 1)
                if hd >= 1:
                    dve.wait_ge(s_ms_, hd)
                dve.tensor_copy(kT_[:, :, :].rearrange("p a b -> p (a b)"), psTR[:, 1, :]).then_inc(s_mtse, 1)
                if hd >= 1:
                    dve.wait_ge(s_cp, hd)
                for t in range(2):
                    dve.tensor_scalar(wk[:, t, :], zm[:, t, 1, hd * MD:(hd + 1) * MD], PC_(2, t, hd), KS, ALU.mult, ALU.mult).then_inc(s_wk, 1)

            head_keys(0)
            for hd in range(MH):
                dve.wait_ge(s_mm, hd + 1)
                if hd >= 1:
                    dve.wait_ge(s_e, 2 * hd)
                dve.tensor_tensor(arg[:, 0:P], CBc("causal"), psM[:, 0:P], ALU.subtract).then_inc(s_arg, 1)
                dve.tensor_scalar(arg[:, P:SEQ], psM[:, P:SEQ], -1.0, None, ALU.mult).then_inc(s_arg, 1)
                dve.tensor_tensor(arg[:, SEQ:3 * P], CBc("causal"), psM[:, P:SEQ], ALU.subtract).then_inc(s_arg, 1)
                dve.wait_ge(s_e, 2 * hd + 2)
                dve.wait_ge(s_ms_, hd + 1)
                if hd >= 1:
                    dve.wait_ge(s_num, hd)
                dve.scalar_tensor_tensor(out=wt[:, :], in0=psS_[:, 0:3 * P], scalar=KS, in1=ex[:, :], op0=ALU.mult, op1=ALU.mult).then_inc(s_w_, 1)
                if hd + 1 < MH:
                    head_keys(hd + 1)
                dve.wait_ge(s_num, hd + 1)
                for t in range(2):
                    finish(psN_[:, t, 0:MD], psN_[:, t, MD:MD + 1], PC_(1, t, hd), zm[:, t, 2, hd * MD:(hd + 1) * MD])
            dve.tensor_copy(sv[:, 0:MD], zw[:, 2, :]).then_inc(s_sv, 1)
            dve.tensor_copy(sv[:, MD:MD + 1], ones[:, 0:1]).then_inc(s_sv, 1)
            dve.wait_ge(s_cp, MH)
            dve.tensor_scalar(wk[:, 0, :], zw[:, 1, :], SC_(2), KS, ALU.mult, ALU.mult).then_inc(s_wk, 1)
            dve.wait_ge(s_ms_, MH)
            for j in range(MH):
                dve.tensor_scalar(wv[:, j, :], zw[:, 2, :], SC_(2), CBc("hcol")[:, j:j + 1], ALU.mult, ALU.mult).then_inc(s_qmm, 1)
            dve.wait_ge(s_mte, MH + 1)
            for half in range(2):
                dve.tensor_tensor(qmm[:, half], sT[:, half, :].unsqueeze(1).to_broadcast([P, NB, P]),
                                  CBc("bcol").rearrange("p (b f) -> p b f", b=NB), ALU.mult).then_inc(s_qmm, 1)
            dve.wait_ge(s_mm, MH + 1)
            dve.wait_ge(s_e, 2 * MH)
            dve.tensor_tensor(arg[:, 0:P], CBc("scausal"), psM[:, 0:P], ALU.subtract).then_inc(s_arg, 1)
            dve.wait_ge(s_e, 2 * MH + 1)
            dve.wait_ge(s_ms_, MH + 1)
            dve.wait_ge(s_num, MH)
            dve.wait_ge(s_sv, 2)
            dve.scalar_tensor_tensor(out=wt[:, 0:P], in0=psS_[:, 0:P], scalar=KS, in1=ex[:, 0:P], op0=ALU.mult, op1=ALU.mult).then_inc(s_w_, 1)
            dve.wait_ge(s_sq, 8)
            dve.tensor_scalar(ssq[:, 0:8], ssq[:, 0:8], 1.0 / MD, EPS, ALU.mult, ALU.add).then_inc(s_sqd, 1)
            dve.wait_ge(s_ac, 1)
            link(dve.reciprocal(rsq[:, 0:8], ssq[:, 0:8]))
            for n in range(8):
                x = zm[:, n % 2, 2, (n // 2) * MD:(n // 2 + 1) * MD]
                dve.tensor_scalar(x, x, rsq[:, n:n + 1], None, ALU.mult).then_inc(s_ha, 1)
            dve.wait_ge(s_ld, 48)
            dve.wait_ge(s_nn, 1)
            dve.scalar_tensor_tensor(out=nrow[:, :], in0=nrow[:, :], scalar=ACC, in1=psX[0:NS, 0:MD], op0=ALU.mult, op1=ALU.add).then_inc(s_nno, 1)
            for b in range(NB):
                if b >= 2:
                    dve.wait_ge(s_up, 2 * (b - 1))
                dve.tensor_scalar(km[:, b % 2, :], zw[:, 1, :], CBc("brow")[:, b:b + 1], KS, ALU.mult, ALU.mult).then_inc(s_km, 1)
                dve.wait_ge(s_cq, b + 1)
                for j in range(MH):
                    dve.wait_ge(s_up, 2 * b + j // 2 + 1)
                    ps = (psTR, psSC)[j // 2][:, :, (j % 2) * MD:(j % 2 + 1) * MD]
                    x = ct[b % 3][:, j, :].rearrange("p (a n) -> p a n", a=2)
                    n = j * NB + b
                    dve.scalar_tensor_tensor(out=x, in0=x, scalar=AC[:, n:n + 1], in1=ps, op0=ALU.mult, op1=ALU.add).then_inc(s_upd, 1)
            link(dve.tensor_tensor(ntok[:, :], ntok[:, :], zw[:, 0, :], ALU.mult))
            link(dve.tensor_reduce(sm1[:, 2:3], ntok[:, :], AX.X, ALU.add))
            dve.wait_ge(s_num, MH + 1)
            link(dve.scalar_tensor_tensor(out=sm1[:, 3:4], in0=sm1[:, 2:3], scalar=SC_(3), in1=psN_[:, 0, MD:MD + 1], op0=ALU.mult, op1=ALU.add))
            link(dve.tensor_scalar(ntok[:, :], psN_[:, 1, 0:MD], SC_(3), None, ALU.mult))
            link(dve.tensor_tensor(ntok[:, :], ntok[:, :], psN_[:, 0, 0:MD], ALU.add))
            finish(ntok[:, :], sm1[:, 3:4], SC_(1), zw[:, 3, :])
            dve.wait_ge(s_sq, 9)
            dve.tensor_scalar(ssq[:, 8:9], ssq[:, 8:9], 1.0 / MD, EPS, ALU.mult, ALU.add).then_inc(s_sqd, 1)
            dve.wait_ge(s_ac, 2)
            link(dve.reciprocal(rsq[:, 8:9], ssq[:, 8:9]))
            dve.tensor_scalar(zw[:, 3, :], zw[:, 3, :], rsq[:, 8:9], None, ALU.mult).then_inc(s_ha, 1)
            dve.wait_ge(s_cts[2], 32)
            for n in range(4):
                dve.wait_ge(s_hat, n + 1)
                t, half = n // 2, n % 2
                dve.tensor_tensor(hAT[:, 4 * half:4 * half + 4, t * P:(t + 1) * P], psTR[:, n % 2, :].rearrange("p (q n) -> p q n", q=4),
                                  mnc[:, 4 * half:4 * half + 4].unsqueeze(2).to_broadcast([P, 4, P]), ALU.mult).then_inc(s_hae, 1)
            for half in range(2):
                dve.wait_ge(s_hat, 5 + half)
                dve.tensor_tensor(hAT[:, half:KT:2, SEQ:TOK], psTR[:, half, 0:P].rearrange("p (h n) -> p h n", h=MH),
                                  mnc[:, half:KT:2].unsqueeze(2).to_broadcast([P, MH, NS]), ALU.mult).then_inc(s_hae, 1)
    ap.close()
    mid.close()
    ring = sb(front, "ring", [P, 6, 4096])
    wb_ = sb(front, "wb", [P, 4096])
    wpb = wb_[:, :].rearrange("p (k n) -> p k n", k=4)
    b2s = wb_[0:E, 0:D]
    wple = wb_[:, D:3 * D].rearrange("p (k n) -> p k n", k=2)
    prow = wb_[:, 3 * D:3 * D + 3 * PLE].rearrange("p (t n) -> p t n", t=3)
    uT = xT
    zflat = zg[:, :, :].rearrange("p t n -> p (t n)")
    x2 = zflat[:, 0:3 * D].rearrange("p (t n) -> p t n", t=3)
    acc2 = zflat[0:2 * NS, 3 * D:3 * D + 512]
    ysb = zflat[:, 3 * D + 512:4 * D]
    xflat = xT[:, :, :].rearrange("p k n -> p (k n)")
    glu, lin, sg, xg = (xflat[:, 512 * i:512 * (i + 1)] for i in range(4))
    hflat = hBT[:, :, :].rearrange("p k n -> p (k n)")
    xgT = hflat[:, 0:512].rearrange("p (j n) -> p j n", j=4)
    prT = hflat[:, 0:2 * TOK].rearrange("p (k n) -> p k n", k=2)
    acT = hflat[:, 512:1024].rearrange("p (j n) -> p j n", j=4)
    wr = sb(front, "wr", [P, KT, E])
    RG = sb(front, "RG", [P, E + 1, 6])
    selU, selG = sb(front, "selU", [P, 3, P]), sb(front, "selG", [P, 3, P])
    GAB = sb(front, "GAB", [P, 2, TOK])
    b1s = sb(front, "b1s", [2, 2 * 512])
    rg6 = sb(front, "rg6", [P, 6])
    nmax = sb(front, "nmax", [P, 1], I32)
    st3 = sb(front, "st3", [P, 12])
    ple = (zaflat[:, KT * D:KT * D + D], wb_[:, 3 * D:4 * D])
    plew = sb(front, "plew", [P, D // 4])
    s_ring = [sem(front, f"s_ring{c}") for c in range(6)]
    w1v = w1[0].rearrange("e (c k p) n -> e c p k n", c=4, p=P)
    w2v = w2[0].rearrange("e (c k p) n -> e c p k n", c=2, p=P)

    def load_chunk(sp, e, c):
        if c < 4:
            src, k = w1v[e, c], 2
        else:
            src, k = w2v[e, c - 4], 4
        if not isinstance(e, int):
            src = (w1v[bass.ds(e, 1), c, :, :, :] if c < 4 else w2v[bass.ds(e, 1), c - 4, :, :, :]).rearrange("a p k n -> (a p) k n")
        sp.dma_start(ring[:, c, :].rearrange("p (k n) -> p k n", k=k), src).then_inc(s_ring[c], 16)

    ap = ExitStack()
    Lg = sb(ap, "Lg", [P, 3, E])
    work = [selU[:, :, i * E:(i + 1) * E] for i in range(4)]
    mask, m8 = selG[:, :, 0:E], selG[:, :, E:E + 8]
    brb = selG[:, 0, 2 * E:3 * E]
    gT = GAB[0:E, :, :].rearrange("p a b -> p (a b)")[:, 0:TOK]
    pX = [pb(ap, "pX0", [P, 2, 512]), pb(ap, "pX1", [P, 2, 512])]
    pX2 = pb(ap, "pX2", [P, 512])
    pT = pb(ap, "pT_", [P, 2, 512])
    pR = pb(ap, "pR", [P, 512])
    s_wb, s_sm, s_b2 = sem(ap, "s_wb"), sem(ap, "s_smallw"), sem(ap, "s_b2")
    s_pa, s_pe_, s_u = sem(ap, "s_products"), sem(ap, "s_products_out"), sem(ap, "s_u")
    s_ut, s_ute = sem(ap, "s_utrans"), sem(ap, "s_utrans_out")
    s_h1, s_sq, s_mq, s_rt, s_x2, s_x2t, s_x2e = (sem(front, "s_" + n) for n in (
        "residual", "sumsq2", "meansq2", "root2", "xn2", "xn2_trans", "xn2_T"))
    s_lg, s_mask, s_rk, s_gt, s_gte, s_bb, s_ex = (sem(ap, n) for n in (
        "s_logits", "s_mask", "s_rank", "s_gtrans", "s_gT", "s_bias2", "s_gexp"))
    s_nx, s_pq = sem(ap, "s_nextweights"), sem(ap, "s_ple_out")

    def xs_products(pe, xt, kt, wts, first_wait, n0, pX, pX2, s_pa, s_pe_):
        for t in range(3):
            if n0 + t >= 3:
                pe.wait_ge(s_pe_, n0 + t - 2)
            for s_ready, value, per_tile in first_wait:
                if t == 0 or per_tile:
                    pe.wait_ge(s_ready, value + per_tile * t)
            if t < 2:
                for c in range(2):
                    for k in range(kt):
                        last = pe.matmul(pX[t][:, c, :], xt[:, k, t * P:(t + 1) * P], wts[:, k, c * 512:(c + 1) * 512],
                                         start=(k == 0), stop=(k == kt - 1))
            else:
                for k in range(kt):
                    for g in range(4):
                        last = pe.matmul(pX2[32 * g:32 * g + 32, 0:D // 4], xt[:, k, SEQ:TOK], wts[:, k, g * 256:(g + 1) * 256],
                                         start=(k == 0), stop=(k == kt - 1))
            last.then_inc(s_pa, 1)

    with nc.Block() as block:
        @block.sync
        def _(sp):
            sp.dma_start(wpb, w_pb[0].rearrange("(k p) n -> p k n", p=P)).then_inc(s_wb, 16)
            sp.dma_start(wr[:, :, :], w_router).then_inc(s_sm, 16)
            sp.dma_start(brb, b_router[0].partition_broadcast(P)).then_inc(s_sm, 16)
            sp.dma_start(b1s[:, :], b1[0].rearrange("a b n -> a (b n)")).then_inc(s_sm, 16)
            for c in range(3):
                load_chunk(sp, 0, c)
            sp.wait_ge(s_pa, 3)
            sp.dma_start(wa, w_o[0].rearrange("(k p) n -> p k n", p=P)).then_inc(s_wa, 16)
            sp.wait_ge(s_pa, 6)
            sp.dma_start(b2s, b2[0]).then_inc(s_b2, 16)
            sp.dma_start(wple, w_ple[0].rearrange("(k p) n -> p k n", p=P)).then_inc(s_nx, 16)
            for t, src in enumerate((p_prompt[0:P], p_prompt[P:SEQ], p_sample)):
                sp.dma_start(prow[0:ROWS[t], t, :], src).then_inc(s_nx, 16)
            for c in range(3, 6):
                load_chunk(sp, 0, c)
            sp.wait_ge(s_pa, 9)
            sp.wait_ge(s_wa, 32)
            sp.dma_start(wa, w_ple_gate[0].rearrange("(k p) n -> p k n", p=P)).then_inc(s_wa, 16)
            while pieces:
                shift_piece(sp)

        @block.tensor
        def _(pe):
            xs_products(pe, hAT, KT, wa, [(s_wa, 16, 0)], 0, pX, pX2, s_pa, s_pe_)
            xs_products(pe, hBT, 4, wpb, [(s_wb, 16, 0)], 3, pX, pX2, s_pa, s_pe_)
            for t in range(2):
                pe.wait_ge(s_u, t + 1)
                for half in range(2):
                    if t:
                        pe.wait_ge(s_ute, half + 1)
                    for q in range(4):
                        k = 4 * half + q
                        last = pe.transpose(pT[:, half, q * P:(q + 1) * P], zg[:, t, k * P:(k + 1) * P], ident)
                    last.then_inc(s_ut, 1)
            pe.wait_ge(s_u, 3)
            for half in range(2):
                pe.wait_ge(s_ute, 3 + half)
                pe.transpose(pT[:, half, 0:P], zgw[:, 0, half * P:(half + 1) * P], ident).then_inc(s_ut, 1)
            xs_products(pe, uT, KT, wa, [(s_wa, 32, 0), (s_ute, 2, 2)], 6, pX, pX2, s_pa, s_pe_)
            pe.wait_ge(s_nx, 64)
            for q in range(2):
                for t in (2, 0, 1):
                    last = pe.transpose(pT[:, q, t * P:t * P + ROWS[t]], prow[0:ROWS[t], t, q * P:(q + 1) * P],
                                        ident[0:ROWS[t], 0:ROWS[t]])
                last.then_inc(s_ut, 1)
            xs_products(pe, prT, 2, wple, [(s_ute, 7, 0), (s_h1, 1, 1)], 0, pX, pX2, s_pa, s_pe_)
            for t in range(3):
                pe.wait_ge(s_x2, t + 1)
                for half in range(2):
                    if t:
                        pe.wait_ge(s_x2e, 2 * (t - 1) + half + 1)
                    for q in range(4):
                        k = 4 * half + q
                        last = pe.transpose(pT[:, half, q * P:q * P + ROWS[t]], x2[0:ROWS[t], t, k * P:(k + 1) * P],
                                            ident[0:ROWS[t], 0:ROWS[t]])
                    last.then_inc(s_x2t, 1)
            pe.wait_ge(s_sm, 48)
            pe.wait_ge(s_x2e, 6)
            for t in range(3):
                for k in range(KT):
                    last = pe.matmul(pR[0:ROWS[t], t * E:(t + 1) * E], uT[:, k, t * P:t * P + ROWS[t]], wr[:, k, :],
                                     start=(k == 0), stop=(k == KT - 1))
            last.then_inc(s_lg, 1)
            pe.wait_ge(s_mask, 1)
            for t in range(3):
                for s in range(t + 1):
                    pe.matmul(pR[:, 128 + t * E:128 + (t + 1) * E], CAc("before") if s == t else ones, mask[:, s, :],
                              start=(s == 0), stop=(s == t))
            for t in range(3):
                last = pe.matmul(pR[:, 256:256 + E], ones, mask[:, t, :], start=(t == 0), stop=(t == 2))
            last.then_inc(s_rk, 1)
            pe.wait_ge(s_mask, 2)
            for t in range(3):
                last = pe.transpose(pT[0:E, 0, t * P:t * P + ROWS[t]], work[0][0:ROWS[t], t, :], ident[0:ROWS[t], 0:ROWS[t]])
            last.then_inc(s_gt, 1)
            pe.wait_ge(s_gte, 1)
            pe.wait_ge(s_b2, 16)
            for t in range(2):
                pe.wait_ge(s_pq, t + 1)
                for c in range(2):
                    last = pe.matmul(pX[t][:, c, :], gT[:, t * P:(t + 1) * P], b2s[:, c * 512:(c + 1) * 512], start=True, stop=True)
                last.then_inc(s_bb, 1)
            pe.wait_ge(s_pq, 3)
            for c in range(2):
                last = pe.matmul(pX2[32 * c:32 * c + 32, :], gT[:, SEQ:TOK], b2s[:, c * 512:(c + 1) * 512], start=True, stop=True)
            last.then_inc(s_bb, 1)

        @block.scalar
        def _(act):
            for t in range(2):
                for half in range(2):
                    n = 2 * t + half
                    act.wait_ge(s_ut, n + 1)
                    act.wait_ge(s_pa, 6)
                    act.activation(uT[:, 4 * half:4 * half + 4, t * P:(t + 1) * P], pT[:, half, :].rearrange("p (q n) -> p q n", q=4),
                                   ACT.Copy).then_inc(s_ute, 1)
            for half in range(2):
                act.wait_ge(s_ut, 5 + half)
                act.activation(uT[:, half:KT:2, SEQ:TOK], pT[:, half, 0:P].rearrange("p (g n) -> p g n", g=4), ACT.Copy).then_inc(s_ute, 1)
            act.wait_ge(s_ut, 8)
            act.activation(prT, pT[:, :, 0:TOK], ACT.Copy).then_inc(s_ute, 1)
            for t in range(3):
                R = ROWS[t]
                act.wait_ge(s_h1, t + 1)
                act.activation(x2[0:R, t, :], h[0:R, t, :], ACT.Square, accum_out=st3[0:R, t:t + 1]).then_inc(s_sq, 1)
                act.wait_ge(s_mq, t + 1)
                act.activation(st3[0:R, t:t + 1], st3[0:R, t:t + 1], ACT.Sqrt).then_inc(s_rt, 1)
            for t, dst in enumerate((ple[0], ple[1], plew[:, :])):
                act.wait_ge(s_pa, 10 + t)
                act.activation(dst, (pX[0][:, :, :].rearrange("p c n -> p (c n)"), pX[1][:, :, :].rearrange("p c n -> p (c n)"),
                                     pX2[:, 0:D // 4])[t], ACT.Copy).then_inc(s_pq, 1)
            act.wait_ge(s_mask, 1)
            act.activation(work[0][:, :, :], work[0][:, :, :], ACT.Exp).then_inc(s_ex, 1)
            act.wait_ge(s_gt, 1)
            act.activation(gT[:, :], pT[0:E, 0, 0:TOK], ACT.Copy).then_inc(s_gte, 1)

        @block.vector
        def _(dve):
            link = Chain(dve)
            flat = lambda x: x[:, :, :].rearrange("p c n -> p (c n)")
            src = (flat(pX[0]), flat(pX[1]), pX2[:, 0:D // 4])
            ga = (zg[:, 0, 0:D], zg[:, 1, 0:D], zgw[:, 0, :])
            gb = (zg[:, 0, D:2 * D], zg[:, 1, D:2 * D], zgw[:, 1, :])
            for n in range(6):
                dve.wait_ge(s_pa, n + 1)
                z = (ga, gb)[n // 3][n % 3]
                dve.tensor_tensor(z, src[n % 3], z, ALU.mult).then_inc(s_pe_, 1)
                if n >= 3:
                    dve.wait_ge(s_pe_, n + 1)
                    dve.tensor_tensor(ga[n % 3], ga[n % 3], gb[n % 3], ALU.add).then_inc(s_u, 1)
            for t in range(2):
                dve.wait_ge(s_pa, 7 + t)
                dve.tensor_tensor(h[:, t, :], src[t], h[:, t, :], ALU.add).then_inc(s_h1, 1)
            dve.wait_ge(s_pa, 9)
            for g in range(4):
                ins = dve.tensor_tensor(h[0:NS, 2, g * 256:(g + 1) * 256], pX2[32 * g:32 * g + 32, 0:256],
                                        h[0:NS, 2, g * 256:(g + 1) * 256], ALU.add)
                if g < 3:
                    ins.then_inc(s_steps, 1)
                    link.n += 1
            ins.then_inc(s_h1, 1)
            dve.wait_ge(s_steps, link.n)
            for t in range(3):
                R = ROWS[t]
                dve.wait_ge(s_sq, t + 1)
                dve.tensor_scalar(st3[0:R, t:t + 1], st3[0:R, t:t + 1], 1.0 / D, EPS, ALU.mult, ALU.add).then_inc(s_mq, 1)
                dve.wait_ge(s_rt, t + 1)
                link(dve.reciprocal(st3[0:R, 3 + t:4 + t], st3[0:R, t:t + 1]))
                if t == 2:
                    link(dve.memset(x2[:, 2, :], 0.0))
                dve.tensor_scalar(x2[0:R, t, :], h[0:R, t, :], st3[0:R, 3 + t:4 + t], None, ALU.mult).then_inc(s_x2, 1)
            for t in range(3):
                R = ROWS[t]
                for half in range(2):
                    dve.wait_ge(s_x2t, 2 * t + half + 1)
                    dve.tensor_tensor(uT[:, 4 * half:4 * half + 4, t * P:t * P + R],
                                      pT[:, half, :].rearrange("p (q n) -> p q n", q=4)[:, :, 0:R],
                                      n2c[:, 4 * half:4 * half + 4].unsqueeze(2).to_broadcast([P, 4, R]), ALU.mult).then_inc(s_x2e, 1)
            link(dve.memset(Lg[:, :, :], 0.0))
            dve.wait_ge(s_lg, 1)
            link.many(*[dve.tensor_tensor(Lg[0:ROWS[t], t, :], pR[0:ROWS[t], t * E:(t + 1) * E], brb[0:ROWS[t], :], ALU.add) for t in range(3)])
            link.many(*[dve.max(m8[:, t, :], Lg[:, t, :]) for t in range(3)])
            wide = lambda x, n: x.to_broadcast([P, 3, n])
            v4 = wide(m8[:, :, TOPK - 1:TOPK], E)
            ex, gt, eq, pc = work
            link.many(dve.tensor_tensor(gt[:, :, :], Lg[:, :, :], v4, ALU.is_gt),
                      dve.tensor_tensor(eq[:, :, :], Lg[:, :, :], v4, ALU.is_equal),
                      dve.tensor_tensor(ex[:, :, :], Lg[:, :, :], wide(m8[:, :, 0:1], E), ALU.subtract))
            link.many(dve.tensor_copy(pc[:, :, :], eq[:, :, :]),
                      dve.tensor_reduce(st3[:, 6:9], gt[:, :, :], AX.X, ALU.add))
            a, b, d = pc, mask, 1
            while d < E:
                link.many(dve.tensor_tensor(b[:, :, d:E], a[:, :, d:E], a[:, :, 0:E - d], ALU.add),
                          dve.tensor_copy(b[:, :, 0:d], a[:, :, 0:d]))
                a, b, d = b, a, 2 * d
            link(dve.tensor_tensor(b[:, :, :], a[:, :, :], wide(st3[:, 6:9].unsqueeze(2), E), ALU.add))
            link(dve.tensor_scalar(b[:, :, :], b[:, :, :], TOPK + 0.5, None, ALU.is_lt))
            link(dve.tensor_tensor(b[:, :, :], b[:, :, :], eq[:, :, :], ALU.mult))
            link(dve.tensor_tensor(gt[:, :, :], gt[:, :, :], b[:, :, :], ALU.add))
            dve.tensor_tensor(mask[:, :, :], gt[:, :, :], wide(CAc("valid").unsqueeze(2), E), ALU.mult).then_inc(s_mask, 1)
            dve.wait_ge(s_mask, 1)
            dve.wait_ge(s_ex, 1)
            link(dve.tensor_tensor(ex[:, :, :], ex[:, :, :], mask[:, :, :], ALU.mult))
            link(dve.tensor_reduce(st3[:, 6:9], ex[:, :, :], AX.X, ALU.add))
            link(dve.tensor_scalar(st3[:, 6:9], st3[:, 6:9], 1e-30, None, ALU.max))
            link(dve.reciprocal(st3[:, 9:12], st3[:, 6:9]))
            dve.tensor_tensor(ex[:, :, :], ex[:, :, :], wide(st3[:, 9:12].unsqueeze(2), E), ALU.mult).then_inc(s_mask, 1)
            dve.wait_ge(s_mask, 2)
            FAR = 4096.0
            link(dve.memset(RG[:, E:E + 1, :], -FAR))
            link(dve.tensor_copy(RG[:, 0:E, 3:6], ex[:, :, :].rearrange("p t e -> p e t")))
            dve.wait_ge(s_rk, 1)
            link(dve.tensor_scalar(eq[:, :, :], pR[:, 128:128 + 3 * E].rearrange("p (t e) -> p t e", t=3), FAR, None, ALU.add))
            link(dve.tensor_tensor(eq[:, :, :], eq[:, :, :], mask[:, :, :], ALU.mult))
            link(dve.tensor_scalar(RG[:, 0:E, 0:3], eq[:, :, :].rearrange("p t e -> p e t"), -FAR, None, ALU.add))
            link(dve.tensor_reduce(st3[:, 6:7], pR[:, 256:256 + E], AX.X, ALU.max))
            link(dve.tensor_copy(nmax[:, :], st3[:, 6:7]))
            for t in range(2):
                dve.wait_ge(s_bb, t + 1)
                link(dve.tensor_tensor(h[:, t, :], src[t], h[:, t, :], ALU.add))
            dve.wait_ge(s_bb, 3)
            link.many(*[dve.tensor_tensor(acc2[32 * c:32 * c + 32, :], pX2[32 * c:32 * c + 32, :], h[0:NS, 2, c * 512:(c + 1) * 512], ALU.add)
                        for c in range(2)])
            link(dve.memset(GAB[:, :, :], 0.0))
    ap.close()

    ap = ExitStack()
    pG, pL, pY = pb(ap, "eG", [P, 512]), pb(ap, "eL", [P, 512]), pb(ap, "eY", [P, 512])
    pSc = [pb(ap, f"eS{i}", [P, 512]) for i in range(2)]
    pA, pB, pC = pb(ap, "eA", [P, 512]), pb(ap, "eB", [P, 512]), pb(ap, "eC", [P, 512])
    names = ("used", "b1", "col", "selU", "selG", "g1", "xg", "g2", "xgT", "h", "glu", "lin", "sg", "prod", "act",
             "at", "acT", "ysb", "gt", "gab", "sc", "acc", "rank")
    S = {n: sem(ap, "e_" + n) for n in names}
    OUT5 = 5

    def experts(p, pe=None, act=None, dve=None, sp=None):
        def w(eng, name, value, per):
            eng.wait_ge(S[name], value + per * p)

        def first(e, p):
            return isinstance(e, int) and isinstance(p, int) and e == 0 and p == 0

        def each(eng, body, start=1):
            with eng.Fori(start, E) as e:
                body(e)

        if sp is not None:
            def loads(e):
                w(sp, "h", e, E)
                sp.dma_start(b1s[:, :], b1[bass.ds(e, 1), :, :, :].rearrange("x a b n -> (x a) (b n)")).then_inc(S["b1"], 16)
                for c in range(6):
                    w(sp, "used", 6 * e - 5 + c, 6 * E)
                    load_chunk(sp, e, c)
            if not isinstance(p, int):
                w(sp, "h", 0, E)
                sp.dma_start(b1s[:, :], b1[0].rearrange("a b n -> a (b n)")).then_inc(S["b1"], 16)
                w(sp, "used", 0, 6 * E)
                for c in range(6):
                    load_chunk(sp, 0, c)
            each(sp, loads)

        if pe is not None:
            def gather(e):
                w(pe, "selU", e + 1, E + 1)
                for t in range(3):
                    for c in range(2):
                        last = pe.matmul(pA[64 * c:64 * c + 64, :], selU[:, t, 0:CAP], x2[:, t, c * 512:(c + 1) * 512],
                                         start=(t == 0), stop=(t == 2))
                last.then_inc(S["g1"], 1)

            def gather_t(e):
                w(pe, "xg", e + 1, E + 1)
                if not isinstance(e, int) or e:
                    w(pe, "gab", 2 * e, 2 * E)
                for j in range(4):
                    last = pe.transpose(pB[:, j * P:(j + 1) * P], xg[:, j * P:(j + 1) * P], ident)
                last.then_inc(S["g2"], 1)

            def up(e):
                w(pe, "xgT", e + 1, E + 1)
                if not first(e, p):
                    w(pe, "b1", 16 * e, 16 * E)
                for i, ps in enumerate((pG, pL)):
                    last = pe.matmul(ps[:, :], CAc("halves")[0:2], b1s[:, i * 512:(i + 1) * 512], start=True, stop=False,
                                     skip_group_check=True)
                last.then_inc(S["h"], 1)
                for k in range(KT):
                    c = k // 2
                    if k % 2 == 0:
                        pe.wait_ge(s_ring[c], 16 * (e + 1) + 16 * E * p)
                    for i, ps in enumerate((pG, pL)):
                        for hh in range(2):
                            col = (k % 2) * 2 * FF + i * FF + hh * 512
                            last = pe.matmul(ps[64 * hh:64 * hh + 64, :], xgT[:, k % 4, (k // 4) * CAP:(k // 4 + 1) * CAP],
                                             ring[:, c, col:col + 512], start=False, stop=(k == KT - 1), skip_group_check=True)
                    if k % 2:
                        last.then_inc(S["used"], 1)

            def gates_t(e):
                w(pe, "selG", e + 1, E + 1)
                w(pe, "xgT", e + 1, E + 1)
                for t in range(3):
                    last = pe.transpose(pB[:, t * P:t * P + ROWS[t]], selG[0:ROWS[t], t, :], ident[0:ROWS[t], 0:ROWS[t]])
                last.then_inc(S["gt"], 1)

            def scatter(e, products=range(OUT5)):
                if 0 in products:
                    w(pe, "ysb", e + 1, E)
                    w(pe, "gab", 2 * e + 2, 2 * E)
                for n in products:
                    if n != 1 and (n or not first(e, p)):
                        w(pe, "acc", OUT5 * e + (0, None, 1, 2, 3)[n], OUT5 * E)
                    ps = pSc[n % 2]
                    if n < 4:
                        t, c = n // 2, n % 2
                        last = pe.matmul(ps[:, :], GAB[:, c, t * P:(t + 1) * P], ysb, start=True, stop=True)
                    else:
                        for c in range(2):
                            last = pe.matmul(ps[32 * c:32 * c + 32, :], GAB[:, c, SEQ:TOK], ysb, start=True, stop=True)
                    last.then_inc(S["sc"], 1)

            def down_t(e):
                w(pe, "act", e + 1, E)
                for j in range(4):
                    last = pe.transpose(pC[:, j * P:(j + 1) * P], sg[:, j * P:(j + 1) * P], ident)
                last.then_inc(S["at"], 1)

            def down(e, c):
                if c == 4:
                    w(pe, "acT", e + 1, E)
                for k in range(4 * (c - 4), 4 * (c - 3)):
                    if k % 4 == 0:
                        pe.wait_ge(s_ring[c], 16 * (e + 1) + 16 * E * p)
                    for hh in range(2):
                        col = (k % 4) * D + hh * 512
                        last = pe.matmul(pY[64 * hh:64 * hh + 64, :], acT[:, k % 4, (k // 4) * CAP:(k // 4 + 1) * CAP],
                                         ring[:, c, col:col + 512], start=(k == 0), stop=(k == KT - 1))
                    if k % 4 == 3:
                        last.then_inc(S["used"], 1)

            def body(e):
                gates_t(e)
                up(e)
                gather(e + 1)
                if not isinstance(e, int) or e:
                    scatter(e - 1, range(4))
                down_t(e)
                if not isinstance(e, int) or e:
                    scatter(e - 1, [4])
                down(e, 4)
                gather_t(e + 1)
                down(e, 5)

            gather(0)
            gather_t(0)
            body(0)
            body(1)
            each(pe, body, 2)
            scatter(E - 1)

        if act is not None:
            def rows(e):
                w(act, "g1", e + 1, E + 1)
                act.activation(xg, pA[:, :], ACT.Copy).then_inc(S["xg"], 1)

            def gates_out(e):
                w(act, "gt", e + 1, E)
                if not first(e, p):
                    w(act, "sc", OUT5 * e, OUT5 * E)
                act.activation(GAB[0:64, 0, :], pB[0:64, 0:TOK], ACT.Copy).then_inc(S["gab"], 1)
                act.activation(GAB[64:P, 1, :], pB[64:P, 0:TOK], ACT.Copy).then_inc(S["gab"], 1)

            def hidden_t(e):
                w(act, "at", e + 1, E)
                act.activation(acT.rearrange("p j n -> p (j n)"), pC[:, :], ACT.Copy).then_inc(S["acT"], 1)

            def out(e):
                w(act, "used", 6 * (e + 1), 6 * E)
                act.activation(ysb, pY[:, :], ACT.Copy).then_inc(S["ysb"], 1)

            def sigm(e):
                w(act, "glu", e + 1, E)
                act.activation(sg, glu, ACT.Sigmoid, scale=ALPHA).then_inc(S["sg"], 1)

            def body(e):
                sigm(e)
                rows(e + 1)
                hidden_t(e)
                gates_out(e)
                out(e)

            rows(0)
            body(0)
            each(act, body)

        if dve is not None:
            def select(e):
                if not first(e, p):
                    w(dve, "g1", e, E + 1)
                    w(dve, "gt", e, E)
                dve.tensor_copy(rg6[:, :], RG[:, bass.ds(e, 1), :].rearrange("p a b -> p (a b)")).then_inc(S["col"], 1)
                w(dve, "col", e + 1, E + 1)
                slot = CAc("slot").unsqueeze(1).to_broadcast([P, 3, P])
                dve.tensor_tensor(selU[:, :, :], slot, rg6[:, 0:3].unsqueeze(2).to_broadcast([P, 3, P]), ALU.is_equal).then_inc(S["selU"], 1)
                w(dve, "selU", e + 1, E + 1)
                dve.tensor_tensor(selG[:, :, :], selU[:, :, :], rg6[:, 3:6].unsqueeze(2).to_broadcast([P, 3, P]), ALU.mult).then_inc(S["selG"], 1)

            def rows_t(e):
                w(dve, "g2", e + 1, E + 1)
                dve.tensor_tensor(xgT.rearrange("p j (c n) -> p j c n", c=2), pB[:, :].rearrange("p (j c n) -> p j c n", j=4, c=2),
                                  n2c.rearrange("p (c j) -> p j c", c=2).unsqueeze(3).to_broadcast([P, 4, 2, CAP]),
                                  ALU.mult).then_inc(S["xgT"], 1)

            def swiglu(e):
                w(dve, "used", 6 * e + 4, 6 * E)
                dve.tensor_scalar(glu, pG[:, :], LIMIT, None, ALU.min).then_inc(S["glu"], 1)
                dve.tensor_scalar(lin, pL[:, :], LIMIT, -LIMIT, ALU.min, ALU.max).then_inc(S["lin"], 1)
                w(dve, "lin", e + 1, E)
                dve.scalar_tensor_tensor(out=lin, in0=lin, scalar=1.0, in1=glu, op0=ALU.add, op1=ALU.mult).then_inc(S["prod"], 1)
                w(dve, "prod", e + 1, E)
                w(dve, "sg", e + 1, E)
                dve.tensor_tensor(sg, sg, lin, ALU.mult).then_inc(S["act"], 1)

            def add(e):
                for n in range(OUT5):
                    w(dve, "sc", OUT5 * e + n + 1, OUT5 * E)
                    ps = pSc[n % 2]
                    if n < 4:
                        x = h[:, n // 2, (n % 2) * 512:(n % 2 + 1) * 512]
                        dve.tensor_tensor(x, ps[:, :], x, ALU.add).then_inc(S["acc"], 1)
                    else:
                        dve.tensor_tensor(acc2, ps[0:2 * NS, :], acc2, ALU.add).then_inc(S["acc"], 1)

            if not isinstance(p, int):
                w(dve, "acc", 0, OUT5 * E)
                dve.tensor_scalar(RG[:, :, 0:3], RG[:, :, 0:3], -float(CAP), None, ALU.add).then_inc(S["rank"], 1)
                dve.wait_ge(S["rank"], p)
            select(0)
            rows_t(0)
            select(1)
            swiglu(0)
            rows_t(1)

            def body(e):
                select(e + 1)
                swiglu(e)
                add(e - 1)
                rows_t(e + 1)
            each(dve, body)
            add(E - 1)

    with nc.Block() as block:
        def passes(eng, **kw):
            experts(0, **kw)
            most = eng.value_load(nmax[0:1, 0:1], min_val=0, max_val=TOK)
            with eng.If(most > CAP):
                with eng.Fori(1, PASSES) as p:
                    experts(p, **kw)

        @block.sync
        def _(sp):
            passes(sp, sp=sp)

        @block.tensor
        def _(pe):
            passes(pe, pe=pe)

        @block.scalar
        def _(act):
            passes(act, act=act)

        @block.vector
        def _(dve):
            passes(dve, dve=dve)
    ap.close()
    ap = ExitStack()
    pX = [pb(ap, "fX0", [P, 2, 512]), pb(ap, "fX1", [P, 2, 512])]
    pX2 = pb(ap, "fX2", [P, 512])
    pT = pb(ap, "fT", [P, 2, 512])
    rflat = ring[:, :, :].rearrange("p c n -> p (c n)")
    sgp = rflat[:, 0:2 * D].rearrange("p (t n) -> p t n", t=2)
    sgw = rflat[:, 2 * D:2 * D + 256]
    tmp2 = rflat[0:NS, 3 * D:4 * D]
    nfb = rflat[:, 4 * D:5 * D]
    y = rflat[:, 5 * D:8 * D].rearrange("p (t n) -> p t n", t=3)
    s_nf = sem(ap, "s_normf")
    s_pa, s_pe_ = sem(ap, "f_products"), sem(ap, "f_products_out")
    s_h3, s_y = (sem(ap, "f_" + n) for n in ("h3", "y"))

    with nc.Block() as block:
        @block.sync
        def _(sp):
            sp.dma_start(nfb, norm_f.partition_broadcast(P)).then_inc(s_nf, 16)
            for t, dst in enumerate((y_prompt[0:P], y_prompt[P:SEQ], y_sample)):
                sp.wait_ge(s_y, t + 1)
                store(sp, dst, y[0:ROWS[t], t, :])
            sp.wait_ge(s_shift, n_shift)
            sp.wait_ge(s_stored, n_stored[0])

        @block.tensor
        def _(pe):
            pe.wait_ge(s_wa, 48)
            for t in range(3):
                pe.wait_ge(s_x2, 4 + t)
                for half in range(2):
                    if t:
                        pe.wait_ge(s_x2e, 6 + 2 * (t - 1) + half + 1)
                    for q in range(4):
                        k = 4 * half + q
                        last = pe.transpose(pT[:, half, q * P:q * P + ROWS[t]], x2[0:ROWS[t], t, k * P:(k + 1) * P],
                                            ident[0:ROWS[t], 0:ROWS[t]])
                    last.then_inc(s_x2t, 1)
            xs_products(pe, uT, KT, wa, [(s_x2e, 8, 2)], 0, pX, pX2, s_pa, s_pe_)

        @block.scalar
        def _(act):
            for t in range(3):
                R = ROWS[t]
                if t == 2:
                    act.wait_ge(s_h1, 5)
                act.activation(x2[0:R, t, :], h[0:R, t, :], ACT.Square, accum_out=st3[0:R, t:t + 1]).then_inc(s_sq, 1)
            for t in range(3):
                R = ROWS[t]
                act.wait_ge(s_mq, 4 + t)
                act.activation(st3[0:R, t:t + 1], st3[0:R, t:t + 1], ACT.Sqrt).then_inc(s_rt, 1)
            src = (pX[0][:, :, :].rearrange("p c n -> p (c n)"), pX[1][:, :, :].rearrange("p c n -> p (c n)"), pX2[:, 0:D // 4])
            for t, dst in enumerate((sgp[:, 0, :], sgp[:, 1, :], sgw)):
                act.wait_ge(s_pa, t + 1)
                act.activation(dst, src[t], ACT.Sigmoid).then_inc(s_pe_, 1)
            for t in range(3):
                R = ROWS[t]
                act.wait_ge(s_h3, t + 1)
                act.activation(y[0:R, t, :], h[0:R, t, :], ACT.Square, accum_out=st3[0:R, 6 + t:7 + t]).then_inc(s_sq, 1)
            for t in range(3):
                R = ROWS[t]
                act.wait_ge(s_mq, 7 + t)
                act.activation(st3[0:R, 6 + t:7 + t], st3[0:R, 6 + t:7 + t], ACT.Sqrt).then_inc(s_rt, 1)

        @block.vector
        def _(dve):
            link = Chain(dve)

            def rstd(n, c, t):
                R = ROWS[t]
                dve.wait_ge(s_sq, n + t + 1)
                dve.tensor_scalar(st3[0:R, c + t:c + t + 1], st3[0:R, c + t:c + t + 1], 1.0 / D, EPS, ALU.mult, ALU.add).then_inc(s_mq, 1)

            for c in range(2):
                dve.tensor_copy(h[0:NS, 2, c * 512:(c + 1) * 512], acc2[c * NS:(c + 1) * NS, :]).then_inc(s_h1, 1)
            for t in range(3):
                rstd(3, 0, t)
            for t in range(3):
                R = ROWS[t]
                dve.wait_ge(s_rt, 4 + t)
                if t == 2:
                    dve.wait_ge(s_h1, 5)
                link(dve.reciprocal(st3[0:R, 3 + t:4 + t], st3[0:R, t:t + 1]))
                dve.tensor_scalar(x2[0:R, t, :], h[0:R, t, :], st3[0:R, 3 + t:4 + t], None, ALU.mult).then_inc(s_x2, 1)
            for t in range(3):
                R = ROWS[t]
                for half in range(2):
                    dve.wait_ge(s_x2t, 6 + 2 * t + half + 1)
                    dve.tensor_tensor(uT[:, 4 * half:4 * half + 4, t * P:t * P + R],
                                      pT[:, half, :].rearrange("p (q n) -> p q n", q=4)[:, :, 0:R],
                                      n3c[:, 4 * half:4 * half + 4].unsqueeze(2).to_broadcast([P, 4, R]), ALU.mult).then_inc(s_x2e, 1)
            for t, (g, x) in enumerate(((sgp[:, 0, :], ple[0]), (sgp[:, 1, :], ple[1]), (sgw, plew[:, :]))):
                dve.wait_ge(s_pe_, t + 1)
                link(dve.tensor_tensor(g, x, g, ALU.mult))
                if t < 2:
                    dve.tensor_tensor(h[:, t, :], h[:, t, :], g, ALU.add).then_inc(s_h3, 1)
                else:
                    link.many(*[dve.tensor_copy(tmp2[:, k * 256:(k + 1) * 256], sgw[32 * k:32 * k + 32, :]) for k in range(4)])
                    dve.tensor_tensor(h[0:NS, 2, :], h[0:NS, 2, :], tmp2, ALU.add).then_inc(s_h3, 1)
            for t in range(3):
                rstd(6, 6, t)
            dve.wait_ge(s_nf, 16)
            for t in range(3):
                R = ROWS[t]
                dve.wait_ge(s_rt, 7 + t)
                link(dve.reciprocal(st3[0:R, 9 + t:10 + t], st3[0:R, 6 + t:7 + t]))
                dve.scalar_tensor_tensor(out=y[0:R, t, :], in0=h[0:R, t, :], scalar=st3[0:R, 9 + t:10 + t], in1=nfb[0:R],
                                         op0=ALU.mult, op1=ALU.mult).then_inc(s_y, 1)
    ap.close()
    front.close()
    top.close()


def kernel(**inputs):
    import concourse.bacc as _bacc
    from concourse.bass_utils import run_bass_kernel_spmd as _run

    nc = _bacc.Bacc("TRN2", target_bir_lowering=False, num_devices=1)
    arrays = lay_out(inputs)
    args = {n: nc.dram_tensor(n, a.shape, mybir.dt.from_np(a.dtype), kind="ExternalInput").ap() for n, a in arrays.items()}
    for n, shape in OUT_SHAPES.items():
        args[n] = nc.dram_tensor(n, shape, F32, kind="ExternalOutput").ap()
    layer(nc, **args)
    r = _run(nc, [arrays], core_ids=[0])
    return arrange({n: r.results[0][n] for n in OUT_SHAPES})
```
